# Optimizing a Trainium2 kernel written in Bass

```python
import math
import jax, jax.numpy as jnp
from jax import lax
import numpy as np

D_MODEL = 1024
BATCH = 1
SEQ = 256
DEPTH = 1

GRID_W = 64
CTX_LEN = 256
RMS_EPS = 1e-6
SHORT_CONV = 3
D_HYENA = 512
HYENA_ORDER = 2
HYENA_EMB_BANDS = 16
HYENA_EMB_DIM = 1 + 2 * HYENA_EMB_BANDS
HYENA_FILTER_HIDDEN = 64
HYENA_DECAY_TARGET = 1e-2
HYENA_MIN_DECAY = math.log(HYENA_DECAY_TARGET) / 1.5
HYENA_MAX_DECAY = math.log(HYENA_DECAY_TARGET) / 0.3
MLSTM_HEADS = 4
MLSTM_HEAD_DIM = 128
D_MLSTM = MLSTM_HEADS * MLSTM_HEAD_DIM
MLSTM_CHUNK = 128
N_BRANCHES = 2
HY_COLS = (HYENA_ORDER + 1) * D_HYENA
ML_COLS = 4 * D_MLSTM
GATE_COLS = 4 * MLSTM_HEADS
MERGE_COLS = N_BRANCHES * D_MODEL
ML_START = HY_COLS
GATE_START = ML_START + ML_COLS
MERGE_START = GATE_START + GATE_COLS
D_IN_PROJ = MERGE_START + MERGE_COLS
N_EXPERTS = 16
EC_CAPACITY_FACTOR = 2
D_FF_EXPERT = 2 * D_MODEL


def rmsnorm(x, g):
    x32 = x.astype(jnp.float32)
    y = x32 * lax.rsqrt(jnp.mean(x32 * x32, axis=-1, keepdims=True) + RMS_EPS)
    return y.astype(x.dtype) * g

def modulate(h, shift, scale):
    return h * (1.0 + scale[:, None, :]) + shift[:, None, :]

def short_conv(u, w, rows, row_len):
    B, L, C = u.shape
    K = w.shape[0]
    ur = u.reshape(B, rows, row_len, C)
    up = jnp.pad(ur, ((0, 0), (0, 0), (K // 2, K // 2), (0, 0)))
    y = sum(up[:, :, j:j + row_len] * w[j] for j in range(K))
    return y.reshape(B, L, C)

def hyena_filters(L, w1, b1, w2, b2, w3):
    f32 = lambda a: a.astype(jnp.float32)
    t = jnp.linspace(0.0, 1.0, L, dtype=jnp.float32)[:, None]
    bands = jnp.linspace(1e-4, HYENA_EMB_BANDS - 1, HYENA_EMB_BANDS, dtype=jnp.float32)[None, :]
    ang = (2.0 * math.pi / L) * jnp.arange(L, dtype=jnp.float32)[:, None] * bands
    z = jnp.concatenate([t, jnp.cos(ang), jnp.sin(ang)], axis=-1)
    h = jnp.sin(z @ f32(w1) + f32(b1))
    h = jnp.sin(h @ f32(w2) + f32(b2))
    h = (h @ f32(w3)).reshape(L, HYENA_ORDER, 2, D_HYENA)
    deltas = jnp.abs(jnp.linspace(HYENA_MIN_DECAY, HYENA_MAX_DECAY, D_HYENA, dtype=jnp.float32))
    return h * jnp.exp(-t * deltas)[:, None, None, :]

def bidir_long_conv(u, h, skip):
    B, L, C = u.shape
    k = jnp.concatenate([h[:, 0], jnp.zeros((1, C), h.dtype), h[:0:-1, 1]], axis=0)
    U = jnp.fft.rfft(u.astype(jnp.float32), n=2 * L, axis=1)
    Kf = jnp.fft.rfft(k, n=2 * L, axis=0)
    y = jnp.fft.irfft(U * Kf[None], n=2 * L, axis=1)[:, :L]
    return (y + u.astype(jnp.float32) * skip.astype(jnp.float32)).astype(u.dtype)

def hyena_branch(hy_p, conv_w, f_w1, f_b1, f_w2, f_b2, f_w3, skip, rows, row_len):
    L = hy_p.shape[1]
    parts = jnp.split(short_conv(hy_p, conv_w, rows, row_len), HYENA_ORDER + 1, axis=-1)
    filt = hyena_filters(L, f_w1, f_b1, f_w2, f_b2, f_w3)
    z = parts[0]
    for o in range(HYENA_ORDER):
        z = parts[o + 1] * bidir_long_conv(z, filt[:, o], skip[o])
    return z

def mlstm_chunk_scan(q, k, v, log_i, log_f, state0):
    G, H, L, dh = q.shape
    nc = L // MLSTM_CHUNK

    def chunks(a):
        return jnp.moveaxis(a.reshape(G, H, nc, MLSTM_CHUNK, *a.shape[3:]), 2, 0)

    tril = jnp.tril(jnp.ones((MLSTM_CHUNK, MLSTM_CHUNK), dtype=bool))

    def step(carry, inp):
        C, n, m = carry
        qc, kc, vc, li, lf = inp
        b = jnp.cumsum(lf, axis=-1)
        logw = jnp.where(tril, b[..., :, None] - b[..., None, :] + li[..., None, :], -jnp.inf)
        m_inter = b + m[..., None]
        m_t = jnp.maximum(m_inter, logw.max(-1))
        a_intra = jnp.exp(logw - m_t[..., None]) * jnp.einsum('ghtd,ghsd->ghts', qc, kc)
        a_inter = jnp.exp(m_inter - m_t)
        num = jnp.einsum('ghts,ghse->ghte', a_intra, vc) + a_inter[..., None] * jnp.einsum('ghtd,ghde->ghte', qc, C)
        den = a_intra.sum(-1) + a_inter * jnp.einsum('ghtd,ghd->ght', qc, n)
        h = num / jnp.maximum(jnp.abs(den), jnp.exp(-m_t))[..., None]
        b_end = b[..., -1]
        logw_end = b_end[..., None] - b + li
        m_new = jnp.maximum(b_end + m, logw_end.max(-1))
        w_end = jnp.exp(logw_end - m_new[..., None])
        decay = jnp.exp(b_end + m - m_new)
        C_new = decay[..., None, None] * C + jnp.einsum('ghs,ghsd,ghse->ghde', w_end, kc, vc)
        n_new = decay[..., None] * n + jnp.einsum('ghs,ghsd->ghd', w_end, kc)
        return (C_new, n_new, m_new), h

    state, hs = lax.scan(step, state0, (chunks(q), chunks(k), chunks(v), chunks(log_i), chunks(log_f)))
    return jnp.moveaxis(hs, 0, 2).reshape(G, H, L, dh), state

def mlstm_zero_state(batch):
    g = 2 * batch
    return (jnp.zeros((g, MLSTM_HEADS, MLSTM_HEAD_DIM, MLSTM_HEAD_DIM), jnp.float32),
            jnp.zeros((g, MLSTM_HEADS, MLSTM_HEAD_DIM), jnp.float32),
            jnp.zeros((g, MLSTM_HEADS), jnp.float32))

def mlstm_branch(ml_p, gate_p, conv_w, norm_g, rows, row_len, state0):
    B, L, _ = ml_p.shape
    q_pre, k_pre, v, o = jnp.split(ml_p, 4, axis=-1)
    qk = jax.nn.silu(short_conv(jnp.concatenate([q_pre, k_pre], axis=-1), conv_w, rows, row_len))
    q, k = jnp.split(qk, 2, axis=-1)

    def heads(a):
        return a.reshape(B, L, MLSTM_HEADS, MLSTM_HEAD_DIM).transpose(0, 2, 1, 3).astype(jnp.float32)

    q = heads(q) * (MLSTM_HEAD_DIM ** -0.5)
    k = heads(k)
    v = heads(v)
    g = gate_p.astype(jnp.float32).reshape(B, L, 4, MLSTM_HEADS).transpose(2, 0, 3, 1)
    i_f, f_f, i_b, f_b = g[0], g[1], g[2], g[3]
    flip = lambda a: jnp.flip(a, axis=2)
    q2 = jnp.concatenate([q, flip(q)], axis=0)
    k2 = jnp.concatenate([k, flip(k)], axis=0)
    v2 = jnp.concatenate([v, flip(v)], axis=0)
    log_i = jnp.concatenate([i_f, flip(i_b)], axis=0)
    log_f = jax.nn.log_sigmoid(jnp.concatenate([f_f, flip(f_b)], axis=0))
    h2, state = mlstm_chunk_scan(q2, k2, v2, log_i, log_f, state0)
    h = h2[:B] + flip(h2[B:])
    h = h * lax.rsqrt(jnp.mean(h * h, axis=-1, keepdims=True) + RMS_EPS)
    h = h.transpose(0, 2, 1, 3).reshape(B, L, D_MLSTM).astype(ml_p.dtype) * norm_g
    return h * jax.nn.sigmoid(o), state

def token_mixer(h, w_in, b_in, hy_conv, hy_f_w1, hy_f_b1, hy_f_w2, hy_f_b2, hy_f_w3, hy_skip,
                ml_conv, ml_norm_g, w_branch_hy, w_branch_ml, w_out, rows, row_len, state0):
    p = h @ w_in + b_in
    y_a = hyena_branch(p[..., :ML_START], hy_conv, hy_f_w1, hy_f_b1, hy_f_w2, hy_f_b2, hy_f_w3, hy_skip, rows, row_len)
    y_b, state = mlstm_branch(p[..., ML_START:GATE_START], p[..., GATE_START:MERGE_START], ml_conv, ml_norm_g, rows, row_len, state0)
    g_a, g_b = jnp.split(jax.nn.sigmoid(p[..., MERGE_START:]), N_BRANCHES, axis=-1)
    y = (g_a * (y_a @ w_branch_hy) + g_b * (y_b @ w_branch_ml)) @ w_out
    return y, state

def expert_choice_ffn(h, w_router, w1, w3, w2):
    B, N, D = h.shape
    cap = EC_CAPACITY_FACTOR * N // N_EXPERTS
    aff = jax.nn.softmax((h @ w_router).astype(jnp.float32), axis=-1)
    gate, idx = lax.top_k(jnp.swapaxes(aff, 1, 2), cap)
    bidx = jnp.arange(B)[:, None, None]
    xg = h[bidx, idx]
    a = jnp.einsum('becd,edf->becf', xg, w1)
    b = jnp.einsum('becd,edf->becf', xg, w3)
    ye = jnp.einsum('becf,efd->becd', jax.nn.silu(a) * b, w2) * gate[..., None].astype(h.dtype)
    return jnp.zeros_like(h).at[bidx, idx].add(ye)

def first_inputs(seed: int = 0) -> dict:
    key = jax.random.key(seed)
    ks = jax.random.split(key, 32)
    D = D_MODEL
    nrm = lambda k, shape, scale: jax.random.normal(k, shape, jnp.float32) * scale
    forget_offset = np.zeros((D_IN_PROJ,), np.float32)
    forget_offset[GATE_START + MLSTM_HEADS:GATE_START + 2 * MLSTM_HEADS] = np.linspace(3.0, 6.0, MLSTM_HEADS)
    forget_offset[GATE_START + 3 * MLSTM_HEADS:GATE_START + 4 * MLSTM_HEADS] = np.linspace(3.0, 6.0, MLSTM_HEADS)
    return {
        'x': nrm(ks[0], (BATCH, SEQ, D), 1.0),
        'c': nrm(ks[1], (BATCH, D), 1.0),
        'ctx': nrm(ks[2], (BATCH, CTX_LEN, D), 1.0),
        'c_ctx': nrm(ks[3], (D,), 1.0),
        'w_ada': nrm(ks[4], (DEPTH, D, 6 * D), 0.5 * D ** -0.5),
        'b_ada': nrm(ks[5], (DEPTH, 6 * D), 0.02),
        'norm_mix_g': 1.0 + nrm(ks[6], (DEPTH, D), 0.02),
        'norm_ffn_g': 1.0 + nrm(ks[7], (DEPTH, D), 0.02),
        'w_in': nrm(ks[8], (DEPTH, D, D_IN_PROJ), D ** -0.5),
        'b_in': nrm(ks[9], (DEPTH, D_IN_PROJ), 0.02) + jnp.asarray(forget_offset),
        'hy_conv': nrm(ks[10], (DEPTH, SHORT_CONV, HY_COLS), 0.5),
        'hy_f_w1': nrm(ks[11], (DEPTH, HYENA_EMB_DIM, HYENA_FILTER_HIDDEN), HYENA_EMB_DIM ** -0.5),
        'hy_f_b1': nrm(ks[12], (DEPTH, HYENA_FILTER_HIDDEN), 0.1),
        'hy_f_w2': nrm(ks[13], (DEPTH, HYENA_FILTER_HIDDEN, HYENA_FILTER_HIDDEN), HYENA_FILTER_HIDDEN ** -0.5),
        'hy_f_b2': nrm(ks[14], (DEPTH, HYENA_FILTER_HIDDEN), 0.1),
        'hy_f_w3': nrm(ks[15], (DEPTH, HYENA_FILTER_HIDDEN, HYENA_ORDER * 2 * D_HYENA), 0.03 * HYENA_FILTER_HIDDEN ** -0.5),
        'hy_skip': nrm(ks[16], (DEPTH, HYENA_ORDER, D_HYENA), 1.0),
        'ml_conv': nrm(ks[17], (DEPTH, SHORT_CONV, 2 * D_MLSTM), 0.5),
        'ml_norm_g': 1.0 + nrm(ks[18], (DEPTH, D_MLSTM), 0.02),
        'w_branch_hy': nrm(ks[19], (DEPTH, D_HYENA, D), D_HYENA ** -0.5),
        'w_branch_ml': nrm(ks[20], (DEPTH, D_MLSTM, D), D_MLSTM ** -0.5),
        'w_out': nrm(ks[21], (DEPTH, D, D), D ** -0.5),
        'w_router': nrm(ks[22], (DEPTH, D, N_EXPERTS), D ** -0.5),
        'w_exp1': nrm(ks[23], (DEPTH, N_EXPERTS, D, D_FF_EXPERT), D ** -0.5),
        'w_exp3': nrm(ks[24], (DEPTH, N_EXPERTS, D, D_FF_EXPERT), D ** -0.5),
        'w_exp2': nrm(ks[25], (DEPTH, N_EXPERTS, D_FF_EXPERT, D), D_FF_EXPERT ** -0.5),
        'final_norm_g': 1.0 + nrm(ks[26], (D,), 0.02),
    }

def first_block(x, c, ctx, c_ctx, w_ada, b_ada, norm_mix_g, norm_ffn_g, w_in, b_in,
              hy_conv, hy_f_w1, hy_f_b1, hy_f_w2, hy_f_b2, hy_f_w3, hy_skip,
              ml_conv, ml_norm_g, w_branch_hy, w_branch_ml, w_out,
              w_router, w_exp1, w_exp3, w_exp2, final_norm_g):
    B, L, _ = x.shape
    rows = L // GRID_W
    Lc = ctx.shape[1]
    s_lat = jax.nn.silu(c)
    s_ctx = jax.nn.silu(c_ctx)[None, :]
    for l in range(DEPTH):
        last = l == DEPTH - 1
        ada_x = jnp.split(s_lat @ w_ada[l] + b_ada[l], 6, axis=-1)
        ada_c = jnp.split(s_ctx @ w_ada[l] + b_ada[l], 6, axis=-1)
        mix_params = (w_in[l], b_in[l], hy_conv[l], hy_f_w1[l], hy_f_b1[l], hy_f_w2[l], hy_f_b2[l], hy_f_w3[l],
                      hy_skip[l], ml_conv[l], ml_norm_g[l], w_branch_hy[l], w_branch_ml[l], w_out[l])
        hc = modulate(rmsnorm(ctx, norm_mix_g[l]), ada_c[0], ada_c[1])
        if last:
            pc = hc @ w_in[l][:, ML_START:MERGE_START] + b_in[l][ML_START:MERGE_START]
            _, ctx_state = mlstm_branch(pc[..., :ML_COLS], pc[..., ML_COLS:], ml_conv[l], ml_norm_g[l],
                                        1, Lc, mlstm_zero_state(B))
        else:
            yc, ctx_state = token_mixer(hc, *mix_params, 1, Lc, mlstm_zero_state(B))
            ctx = ctx + ada_c[2][:, None, :] * yc
            hc2 = modulate(rmsnorm(ctx, norm_ffn_g[l]), ada_c[3], ada_c[4])
            ctx = ctx + ada_c[5][:, None, :] * expert_choice_ffn(hc2, w_router[l], w_exp1[l], w_exp3[l], w_exp2[l])
        hx = modulate(rmsnorm(x, norm_mix_g[l]), ada_x[0], ada_x[1])
        yx, _ = token_mixer(hx, *mix_params, rows, GRID_W, ctx_state)
        x = x + ada_x[2][:, None, :] * yx
        hx2 = modulate(rmsnorm(x, norm_ffn_g[l]), ada_x[3], ada_x[4])
        x = x + ada_x[5][:, None, :] * expert_choice_ffn(hx2, w_router[l], w_exp1[l], w_exp3[l], w_exp2[l])
    return rmsnorm(x, final_norm_g)


DEPTH_2 = 2

N_HEADS = 8
N_KV_HEADS = 2
HEAD_DIM = 64
GQA_GROUP = N_HEADS // N_KV_HEADS
ATTN_WIDTH = N_HEADS * HEAD_DIM
KV_WIDTH = N_KV_HEADS * HEAD_DIM
WINDOW = 128
BLOCK = 128
ROPE_THETA = 500000.0
ROT_DIM = HEAD_DIM // 4
POOL_SIZES = (2, 4, 8, 16)
POOL_WIDTH = D_MODEL // 2
POOL_GROUP = POOL_WIDTH // len(POOL_SIZES)
IN_WIDTH = ATTN_WIDTH + 2 * KV_WIDTH + POOL_WIDTH + N_BRANCHES * D_MODEL
D_FF = 2816
EPS = 1e-6


def rms_norm(x, g):
    x32 = x.astype(jnp.float32)
    y = x32 * lax.rsqrt(jnp.mean(x32 * x32, axis=-1, keepdims=True) + EPS)
    return (y * g.astype(jnp.float32)).astype(x.dtype)

def swiglu(u, w1, w3, w2):
    return (jax.nn.silu(u @ w1) * (u @ w3)) @ w2

def rope_tables(s):
    inv_freq = 1.0 / (ROPE_THETA ** (jnp.arange(0, ROT_DIM, 2, dtype=jnp.float32) / ROT_DIM))
    ang = jnp.arange(s, dtype=jnp.float32)[:, None] * inv_freq[None, :]
    return jnp.cos(ang), jnp.sin(ang)

def partial_rope(t, cos, sin):
    half = ROT_DIM // 2
    t32 = t.astype(jnp.float32)
    t1 = t32[..., :half]
    t2 = t32[..., half:ROT_DIM]
    c = cos[None, :, None, :]
    s = sin[None, :, None, :]
    rot = jnp.concatenate([t1 * c - t2 * s, t2 * c + t1 * s, t32[..., ROT_DIM:]], axis=-1)
    return rot.astype(t.dtype)

def banded_blocks(t):
    b, s = t.shape[0], t.shape[1]
    nb = s // BLOCK
    tp = jnp.pad(t, ((0, 0), (BLOCK, BLOCK), (0, 0), (0, 0)))
    parts = [tp[:, i * BLOCK:i * BLOCK + s].reshape(b, nb, BLOCK, t.shape[2], t.shape[3]) for i in range(3)]
    return jnp.concatenate(parts, axis=2)

def windowed_gqa(q, k, v, sink):
    b, s = q.shape[0], q.shape[1]
    nb = s // BLOCK
    qb = q.reshape(b, nb, BLOCK, N_KV_HEADS, GQA_GROUP, HEAD_DIM)
    kb = banded_blocks(k)
    vb = banded_blocks(v)
    scores = jnp.einsum('bnqhgd,bnkhd->bhgnqk', qb, kb).astype(jnp.float32) * (HEAD_DIM ** -0.5)
    blk = jnp.arange(nb)[:, None, None]
    qpos = blk * BLOCK + jnp.arange(BLOCK)[None, :, None]
    kpos = blk * BLOCK - BLOCK + jnp.arange(3 * BLOCK)[None, None, :]
    valid = (jnp.abs(qpos - kpos) <= WINDOW) & (kpos >= 0) & (kpos < s)
    scores = jnp.where(valid, scores, -1e30)
    sink_logit = jnp.broadcast_to(
        sink.astype(jnp.float32).reshape(1, N_KV_HEADS, GQA_GROUP, 1, 1, 1), scores.shape[:-1] + (1,))
    probs = jax.nn.softmax(jnp.concatenate([scores, sink_logit], axis=-1), axis=-1)[..., :-1]
    out = jnp.einsum('bhgnqk,bnkhd->bnqhgd', probs.astype(v.dtype), vb)
    return out.reshape(b, s, ATTN_WIDTH)

def multiscale_pool(p, pool_w, pool_scale):
    b, s, _ = p.shape
    p32 = p.astype(jnp.float32)
    cs = jnp.concatenate([jnp.zeros((b, 1, POOL_WIDTH), jnp.float32), jnp.cumsum(p32, axis=1)], axis=1)
    t = jnp.arange(s)
    outs = []
    for gi, w in enumerate(POOL_SIZES):
        sl = slice(gi * POOL_GROUP, (gi + 1) * POOL_GROUP)
        lo = jnp.clip(t - w // 2, 0, s)
        hi = jnp.clip(t + w // 2, 0, s)
        cnt = (hi - lo).astype(jnp.float32)[None, :, None]
        csg = cs[..., sl]
        mean = (jnp.take(csg, hi, axis=1) - jnp.take(csg, lo, axis=1)) / cnt
        outs.append(mean - p32[..., sl])
    pooled = jnp.stack(outs, axis=2).astype(p.dtype)
    mixed = jnp.einsum('bsgc,gcd->bsgd', pooled, pool_w).reshape(b, s, POOL_WIDTH)
    return mixed * pool_scale

def token_mixer_2(u, w_in, b_gate, attn_sink, pool_w, pool_scale, w_br_attn, w_br_pool, w_out, cos, sin):
    b, s, _ = u.shape
    proj = u @ w_in
    splits = np.cumsum([ATTN_WIDTH, KV_WIDTH, KV_WIDTH, POOL_WIDTH, D_MODEL]).tolist()
    q, k, v, p, ga, gb = jnp.split(proj, splits, axis=-1)
    q = partial_rope(q.reshape(b, s, N_HEADS, HEAD_DIM), cos, sin)
    k = partial_rope(k.reshape(b, s, N_KV_HEADS, HEAD_DIM), cos, sin)
    v = v.reshape(b, s, N_KV_HEADS, HEAD_DIM)
    y_attn = windowed_gqa(q, k, v, attn_sink) @ w_br_attn
    y_pool = multiscale_pool(p, pool_w, pool_scale) @ w_br_pool
    gate_a = jax.nn.sigmoid(ga + b_gate[:D_MODEL])
    gate_b = jax.nn.sigmoid(gb + b_gate[D_MODEL:])
    return (gate_a * y_attn + gate_b * y_pool) @ w_out

def _w(key, shape, fan_in):
    return jax.random.normal(key, shape, jnp.float32) * (fan_in ** -0.5)

def _gain(key, shape):
    return 1.0 + 0.05 * jax.random.normal(key, shape, jnp.float32)

def second_inputs(seed: int = 0) -> dict:
    key = jax.random.key(seed)
    ks = jax.random.split(key, 22)
    L = DEPTH_2
    return {
        "x": jax.random.normal(ks[0], (BATCH, SEQ, D_MODEL), jnp.float32),
        "ffn1_norm": _gain(ks[1], (L, D_MODEL)),
        "ffn1_w1": _w(ks[2], (L, D_MODEL, D_FF), D_MODEL),
        "ffn1_w3": _w(ks[3], (L, D_MODEL, D_FF), D_MODEL),
        "ffn1_w2": _w(ks[4], (L, D_FF, D_MODEL), D_FF),
        "mix_norm": _gain(ks[5], (L, D_MODEL)),
        "w_in": _w(ks[6], (L, D_MODEL, IN_WIDTH), D_MODEL),
        "b_gate": 0.02 * jax.random.normal(ks[7], (L, N_BRANCHES * D_MODEL), jnp.float32),
        "attn_sink": 0.5 * jax.random.normal(ks[8], (L, N_HEADS), jnp.float32),
        "pool_w": _w(ks[9], (L, len(POOL_SIZES), POOL_GROUP, POOL_GROUP), POOL_GROUP),
        "pool_scale": _gain(ks[10], (L, POOL_WIDTH)),
        "w_branch_attn": _w(ks[11], (L, ATTN_WIDTH, D_MODEL), ATTN_WIDTH),
        "w_branch_pool": _w(ks[12], (L, POOL_WIDTH, D_MODEL), POOL_WIDTH),
        "w_out": _w(ks[13], (L, D_MODEL, D_MODEL), D_MODEL),
        "ffn2_norm": _gain(ks[14], (L, D_MODEL)),
        "ffn2_w1": _w(ks[15], (L, D_MODEL, D_FF), D_MODEL),
        "ffn2_w3": _w(ks[16], (L, D_MODEL, D_FF), D_MODEL),
        "ffn2_w2": _w(ks[17], (L, D_FF, D_MODEL), D_FF),
        "final_norm": _gain(ks[18], (D_MODEL,)),
    }

def second_block(x, ffn1_norm, ffn1_w1, ffn1_w3, ffn1_w2, mix_norm, w_in, b_gate, attn_sink, pool_w,
              pool_scale, w_branch_attn, w_branch_pool, w_out, ffn2_norm, ffn2_w1, ffn2_w3, ffn2_w2,
              final_norm):
    cos, sin = rope_tables(x.shape[1])
    h = x
    for l in range(DEPTH_2):
        h = h + 0.5 * swiglu(rms_norm(h, ffn1_norm[l]), ffn1_w1[l], ffn1_w3[l], ffn1_w2[l])
        h = h + token_mixer_2(rms_norm(h, mix_norm[l]), w_in[l], b_gate[l], attn_sink[l], pool_w[l],
                            pool_scale[l], w_branch_attn[l], w_branch_pool[l], w_out[l], cos, sin)
        h = h + 0.5 * swiglu(rms_norm(h, ffn2_norm[l]), ffn2_w1[l], ffn2_w3[l], ffn2_w2[l])
    return rms_norm(h, final_norm)


def setup_inputs(seed=0):
    out = dict(first_inputs(seed))
    for name, value in second_inputs(seed + 1).items():
        if name != "x":
            out[name + "_2"] = value
    return out


def reference(
    x, c, ctx, c_ctx, w_ada, b_ada, norm_mix_g, norm_ffn_g, w_in, b_in, hy_conv, hy_f_w1,
    hy_f_b1, hy_f_w2, hy_f_b2, hy_f_w3, hy_skip, ml_conv, ml_norm_g, w_branch_hy, w_branch_ml,
    w_out, w_router, w_exp1, w_exp3, w_exp2, final_norm_g, ffn1_norm_2, ffn1_w1_2, ffn1_w3_2,
    ffn1_w2_2, mix_norm_2, w_in_2, b_gate_2, attn_sink_2, pool_w_2, pool_scale_2,
    w_branch_attn_2, w_branch_pool_2, w_out_2, ffn2_norm_2, ffn2_w1_2, ffn2_w3_2, ffn2_w2_2,
    final_norm_2,
):
    x = first_block(
        x, c, ctx, c_ctx, w_ada, b_ada, norm_mix_g, norm_ffn_g, w_in, b_in, hy_conv, hy_f_w1,
        hy_f_b1, hy_f_w2, hy_f_b2, hy_f_w3, hy_skip, ml_conv, ml_norm_g, w_branch_hy,
        w_branch_ml, w_out, w_router, w_exp1, w_exp3, w_exp2, final_norm_g,
    )
    return second_block(
        x, ffn1_norm_2, ffn1_w1_2, ffn1_w3_2, ffn1_w2_2, mix_norm_2, w_in_2, b_gate_2,
        attn_sink_2, pool_w_2, pool_scale_2, w_branch_attn_2, w_branch_pool_2, w_out_2,
        ffn2_norm_2, ffn2_w1_2, ffn2_w3_2, ffn2_w2_2, final_norm_2,
    )


_drawn_inputs = setup_inputs


def setup_inputs(seed=0):
    import zlib

    import numpy as np

    out = dict(_drawn_inputs(seed))
    spreads = {}
    factors = {'b_ada': 2.824,
     'norm_mix_g': 7.892,
     'norm_ffn_g': 39.789,
     'hy_f_b1': 8.0,
     'hy_f_b2': 6.321,
     'ml_norm_g': 200.0,
     'b_gate_2': 8.0,
     'attn_sink_2': 27.794,
     'ctx': 8.0,
     'c_ctx': 8.0,
     'b_in': 4.137,
     'ml_conv': 8.0}
    for name, (base, spread) in spreads.items():
        noise = np.random.default_rng([zlib.crc32(name.encode()), seed]).standard_normal(out[name].shape)
        drawn = base * np.exp(spread * noise) if base else spread * noise
        out[name] = __import__('jax').numpy.asarray(drawn.astype(out[name].dtype))
    for name, factor in factors.items():
        out[name] = (out[name] * factor).astype(out[name].dtype)
    return out
```

```python
from contextlib import ExitStack

import numpy as np
import concourse.bass as bass
from concourse import mybir
from concourse.alu_op_type import AluOpType as ALU

F32 = mybir.dt.float32
F32R = mybir.dt.float32r
U32 = mybir.dt.uint32
ACT = mybir.ActivationFunctionType
X = mybir.AxisListType.X

P = 128
D = 1024
KD = D // P
T = 256
TT = T // P
ROW = 64
HYC = 512
ORDERS = 2
HID = 64
EMB = 33
H = 4
VW = P + 2
NE = 16
CAP = 2 * T // NE
DFE = 2 * D
FT = 22
LAYERS = 2
POOLS = (2, 4, 8, 16)
EPS = 1e-6
QSCALE = P ** -0.5
BIG = 30000.0

RING = 8
SLOT = 2048
FIRST_SLOTS = 56
EXPERT_SLOTS = 24
LAYER_SLOTS = 88
N_SLOTS = FIRST_SLOTS + NE * EXPERT_SLOTS + LAYERS * LAYER_SLOTS


def offsets(*widths):
    at, out = 0, {}
    for name, n in widths:
        out[name] = at
        at += n
    return out, at


SPLITS = 3
FFN_SLOTS = [("up", 0), ("up", 1)]
for _i in range(1, FT // 2):
    FFN_SLOTS += [("up", 2 * _i), ("up", 2 * _i + 1), ("down", _i - 1)]
FFN_SLOTS.append(("down", FT // 2 - 1))

COLS, N_COLS = offsets(("c", 16), ("g_mix", 8), ("g_ffn", 8), ("b_hy", 12), ("b_q", 4), ("b_k", 4), ("b_o", 4),
                       ("b_merge", 16), ("hy_conv", 36), ("ml_conv", 24), ("skip", 8), ("ml_g", 4),
                       ("f_b1", 1), ("f_b2", 1), ("b_gate", 4), ("not_first", 2), ("eps", 1), ("one", 1),
                       ("token", 2))
LCOLS, N_LCOLS = offsets(("norm", 24), ("b_gates", 16), ("pool_scale", 4), ("sink", 8), ("pool_w", 512))
FILT, N_FILT = offsets(("z", T), ("w1", HID), ("w2", HID), ("w3", 4 * HYC), ("decay", TT * HYC))
TABS, N_TABS = offsets(("dft", 2 * TT * T), ("idft", 2 * TT * T), ("causal", 2 * 384))
TABS2, N_TABS2 = offsets(("rope", 2 * TT * 8), ("amask", TT * T), ("pool", 4 * TT * T))


class Link:

    def __init__(self, eng, sem, trip=None, per_trip=0):
        self.eng, self.sem, self.trip, self.per_trip, self.n = eng, sem, trip, per_trip, 0

    def __call__(self, ins):
        self.n += 1
        ins.then_inc(self.sem, 1)
        self.eng.wait_ge(self.sem, self.n if self.trip is None else self.trip * self.per_trip + self.n)

    def close(self):
        assert self.trip is None or self.n == self.per_trip, self.n


class Region:

    def __init__(self, tensor, at, end):
        self.tensor, self.at, self.end = tensor, at, end

    def take(self, *dims):
        n = int(np.prod(dims))
        v = self.tensor[:, self.at:self.at + n]
        self.at += n
        assert self.at <= self.end, (self.at, self.end)
        if len(dims) == 2:
            return v.rearrange("p (a b) -> p a b", a=dims[0])
        if len(dims) == 3:
            return v.rearrange("p (a b c) -> p a b c", a=dims[0], b=dims[1])
        if len(dims) == 4:
            return v.rearrange("p (a b c d) -> p a b c d", a=dims[0], b=dims[1], c=dims[2])
        return v


def build(nc, d):
    with ExitStack() as ctx:
        def sb(name, shape, dt=F32):
            return ctx.enter_context(nc.sbuf_tensor(name, shape, dt))

        signals = {}

        def sig(name):
            if name not in signals:
                signals[name] = ctx.enter_context(nc.semaphore(name))
            return signals[name]

        ring = sb("ring", [P, RING, SLOT])
        cols = sb("cols", [P, N_COLS])
        lcols = sb("lcols", [P, N_LCOLS])
        const = sb("const", [P, 2 * P + T])
        ident, ones, iota = const[:, 0:P], const[:, P:2 * P], const[:, 2 * P:]
        x_tok = sb("x_tok", [P, TT, D])
        area_n = sb("area_n", [P, 4096])
        area_h = sb("area_h", [P, 4096])
        ada_rows = sb("ada_rows", [P, 3, 512])
        ada_cols = sb("ada_cols", [P, 2, 48])
        mod1 = sb("mod1", [P, 2, KD])
        mod2 = sb("mod2", [P, KD])
        stat = sb("stat", [P, 3, 4])
        silu_c = sb("silu_c", [P, KD, 32])
        wgate = sb("wgate", [P, KD, 16])
        vbias = sb("vbias", [P, HYC])
        wrouter = sb("wrouter", [P, KD, NE])
        topi = sb("topi", [P, NE * 2], U32)
        fin_rows = sb("fin_rows", [P, D])
        WIDE = 21590
        with nc.sbuf_tensor("wide", [P, WIDE], F32) as wide:
            pass
        tabs2 = sb("tabs2", [P, N_TABS2])
        LATER = WIDE - N_TABS2
        with nc.sbuf_tensor("later", [P, LATER], F32) as later:
            pass
        w_hi = sb("w_hi", [P, SPLITS, SLOT], F32R)
        w_lo = sb("w_lo", [P, SPLITS, SLOT], F32R)
        u_hi = sb("u_hi", [P, KD, T], F32R)
        u_lo = sb("u_lo", [P, KD, T], F32R)
        hid_hi = sb("hid_hi", [P, 4, T], F32R)
        hid_lo = sb("hid_lo", [P, 4, T], F32R)
        ps = ctx.enter_context(nc.psum_tensor("ps", [P, 8, 512], F32))

        def bank(i):
            return ps[:, i, :]

        def col(name, i=0, n=1, rows=P):
            return cols[0:rows, COLS[name] + i:COLS[name] + i + n]

        def lcol(name, i=0, n=1):
            return lcols[:, LCOLS[name] + i:LCOLS[name] + i + n]

        xn = area_n[:, 0:2048].rearrange("p (t d) -> p t d", t=TT)
        cn = area_n[:, 2048:].rearrange("p (t d) -> p t d", t=TT)
        merge = area_n[:, :].rearrange("p (d g t) -> p d g t", d=KD, g=2)
        hT = area_h[:, :].rearrange("p (k t) -> p k t", k=KD)
        r = Region(area_h, 0, 4096)
        pm = r.take(2, TT, HYC)
        pm_tmp = r.take(2, HYC)
        r = Region(area_n, 0, 4096)
        gates = r.take(4, 2 * T)
        lnb = r.take(2, 2 * T)
        bcum = r.take(2, 2 * T)
        g_in, g_forget = gates[:, 0::2, :], gates[:, 1::2, :]
        r = Region(wide, 0, WIDE)
        dft = r.take(2, TT, T)
        idft = r.take(2, TT, T)
        causal = r.take(2, 384)
        spec = r.take(ORDERS, 2, TT, HYC)
        hy = r.take(12, T)
        kT = r.take(H, 2 * T)
        qT = r.take(H, T)
        oT = r.take(H, T)
        z_tok = wide[:, r.at:r.at + TT * HYC].rearrange("p (t c) -> p t c", t=TT)
        v_tok = r.take(2 * TT, H, VW)
        base = r.at
        filt = r.take(N_FILT)
        hid1 = r.take(T)
        hid2 = r.take(T)
        arg = r.take(T)
        turns = r.take(T)
        r = Region(wide, base, WIDE)
        raw = r.take(4, 2 * T)
        mrow = r.take(2, T)
        zrow = r.take(T)
        kw = r.take(TT, 2, P)
        states = r.take(2 * H, VW)
        hm = r.take(TT, H, P)
        r = Region(lcols, 0, N_LCOLS)
        gcols = r.take(4, 2, TT, H)
        mcols = r.take(8)
        r = Region(wide, base, base + 2048)
        ee = r.take(2, TT, T)
        inter = r.take(TT, 2 * VW)
        den = r.take(TT, 2)
        hsq = wide[:, base:base + 1024].rearrange("p (h e) -> p h e", h=TT * H)
        hstat = stat[:, 0:2, :].rearrange("p a b -> p (a b)")
        r = Region(wide, base, WIDE)
        yspec = r.take(2, TT, HYC)
        yt = r.take(4, HYC)
        r = Region(wide, base, WIDE)
        grow = r.take(D)
        gtmp = r.take(TT, D)
        sq1 = hy[:, 0:4, :].rearrange("p a b -> p (a b)")

        r = Region(later, 0, LATER)
        sel = r.take(TT, NE * CAP)
        h2T = r.take(KD, T)
        aff = r.take(TT, NE)
        esum = r.take(TT)
        affT = r.take(T)
        topv = r.take(NE * 2)
        topf = r.take(NE * 2)
        rep = r.take(2, 4, CAP)
        bdiag = r.take(NE, CAP)
        bmask = r.take(NE, CAP)
        igcols = r.take(2, NE)
        zeros = r.take(512)
        xe = r.take(KD, CAP)
        sa = r.take(512)
        hid_e = r.take(512)
        hTe = r.take(4, P)
        ye = r.take(D)
        scat = r.take(T)
        grow2 = r.take(D)
        gtmp2 = r.take(TT, D)
        xgT = area_h[:, :].rearrange("p (k c) -> p k c", k=KD)

        sq = area_n[:, 2048:3072]
        uT = area_h[:, 0:2048].rearrange("p (k t) -> p k t", k=KD)
        mT = area_h[:, 2048:].rearrange("p (k t) -> p k t", k=KD)
        r = Region(area_n, 3072, 4096)
        sa2 = r.take(2, T)
        hid = r.take(2, T)
        r = Region(later, 0, LATER)
        qk = r.take(TT, 10, 64)
        p_tok = r.take(TT, 512)
        v2 = r.take(TT, P)
        q2T = r.take(4, T)
        k2T = r.take(T)
        sgate = r.take(KD, 2, T)
        att = r.take(TT, 8, T)
        a2T = r.take(4, T)
        rtmp = r.take(4, TT, 80)
        pooledT = r.take(4, T)
        mixT = r.take(4, T)
        mst = r.take(TT, 4, 8)
        attT = area_n[:, :].rearrange("p (k h q) -> p k h q", k=TT, h=8)
        rope = tabs2[:, 0:32].rearrange("p (f t c) -> p f t c", f=2, t=TT)
        amask = tabs2[:, TABS2["amask"]:TABS2["pool"]].rearrange("p (t k) -> p t k", t=TT)
        poolm = tabs2[:, TABS2["pool"]:].rearrange("p (g s t) -> p g s t", g=4, s=TT)
        pool_w = lcols[:, LCOLS["pool_w"]:].rearrange("p (g e) -> p g e", g=4)

        block = ctx.enter_context(nc.Block())

        @block.sync
        def _(sp):
            for s in range(RING):
                sp.dma_start(ring[:, s, :], d["stream"][s]).then_inc(sig(f"slot_loaded{s}"), 16)
            with sp.Fori(1, N_SLOTS // RING) as rev:
                for s in range(RING):
                    sp.wait_ge(sig("slot_used"), rev * RING + (s + 1 - RING))
                    sp.dma_start(ring[:, s, :], d["stream"][rev * RING + s]).then_inc(sig(f"slot_loaded{s}"), 16)
            sp.wait_ge(sig("out_ready"), 1)
            sp.dma_start(d["out"], x_tok[:, :, :]).then_inc(sig("stored"), 16)
            sp.wait_ge(sig("stored"), 16)

        @block.scalar
        def _(act):
            A = nc.scalar
            act.dma_start(cols[:, :], d["cols"]).then_inc(sig("cols_loaded"), 16)
            act.dma_start(filt, d["filt"]).then_inc(sig("filt_loaded"), 16)
            act.dma_start(x_tok[:, :, :], d["x"]).then_inc(sig("x_loaded"), 16)
            act.dma_start(cn, d["ctx"]).then_inc(sig("ctx_loaded"), 16)
            act.dma_start(const[:, :], d["const"]).then_inc(sig("const_loaded"), 16)
            act.dma_start(wide[:, 0:N_TABS], d["tabs"]).then_inc(sig("tabs_loaded"), 16)
            act.dma_start(ada_rows[:, :, :], d["ada_rows"]).then_inc(sig("ada_bias_loaded"), 16)
            act.dma_start(wgate[:, :, :], d["wgate"]).then_inc(sig("wgate_loaded"), 16)
            act.dma_start(vbias[:, :], d["vbias"]).then_inc(sig("vbias_loaded"), 16)
            act.dma_start(wrouter[:, :, :], d["wrouter"]).then_inc(sig("wrouter_loaded"), 16)
            act.dma_start(fin_rows[:, :], d["fin_rows"][0]).then_inc(sig("fin_loaded"), 16)
            step = Link(act, sig("act_step"))

            def root_mean_square(step, src, scratch, at, ready):
                for t in range(TT):
                    step(A.activation(scratch, src[:, t, :], ACT.Square, accum_out=stat[:, at, t:t + 1]))
                A.activation(stat[:, at, 2:4], stat[:, at, 0:2], ACT.Sqrt, scale=1.0 / D,
                             bias=col("eps")).then_inc(ready, 1)

            act.wait_ge(sig("cols_loaded"), 16)
            act.wait_ge(sig("cleared"), 1)
            A.activation(silu_c[:, :, 0:2], cols[:, 0:16].rearrange("p (k s) -> p k s", s=2),
                         ACT.Silu).then_inc(sig("silu_ready"), 1)
            act.wait_ge(sig("x_loaded"), 16)
            root_mean_square(step, x_tok, sq1, 0, sig("rms_ready"))
            act.wait_ge(sig("ctx_loaded"), 16)
            act.wait_ge(sig("rms_ready"), 1)
            root_mean_square(step, cn, sq1, 1, sig("rms_ready"))
            for n, h in enumerate((hid1, hid2)):
                act.wait_ge(sig("arg_ready"), n + 1)
                A.activation(h[0:HID, :], arg[0:HID, :], ACT.Sin).then_inc(sig("hid_ready"), 1)
            for o in range(ORDERS):
                act.wait_ge(sig("spec_ready"), o + 1)
                for j in range(2):
                    last = A.copy(spec[:, o, j, :, :], ps[:, 2 + 2 * j:4 + 2 * j, :])
                last.then_inc(sig("spec_kept"), 1)
            act.wait_ge(sig("mod1_ready"), 1)
            for k in range(0, KD, 2):
                act.wait_ge(sig("hT_ps"), k + 1)
                for s in range(2):
                    last = A.activation(hT[:, k, s * T:(s + 1) * T], ps[:, k, s * T:(s + 1) * T], ACT.Identity,
                                        scale=mod1[:, s, k:k + 1], bias=ada_cols[:, s, k:k + 1])
                last.then_inc(sig("hT_ready_a"), 1)

            def unit_ready(n):
                act.wait_ge(sig("unit_ready"), n + 1)
                return bank(n % 4 if n < 33 else 6 + n % 2)

            def to_conv(n, c, bias, width):
                b = unit_ready(n)
                if c >= 4:
                    act.wait_ge(sig("conv_done"), c - 3)
                A.activation(raw[:, c % 4, 0:width], b[:, 0:width], ACT.Identity,
                             bias=bias).then_inc(sig("unit_kept"), 1)

            b = unit_ready(0)
            for g in range(4):
                last = A.copy(gates[0:H, g, :], b[32 * g:32 * g + H, :])
            last.then_inc(sig("unit_kept"), 1)
            for h in range(H):
                to_conv(1 + h, h, col("b_k", h), 2 * T)
            act.wait_ge(sig("gates_biased"), 1)
            step(A.activation(lnb[0:H, :, :], g_forget[0:H], ACT.Abs))
            step(A.activation(lnb[0:H, :, :], lnb[0:H, :, :], ACT.Exp, scale=-1.0))
            A.activation(lnb[0:H, :, :], lnb[0:H, :, :], ACT.Ln,
                         bias=col("one", rows=H)).then_inc(sig("softplus_ready"), 1)
            for h in range(H):
                to_conv(5 + h, 4 + h, col("b_q", h), T)
            act.wait_ge(sig("gate_rows"), 1)
            act.wait_ge(sig("softplus_ready"), 1)
            A.activation(g_in[0:H, :, T:], g_in[0:H, :, T:], ACT.Exp)
            A.activation(lnb[0:H, :, :], lnb[0:H, :, :], ACT.Exp, scale=-1.0).then_inc(sig("gate_exps"), 1)
            for h in range(H):
                act.wait_ge(sig("conv_done"), h + 1)
                A.activation(kT[:, h, :], kT[:, h, :], ACT.Silu).then_inc(sig("k_ready"), 1)
            for h in range(H):
                act.wait_ge(sig("conv_done"), 4 + h + 1)
                A.activation(qT[:, h, :], qT[:, h, :], ACT.Silu).then_inc(sig("q_ready"), 1)
            for h in range(H):
                b = unit_ready(9 + h)
                A.activation(oT[:, h, :], b[:, 0:T], ACT.Sigmoid, bias=col("b_o", h)).then_inc(sig("unit_kept"), 1)
            for c in range(12):
                to_conv(13 + c, 8 + c, col("b_hy", c), T)
            act.wait_ge(sig("gcols_ps"), 1)

            def merge_gates(*units):
                for n in units:
                    b, m = unit_ready(n), n - 25
                    A.activation(merge[:, m // 2, m % 2, :], b[:, 0:T], ACT.Sigmoid,
                                 bias=col("b_merge", m)).then_inc(sig("unit_kept"), 1)

            merge_gates(*range(25, 33))

            for h in range(H):
                act.wait_ge(sig("state_ps"), h + 1)
                A.copy(states[:, 2 * h:2 * h + 2, :],
                       bank(6)[:, 0:2 * VW].rearrange("p (s e) -> p s e", s=2)).then_inc(sig("state_kept"), 1)
            for h in range(H):
                act.wait_ge(sig("gaps_ready"), h + 1)
                A.activation(ee, ee, ACT.Exp, scale=-1.0).then_inc(sig("decay_ready"), 1)
                act.wait_ge(sig("inter_ps"), h + 1)
                if h >= 1:
                    act.wait_ge(sig("head_done"), h)
                for t in range(TT):
                    for s in range(2):
                        last = A.activation(inter[:, t, s * VW:(s + 1) * VW], bank(t)[:, s * VW:(s + 1) * VW],
                                            ACT.Copy, scale=gcols[:, 1, s, t, h:h + 1])
                last.then_inc(sig("inter_kept"), 1)
            for o in range(ORDERS):
                act.wait_ge(sig("z_ps"), o + 1)
                if o >= 1:
                    act.wait_ge(sig("signal_ps"), o)
                A.copy(z_tok, ps[:, 4:6, :]).then_inc(sig("z_kept"), 1)
                if o == 0:
                    act.wait_ge(sig("hsum_ready"), 1)
                    A.activation(hstat, hstat, ACT.Sqrt, scale=1.0 / P, bias=col("eps")).then_inc(sig("hrms_ready"), 1)
                    merge_gates(33, 34, 35, 36)
                else:
                    merge_gates(37, 38, 39, 40)
            act.wait_ge(sig("grow_ps"), 1)
            A.copy(grow, ps[:, 0:2, :].rearrange("p b n -> p (b n)")).then_inc(sig("grow_ready"), 1)

            act.wait_ge(sig("x1_ready"), 1)
            act.dma_start(tabs2[:, :], d["tabs2"]).then_inc(sig("tabs2_loaded"), 16)
            act.dma_start(bmask, d["bmask"]).then_inc(sig("bmask_loaded"), 16)
            root_mean_square(step, x_tok, sq, 0, sig("rms_ready"))
            for k in range(KD):
                if k % 2 == 0:
                    act.wait_ge(sig("h2T_ps"), k // 2 + 1)
                A.activation(h2T[:, k, :], bank(k // 2)[:, (k % 2) * T:(k % 2 + 1) * T], ACT.Identity,
                             scale=mod2[:, k:k + 1], bias=ada_cols[:, 0, 24 + k:25 + k]).then_inc(sig("h2T_ready"), 1)
            act.wait_ge(sig("logits_ready"), 1)
            A.activation(aff, aff, ACT.Exp).then_inc(sig("exp_ready"), 1)
            for k in range(1, KD, 2):
                act.wait_ge(sig("xg_ps"), k + 1)
                A.activation(xgT[:, k, :], bank(k % 4), ACT.Identity, scale=mod2[:, k:k + 1],
                             bias=ada_cols[:, 0, 24 + k:25 + k]).then_inc(sig("xg_ready_a"), 1)
            with act.Fori(0, NE) as e:
                act.wait_ge(sig("a_ps"), e + 1)
                A.activation(sa, bank(4), ACT.Silu).then_inc(sig("sa_ready"), 1)
                act.wait_ge(sig("ye_ps"), e + 1)
                A.copy(ye, ps[:, 6:8, :].rearrange("p b n -> p (b n)")).then_inc(sig("ye_ready"), 1)
            act.wait_ge(sig("grow_ps"), 2)
            A.copy(grow2, ps[:, 4:6, :].rearrange("p b n -> p (b n)")).then_inc(sig("grow_ready"), 1)
            act.wait_ge(sig("x2_ready"), 1)
            root_mean_square(step, x_tok, sq, 0, sig("rms_ready"))
            before = step.n

            with act.Fori(0, LAYERS) as l:
                step = Link(act, sig("act_layer_step"), l, 6)
                act.wait_ge(sig("h_ready"), l * 3 + 1)
                act.dma_start(lcols[:, :], d["lcols"][l]).then_inc(sig("lcols_loaded"), 16)
                act.wait_ge(sig("lcols_loaded"), l * 16 + 16)

                def norm(n, meanwhile=None):
                    act.wait_ge(sig("h_ready"), l * 3 + n + 1)
                    root_mean_square(step, x_tok, sq, 0, sig("rms2_ready"))
                    if meanwhile:
                        meanwhile()
                    for b in (1, 3):
                        act.wait_ge(sig("uT_ps"), l * 12 + n * 4 + b + 1)
                        for k in (2 * b, 2 * b + 1):
                            last = A.activation(uT[:, k, :], bank(b)[:, (k % 2) * T:(k % 2 + 1) * T], ACT.Copy,
                                                scale=lcol("norm", 8 * n + k))
                        last.then_inc(sig("uT_ready_a"), 1)

                def ffn(f, at):
                    first = FIRST_SLOTS + NE * EXPERT_SLOTS + at

                    def upper(n):
                        if n >= len(FFN_SLOTS):
                            return
                        turn = l * (LAYER_SLOTS // RING) + (first + n) // RING
                        act.wait_ge(sig(f"slot_loaded{(first + n) % RING}"), turn * 16 + 16)
                        if n >= SPLITS:
                            act.wait_ge(sig("slot_used"), l * LAYER_SLOTS + first + n + 1 - SPLITS)
                        A.copy(w_hi[:, n % SPLITS, :], ring[:, (first + n) % RING, :]).then_inc(sig("w_hi_ready"), 1)

                    norm(2 * f, lambda: [upper(n) for n in range(2)])
                    for b in range(4):
                        ready = sig("uT_ready") if b % 2 == 0 else sig("uT_ready_a")
                        act.wait_ge(ready, l * 6 + 4 * f + b // 2 + 1)
                        A.copy(u_hi[:, 2 * b:2 * b + 2, :], uT[:, 2 * b:2 * b + 2, :]).then_inc(sig("u_hi_ready"), 1)
                    upper(2)
                    for n, (kind, i) in enumerate(FFN_SLOTS):
                        if kind == "up":
                            act.wait_ge(sig("ffn_ps"), l * 2 * FT + f * FT + i + 1)
                            if i >= 2:
                                act.wait_ge(sig("hid_done"), l * 2 * FT + f * FT + i - 1)
                            A.activation(sa2[:, i % 2, :], bank(4 + i % 4)[:, 0:T],
                                         ACT.Silu).then_inc(sig("silu2_ready"), 1)
                        upper(n + SPLITS)

                ffn(0, 0)
                norm(1)
                act.wait_ge(sig("qkvp_ps"), l + 1)
                for t in range(TT):
                    A.copy(qk[:, t, 0:8, :].rearrange("p (j f) c -> p j f c", f=2),
                           bank(t).rearrange("p (f j c) -> p j f c", f=2, j=4))
                    last = A.copy(qk[:, t, 8:10, :],
                                  bank(2)[:, t * T:t * T + P].rearrange("p (f c) -> p f c", f=2))
                last.then_inc(sig("qk_kept"), 1)
                for t in range(TT):
                    A.copy(v2[:, t, :], bank(2)[:, t * T + P:(t + 1) * T])
                    last = A.copy(p_tok[:, t, :], bank(3 + t))
                last.then_inc(sig("vp_kept"), 1)

                def gate(k):
                    act.wait_ge(sig("gate_ps"), l * KD + k + 1)
                    for g in range(2):
                        last = A.activation(sgate[:, k, g, :], bank(6 + k % 2)[:, g * T:(g + 1) * T], ACT.Sigmoid,
                                            bias=lcol("b_gates", 8 * g + k))
                    last.then_inc(sig("gate_kept"), 1)

                for k in range(4):
                    gate(k)
                act.wait_ge(sig("qkT_ps"), l + 1)
                A.copy(q2T[:, 0:2, :], bank(0).rearrange("p (j t) -> p j t", j=2))
                A.copy(q2T[:, 2:4, :], bank(1).rearrange("p (j t) -> p j t", j=2))
                A.copy(k2T, bank(2)[:, 0:T]).then_inc(sig("qkT_kept"), 1)
                for k in range(4, KD):
                    gate(k)
                for t in range(TT):
                    act.wait_ge(sig("att_sub"), l * TT + t + 1)
                    A.activation(att[:, t, :, :], att[:, t, :, :], ACT.Exp)
                    A.activation(mst[:, t, 1, :], mst[:, t, 1, :], ACT.Exp).then_inc(sig("att_exp"), 1)
                for c in range(1, 8, 2):
                    act.wait_ge(sig("attT_ps"), l * 8 + c + 1)
                    A.copy(attT[:, (c // 2) % 2, (c % 2) * 4:(c % 2) * 4 + 4, (c // 4) * P:(c // 4 + 1) * P],
                           bank(4 + c % 2).rearrange("p (h q) -> p h q", h=4)).then_inc(sig("attT_kept_a"), 1)
                act.wait_ge(sig("a2T_ps"), l + 1)
                A.copy(a2T, ps[:, 0:2, :].rearrange("p b (j t) -> p (b j) t", j=2)).then_inc(sig("a2T_kept"), 1)
                act.wait_ge(sig("pooled_ps"), l + 1)
                A.copy(pooledT, ps[:, 2:4, :].rearrange("p b (j t) -> p (b j) t", j=2)).then_inc(sig("pooled_kept"), 1)
                for g in range(4):
                    if g == 0:
                        act.wait_ge(sig("mixed_ps"), l + 1)
                    last = A.activation(mixT[:, g, :], bank(4 + g // 2)[:, (g % 2) * T:(g % 2 + 1) * T], ACT.Copy,
                                        scale=lcol("pool_scale", g))
                last.then_inc(sig("mixT_ready"), 1)
                ffn(1, 54)
                step.close()

            act.dma_start(fin_rows[:, :], d["fin_rows"][1]).then_inc(sig("fin_loaded"), 16)
            act.wait_ge(sig("h_ready"), LAYERS * 3 + 1)
            step = Link(act, sig("act_step"))
            step.n = before
            root_mean_square(step, x_tok, sq, 0, sig("rms_ready"))

        @block.vector
        def _(dve):
            V = nc.vector
            step = Link(dve, sig("dve_step"))
            V.memset(silu_c[:, :, :], 0.0)
            V.memset(v_tok[:, :, :, P:], 1.0).then_inc(sig("cleared"), 1)

            def normalize(n, at, src, out, rms):
                dve.wait_ge(rms, n)
                step(V.reciprocal(stat[:, at, 0:2], stat[:, at, 2:4]))
                for t in range(TT):
                    last = V.tensor_scalar(out[:, t, :], src[:, t, :], stat[:, at, t:t + 1], None, ALU.mult)
                return last

            def sine_argument(n, bias):
                dve.wait_ge(sig("filter_ps"), n + 1)
                a, k = arg[0:HID, :], turns[0:HID, :]
                step(V.tensor_scalar(a, bank(n)[0:HID, 0:T], bias, None, ALU.add))
                step(V.tensor_scalar(k, a, 1 / (2 * np.pi), 12582912.0, ALU.mult, ALU.add))
                step(V.tensor_scalar(k, k, 12582912.0, None, ALU.subtract))
                step(V.scalar_tensor_tensor(a, k, -6.28125, a, ALU.mult, ALU.add))
                step(V.scalar_tensor_tensor(a, k, -(2 * np.pi - 6.28125), a, ALU.mult, ALU.add))
                V.tensor_scalar(a, a, 3.14159, -3.14159, ALU.min, ALU.max).then_inc(sig("arg_ready"), 1)

            dve.wait_ge(sig("cols_loaded"), 16)
            sine_argument(0, col("f_b1", rows=HID))
            dve.wait_ge(sig("hid_ready"), 1)
            sine_argument(1, col("f_b2", rows=HID))
            decay = filt[:, FILT["decay"]:].rearrange("p (t c) -> p t c", t=TT)
            for o in range(ORDERS):
                dve.wait_ge(sig("filter_ps"), 3 + o)
                if o == 1:
                    dve.wait_ge(sig("spec_ready"), 1)
                for t in range(TT):
                    b0, b1 = bank((2 + 4 * o + t) % 8), bank((4 + 4 * o + t) % 8)
                    V.tensor_tensor(pm_tmp[:, 0, :], b0, decay[:, t, :], ALU.mult)
                    step(V.scalar_tensor_tensor(pm_tmp[:, 1, :], b1, col("not_first", t), decay[:, t, :],
                                                ALU.mult, ALU.mult))
                    V.tensor_tensor(pm[:, 0, t, :], pm_tmp[:, 0, :], pm_tmp[:, 1, :], ALU.add)
                    last = V.tensor_tensor(pm[:, 1, t, :], pm_tmp[:, 0, :], pm_tmp[:, 1, :], ALU.subtract)
                    if t == 0:
                        step(last)
                last.then_inc(sig("pm_ready"), 1)
                dve.wait_ge(sig("pm_ready"), o + 1)
            V.memset(mrow, 0.0)
            step(V.memset(zrow, 0.0))
            dve.wait_ge(sig("x_loaded"), 16)
            dve.wait_ge(sig("ctx_loaded"), 16)
            step(normalize(1, 0, x_tok, xn, sig("rms_ready")))
            normalize(2, 1, cn, cn, sig("rms_ready")).then_inc(sig("norm_ready"), 1)

            def ada_row(r, b):
                dve.wait_ge(sig("ada_ps"), r + 1)
                V.tensor_tensor(ada_rows[:, r, :], bank(b), ada_rows[:, r, :], ALU.add).then_inc(sig("ada_row"), 1)

            def ada_col(r, b):
                dve.wait_ge(sig("ada_T_ps"), r + 1)
                v = bank(b).rearrange("p (q g s) -> p q g s", q=4, g=4)
                for s in range(2):
                    out = ada_cols[:, s, 16 * r:16 * r + 16].rearrange("p (g q) -> p q g", q=4)
                    last = V.tensor_copy(out, v[:, :, :, s])
                last.then_inc(sig("ada_cols_ready"), 1)

            dve.wait_ge(sig("ada_bias_loaded"), 16)
            ada_row(0, 6)
            ada_col(0, 7)
            dve.wait_ge(sig("ada_cols_ready"), 1)
            for s in range(2):
                last = V.scalar_tensor_tensor(mod1[:, s, :], ada_cols[:, s, 8:16], 1.0, col("g_mix", 0, 8),
                                              ALU.add, ALU.mult)
            last.then_inc(sig("mod1_ready"), 1)
            dve.wait_ge(sig("mod1_ready"), 1)
            for k in range(1, KD, 2):
                dve.wait_ge(sig("hT_ps"), k + 1)
                for s in range(2):
                    last = V.tensor_scalar(hT[:, k, s * T:(s + 1) * T], ps[:, k, s * T:(s + 1) * T],
                                           mod1[:, s, k:k + 1], ada_cols[:, s, k:k + 1], ALU.mult, ALU.add)
                last.then_inc(sig("hT_ready"), 1)

            dve.wait_ge(sig("unit_kept"), 1)
            V.tensor_tensor(gates[0:H], gates[0:H], cols[0:H, COLS["b_gate"]:COLS["b_gate"] + 4].unsqueeze(2)
                            .broadcast_to([H, 4, 2 * T]), ALU.add).then_inc(sig("gates_biased"), 1)

            def short_conv(c, dst, taps, parts):
                dve.wait_ge(sig("unit_kept"), 1 + c + 1 if c < 8 else 1 + c + 4 + 1)
                width = sum(n * w for _, n, w in parts)
                u = raw[:, c % 4, 0:width]
                step(V.tensor_scalar(dst[:, 0:width], u, taps[:, 1:2], None, ALU.mult))
                for start, n, w in parts:
                    ui = u[:, start:start + n * w].rearrange("p (n w) -> p n w", w=w)
                    yi = dst[:, start:start + n * w].rearrange("p (n w) -> p n w", w=w)
                    step(V.scalar_tensor_tensor(yi[:, :, 1:], ui[:, :, 0:w - 1], taps[:, 0:1], yi[:, :, 1:],
                                                ALU.mult, ALU.add))
                    last = V.scalar_tensor_tensor(yi[:, :, 0:w - 1], ui[:, :, 1:], taps[:, 2:3],
                                                  yi[:, :, 0:w - 1], ALU.mult, ALU.add)
                    if start + n * w < width:
                        step(last)
                last.then_inc(sig("conv_done"), 1)

            on_x, on_ctx = (0, T // ROW, ROW), (T, 1, T)
            for h in range(H):
                short_conv(h, kT[:, h, :], col("ml_conv", 3 * (4 + h), 3), (on_x, on_ctx))
            dve.wait_ge(sig("softplus_ready"), 1)
            dve.wait_ge(sig("gates_biased"), 1)
            step(V.scalar_tensor_tensor(g_forget[0:H], g_forget[0:H], 0.0, lnb[0:H], ALU.min, ALU.subtract))

            def along(v, s, part):
                w = v[0:H, s, part * T:(part + 1) * T]
                return w if s == 0 else w[:, ::-1]

            for s in range(2):
                for part in range(2):
                    last = V.tensor_tensor_scan(along(bcum, s, part), along(g_forget, s, part), zrow[0:H, :], 0.0,
                                                ALU.add, ALU.add)
            step(last)
            step(V.tensor_tensor(g_in[0:H], g_in[0:H], bcum[0:H], ALU.subtract))
            step(V.tensor_reduce(mcols[0:H, 0:2], g_in[0:H, :, T:], X, ALU.max))
            step(V.tensor_scalar(mcols[0:H, 2:4], mcols[0:H, 0:2], 0.0, None, ALU.max))
            for s in range(2):
                end = 2 * T - 1 if s == 0 else T
                last = V.tensor_tensor(mcols[0:H, 4 + s:5 + s], mcols[0:H, 2 + s:3 + s],
                                       bcum[0:H, s, end:end + 1], ALU.add)
            step(last)
            for s in range(2):
                V.tensor_scalar(g_in[0:H, s, T:], g_in[0:H, s, T:], mcols[0:H, 2 + s:3 + s], None, ALU.subtract)
                m = mrow[0:H, s, :] if s == 0 else mrow[0:H, s, ::-1]
                step(V.tensor_tensor_scan(m, along(g_in, s, 0), along(g_in, s, 0), mcols[0:H, 4 + s:5 + s],
                                          ALU.max, ALU.max))
            for s in range(2):
                V.tensor_scalar(lnb[0:H, s, 0:T], mrow[0:H, s, :], mcols[0:H, 4 + s:5 + s], None, ALU.subtract)
                last = V.tensor_tensor(lnb[0:H, s, T:], mrow[0:H, s, :], bcum[0:H, s, 0:T], ALU.add)
            last.then_inc(sig("gate_rows"), 1)
            for h in range(H):
                short_conv(4 + h, qT[:, h, :], col("ml_conv", 3 * h, 3), (on_x,))
            dve.wait_ge(sig("vbias_loaded"), 16)
            for t in range(2 * TT):
                dve.wait_ge(sig("v_ps"), t + 1)
                V.tensor_tensor(v_tok[:, t, :, 0:P], bank(4 + t).rearrange("p (h e) -> p h e", h=H),
                                vbias[:, :].rearrange("p (h e) -> p h e", h=H), ALU.add).then_inc(sig("v_kept"), 1)
            for c in range(12):
                short_conv(8 + c, hy[:, c, :], col("hy_conv", 3 * c, 3), (on_x,))
            dve.wait_ge(sig("gcols_ps"), 1)
            step(V.tensor_copy(gcols, bank(4)[:, 0:64].rearrange("p (n s t h) -> p n s t h", n=4, s=2, t=TT)))
            V.tensor_scalar(gcols[:, 1], gcols[:, 1], QSCALE, None, ALU.mult).then_inc(sig("gcols_ready"), 1)
            dve.wait_ge(sig("gcols_ready"), 1)

            for h in range(H):
                dve.wait_ge(sig("kc_ps"), h + 1)
                if h >= 1:
                    dve.wait_ge(sig("state_ps"), h)
                for t in range(TT):
                    for s in range(2):
                        last = V.tensor_scalar(kw[:, t, s, :], bank(5)[:, t * P:(t + 1) * P],
                                               gcols[:, 3, s, t, h:h + 1], None, ALU.mult)
                last.then_inc(sig("kw_ready"), 1)
            ada_row(1, 2)
            for h in range(H):
                dve.wait_ge(sig("st_ps"), h + 1)
                if h >= 1:
                    dve.wait_ge(sig("intra_ps"), h)
                for s in range(2):
                    for t in range(TT):
                        a = P - t * P if s == 0 else t * P
                        a = (P if t == 0 else 0) if s == 0 else (P if t == 0 else 0)
                        last = V.scalar_tensor_tensor(ee[:, s, t, :], bank(5)[:, s * T:(s + 1) * T],
                                                      gcols[:, 0, s, t, h:h + 1], causal[:, s, a:a + T],
                                                      ALU.subtract, ALU.max)
                last.then_inc(sig("gaps_ready"), 1)
                dve.wait_ge(sig("decay_ready"), h + 1)
                for s in range(2):
                    e2 = ee[:, s, :, :].rearrange("p t q -> p (t q)")
                    last = V.scalar_tensor_tensor(e2, bank(4), QSCALE, e2, ALU.mult, ALU.mult)
                last.then_inc(sig("pairs_ready"), 1)
                if h == 0:
                    ada_col(1, 3)
                elif h == 2:
                    ada_row(2, 2)
                elif h == 3:
                    ada_col(2, 3)
                dve.wait_ge(sig("inter_kept"), h + 1)
                dve.wait_ge(sig("intra_ps"), h + 1)
                for t in range(TT):
                    step(V.tensor_tensor(inter[:, t, :], bank(6 + t)[:, 0:2 * VW], inter[:, t, :], ALU.add))
                n = inter.rearrange("p t (s e) -> p t s e", s=2)[:, :, :, P]
                step(V.scalar_tensor_tensor(den, n, -1.0, n, ALU.mult, ALU.max))
                step(V.tensor_tensor(den, den, gcols[:, 2, :, :, h].rearrange("p s t -> p t s"), ALU.max))
                step(V.reciprocal(den, den))
                for t in range(TT):
                    step(V.tensor_scalar(hm[:, t, h, :], inter[:, t, 0:P], den[:, t, 0:1], None, ALU.mult))
                    last = V.scalar_tensor_tensor(hm[:, t, h, :], inter[:, t, VW:VW + P], den[:, t, 1:2],
                                                  hm[:, t, h, :], ALU.mult, ALU.add)
                last.then_inc(sig("head_done"), 1)
            dve.wait_ge(sig("head_done"), H)
            h8 = hm.rearrange("p t h e -> p (t h) e")
            step(V.tensor_tensor(hsq, h8, h8, ALU.mult))
            V.tensor_reduce(hstat, hsq, X, ALU.add).then_inc(sig("hsum_ready"), 1)
            dve.wait_ge(sig("hrms_ready"), 1)
            step(V.reciprocal(hstat, hstat))
            V.tensor_tensor(h8, h8, hstat.unsqueeze(2).broadcast_to([P, TT * H, P]),
                            ALU.mult).then_inc(sig("hm_ready"), 1)
            dve.wait_ge(sig("hmT_ps"), 1)
            for h in range(H):
                last = V.scalar_tensor_tensor(oT[:, h, :], bank(6 + h // 2)[:, (h % 2) * T:(h % 2 + 1) * T],
                                              col("ml_g", h), oT[:, h, :], ALU.mult, ALU.mult)
            last.then_inc(sig("yb_ready"), 1)

            for o in range(ORDERS):
                dve.wait_ge(sig("signal_ps"), o + 1)
                for t in range(TT):
                    re, im = bank(t), bank(2 + t)
                    V.tensor_tensor(yt[:, 0, :], re, spec[:, o, 0, t, :], ALU.mult)
                    V.tensor_tensor(yt[:, 1, :], im, spec[:, o, 1, t, :], ALU.mult)
                    V.tensor_tensor(yt[:, 2, :], im, spec[:, o, 0, t, :], ALU.mult)
                    step(V.tensor_tensor(yt[:, 3, :], re, spec[:, o, 1, t, :], ALU.mult))
                    V.tensor_tensor(yspec[:, 0, t, :], yt[:, 0, :], yt[:, 1, :], ALU.subtract)
                    last = V.tensor_tensor(yspec[:, 1, t, :], yt[:, 2, :], yt[:, 3, :], ALU.add)
                    if t == 0:
                        step(last)
                last.then_inc(sig("yspec_ready"), 1)
                dve.wait_ge(sig("conv_ps"), o + 1)
                for j in range(4):
                    z = hy[:, 4 * o + j, :]
                    step(V.scalar_tensor_tensor(z, z, col("skip", 4 * o + j),
                                                bank(4 + j // 2)[:, (j % 2) * T:(j % 2 + 1) * T], ALU.mult, ALU.add))
                    last = V.tensor_tensor(hy[:, 4 * o + 4 + j, :], hy[:, 4 * o + 4 + j, :], z, ALU.mult)
                last.then_inc(sig("z_done"), 1)
            dve.wait_ge(sig("unit_kept"), 41)
            for k in range(KD):
                dve.wait_ge(sig("branch_ps"), k + 1)
                m = merge[:, k, :, :].rearrange("p g t -> p (g t)")
                step(V.tensor_tensor(m, bank(k % 4), m, ALU.mult))
                V.tensor_tensor(merge[:, k, 0, :], merge[:, k, 0, :], merge[:, k, 1, :],
                                ALU.add).then_inc(sig("merged"), 1)

            def two_banks(b):
                return ps[:, b:b + 2, :].rearrange("p b n -> p (b n)")

            dve.wait_ge(sig("grow_ready"), 1)
            dve.wait_ge(sig("mixed1_ps"), 1)
            for t in range(TT):
                step(V.tensor_tensor(gtmp[:, t, :], two_banks(4 + 2 * t), grow, ALU.mult))
                last = V.tensor_tensor(x_tok[:, t, :], x_tok[:, t, :], gtmp[:, t, :], ALU.add)
            last.then_inc(sig("x1_ready"), 1)
            dve.wait_ge(sig("ada_cols_ready"), 3)
            step(V.scalar_tensor_tensor(mod2[:, :], ada_cols[:, 0, 32:40], 1.0, col("g_ffn", 0, 8),
                                        ALU.add, ALU.mult))
            V.memset(zeros, 0.0)
            normalize(3, 0, x_tok, xn, sig("rms_ready")).then_inc(sig("norm_ready"), 1)

            dve.wait_ge(sig("logits_ps"), 1)
            lg = bank(4)[:, 0:TT * NE].rearrange("p (t e) -> p t e", t=TT)
            step(V.tensor_reduce(esum, lg, X, ALU.max))
            V.tensor_tensor(aff, lg, esum.unsqueeze(2).broadcast_to([P, TT, NE]),
                            ALU.subtract).then_inc(sig("logits_ready"), 1)
            dve.wait_ge(sig("exp_ready"), 1)
            step(V.tensor_reduce(esum, aff, X, ALU.add))
            step(V.reciprocal(esum, esum))
            V.tensor_tensor(aff, aff, esum.unsqueeze(2).broadcast_to([P, TT, NE]),
                            ALU.mult).then_inc(sig("aff_ready"), 1)
            dve.wait_ge(sig("affT_ps"), 1)
            step(V.tensor_copy(affT[0:NE, :], bank(5)[0:NE, 0:T]))
            for n in range(CAP // 8):
                v, i = topv[0:NE, 8 * n:8 * n + 8], topi[0:NE, 8 * n:8 * n + 8]
                step(V.max(v, affT[0:NE, :]))
                step(V.max_index(i, v, affT[0:NE, :]))
                step(V.match_replace(affT[0:NE, :], v, affT[0:NE, :], -1.0))
            step(V.tensor_copy(topf[0:NE, :], topi[0:NE, :]))
            dve.wait_ge(sig("bmask_loaded"), 16)
            V.tensor_tensor(bdiag[0:NE], bmask[0:NE], topf[0:NE, :].unsqueeze(1).broadcast_to([NE, NE, CAP]), ALU.mult)
            V.tensor_copy(rep[0:NE, 0], topf[0:NE, :].unsqueeze(1).broadcast_to([NE, 4, CAP]))
            V.tensor_copy(rep[0:NE, 1], topv[0:NE, :].unsqueeze(1).broadcast_to([NE, 4, CAP])).then_inc(sig("top_ready"), 1)
            dve.wait_ge(sig("top_ps"), 1)
            for t in range(TT):
                last = V.tensor_scalar(sel[:, t, :], bank(6), col("token", t), None, ALU.is_equal)
            last.then_inc(sig("sel_ready"), 1)
            step(V.tensor_copy(igcols, bank(7)[:, 0:2 * NE].rearrange("p (a e) -> p a e", a=2)))
            for k in range(0, KD, 2):
                dve.wait_ge(sig("xg_ps"), k + 1)
                V.tensor_scalar(xgT[:, k, :], bank(k % 4), mod2[:, k:k + 1], ada_cols[:, 0, 24 + k:25 + k],
                                ALU.mult, ALU.add).then_inc(sig("xg_ready"), 1)

            dve.wait_ge(sig("xg_ready"), KD // 2)
            dve.wait_ge(sig("xg_ready_a"), KD // 2)
            with dve.Fori(0, NE) as e:
                dve.wait_ge(sig("combined"), e + 1)
                V.tensor_copy(xe, xgT[:, :, bass.ds(e * CAP, CAP)]).then_inc(sig("xe_ready"), 1)
                V.tensor_scalar(scat, iota, igcols[:, 0, bass.ds(e, 1)], igcols[:, 1, bass.ds(e, 1)],
                                ALU.is_equal, ALU.mult).then_inc(sig("scat_ready"), 1)
                dve.wait_ge(sig("b_ps"), e + 1)
                dve.wait_ge(sig("sa_ready"), e + 1)
                V.tensor_tensor(hid_e, sa, bank(5), ALU.mult).then_inc(sig("hid_e_ready"), 1)
                dve.wait_ge(sig("hTe_ps"), e + 1)
                V.tensor_copy(hTe, bank(4).rearrange("p (q c) -> p q c", q=4)).then_inc(sig("hTe_ready"), 1)

            step2 = Link(dve, sig("dve_step2"))
            dve.wait_ge(sig("grow_ready"), 2)
            dve.wait_ge(sig("moe_ps"), 1)
            for t in range(TT):
                step2(V.tensor_tensor(gtmp2[:, t, :], two_banks(2 * t), grow2, ALU.mult))
                last = V.tensor_tensor(x_tok[:, t, :], x_tok[:, t, :], gtmp2[:, t, :], ALU.add)
            last.then_inc(sig("x2_ready"), 1)

            def final_norm(n, done):
                dve.wait_ge(sig("rms_ready"), n)
                step2(V.reciprocal(stat[:, 0, 0:2], stat[:, 0, 2:4]))
                for t in range(TT):
                    last = V.scalar_tensor_tensor(x_tok[:, t, :], x_tok[:, t, :], stat[:, 0, t:t + 1], fin_rows[:, :],
                                                  ALU.mult, ALU.mult)
                last.then_inc(done, 1)

            dve.wait_ge(sig("fin_loaded"), 16)
            final_norm(4, sig("h_ready"))

            with dve.Fori(0, LAYERS) as l:
                step = Link(dve, sig("dve_layer_step"), l, 3 + 1 + 2 * 5 + KD)

                def norm(n, meanwhile=None):
                    dve.wait_ge(sig("rms2_ready"), l * 3 + n + 1)
                    step(V.reciprocal(stat[:, 0, 0:2], stat[:, 0, 2:4]))
                    for t in range(TT):
                        last = V.tensor_scalar(xn[:, t, :], x_tok[:, t, :], stat[:, 0, t:t + 1], None, ALU.mult)
                    last.then_inc(sig("norm2_ready"), 1)
                    if meanwhile:
                        meanwhile()
                    dve.wait_ge(sig("lcols_loaded"), l * 16 + 16)
                    for b in (0, 2):
                        dve.wait_ge(sig("uT_ps"), l * 12 + n * 4 + b + 1)
                        for k in (2 * b, 2 * b + 1):
                            last = V.tensor_scalar(uT[:, k, :], bank(b)[:, (k % 2) * T:(k % 2 + 1) * T],
                                                   lcol("norm", 8 * n + k), None, ALU.mult)
                        last.then_inc(sig("uT_ready"), 1)

                def ffn(f, at):
                    first = FIRST_SLOTS + NE * EXPERT_SLOTS + at
                    slots0 = l * 2 * len(FFN_SLOTS) + f * len(FFN_SLOTS)

                    def lower(n):
                        if n < len(FFN_SLOTS):
                            dve.wait_ge(sig("w_hi_ready"), slots0 + n + 1)
                            V.tensor_tensor(w_lo[:, n % SPLITS, :], ring[:, (first + n) % RING, :],
                                            w_hi[:, n % SPLITS, :].bitcast(F32),
                                            ALU.subtract).then_inc(sig("w_ready"), 1)

                    norm(2 * f, lambda: lower(0))
                    for b in range(4):
                        dve.wait_ge(sig("u_hi_ready"), l * 8 + f * 4 + b + 1)
                        V.tensor_tensor(u_lo[:, 2 * b:2 * b + 2, :], uT[:, 2 * b:2 * b + 2, :],
                                        u_hi[:, 2 * b:2 * b + 2, :].bitcast(F32),
                                        ALU.subtract).then_inc(sig("u_ready"), 1)
                    lower(1)
                    lower(2)
                    for n, (kind, i) in enumerate(FFN_SLOTS):
                        if kind == "up":
                            dve.wait_ge(sig("silu2_ready"), l * 2 * FT + f * FT + i + 1)
                            if i >= 4:
                                dve.wait_ge(sig("down_step"), l * FT + f * (FT // 2) + (i - 4) // 2 + 1)
                            b = bank(4 + i % 4)[:, T:]
                            V.tensor_tensor(hid_hi[:, i % 4, :], b, sa2[:, i % 2, :], ALU.mult)
                            V.tensor_tensor(hid[:, i % 2, :], b, sa2[:, i % 2, :], ALU.mult).then_inc(sig("hid_mid"), 1)
                            dve.wait_ge(sig("hid_mid"), l * 2 * FT + f * FT + i + 1)
                            V.tensor_tensor(hid_lo[:, i % 4, :], hid[:, i % 2, :], hid_hi[:, i % 4, :].bitcast(F32),
                                            ALU.subtract).then_inc(sig("hid_done"), 1)
                        lower(n + SPLITS)
                    dve.wait_ge(sig("down_step"), l * FT + (f + 1) * (FT // 2))
                    for t in range(TT):
                        last = V.scalar_tensor_tensor(x_tok[:, t, :], two_banks(2 * t), 0.5, x_tok[:, t, :],
                                                      ALU.mult, ALU.add)
                    last.then_inc(sig("h_ready"), 1)

                ffn(0, 0)
                norm(1)
                dve.wait_ge(sig("qk_kept"), l + 1)
                dve.wait_ge(sig("tabs2_loaded"), 16)
                q1, q2 = qk[:, :, :, 0:8], qk[:, :, :, 8:16]

                def table(f):
                    return rope[:, f].unsqueeze(2).broadcast_to([P, TT, 10, 8])

                tmp = [rtmp[:, i].rearrange("p t (h c) -> p t h c", c=8) for i in range(4)]
                V.tensor_tensor(tmp[0], q1, table(0), ALU.mult)
                V.tensor_tensor(tmp[1], q2, table(1), ALU.mult)
                V.tensor_tensor(tmp[2], q2, table(0), ALU.mult)
                step(V.tensor_tensor(tmp[3], q1, table(1), ALU.mult))
                V.tensor_tensor(q1, tmp[0], tmp[1], ALU.subtract)
                V.tensor_tensor(q2, tmp[2], tmp[3], ALU.add).then_inc(sig("rope_ready"), 1)
                for t in range(TT):
                    dve.wait_ge(sig("scores_ps"), l * TT + t + 1)
                    a = att[:, t, :, :]
                    m = mst[:, t, 0, :]
                    V.scalar_tensor_tensor(a, ps[:, 0:4, :].rearrange("p b (f k) -> p (b f) k", f=2), 0.125,
                                           amask[:, t, :].unsqueeze(1).broadcast_to([P, 8, T]),
                                           ALU.mult, ALU.add).then_inc(sig("scores_kept"), 1)
                    dve.wait_ge(sig("scores_kept"), l * TT + t + 1)
                    step(V.tensor_reduce(m, a, X, ALU.max))
                    step(V.tensor_tensor(m, m, lcol("sink", 0, 8), ALU.max))
                    V.tensor_tensor(mst[:, t, 1, :], lcol("sink", 0, 8), m, ALU.subtract)
                    V.tensor_tensor(a, a, m.unsqueeze(2).broadcast_to([P, 8, T]),
                                    ALU.subtract).then_inc(sig("att_sub"), 1)
                    dve.wait_ge(sig("att_exp"), l * TT + t + 1)
                    step(V.tensor_reduce(m, a, X, ALU.add))
                    step(V.tensor_tensor(m, m, mst[:, t, 1, :], ALU.add))
                    step(V.reciprocal(m, m))
                    V.tensor_tensor(a, a, m.unsqueeze(2).broadcast_to([P, 8, T]),
                                    ALU.mult).then_inc(sig("att_ready"), 1)
                for c in range(0, 8, 2):
                    dve.wait_ge(sig("attT_ps"), l * 8 + c + 1)
                    V.tensor_copy(attT[:, (c // 2) % 2, 0:4, (c // 4) * P:(c // 4 + 1) * P],
                                  bank(4).rearrange("p (h q) -> p h q", h=4)).then_inc(sig("attT_kept"), 1)
                for k in range(KD):
                    dve.wait_ge(sig("branch2_ps"), l * KD + k + 1)
                    g = sgate[:, k, :, :].rearrange("p g t -> p (g t)")
                    step(V.tensor_tensor(g, bank(6 + k % 2), g, ALU.mult))
                    V.tensor_tensor(mT[:, k, :], sgate[:, k, 0, :], sgate[:, k, 1, :],
                                    ALU.add).then_inc(sig("mT_ready"), 1)
                dve.wait_ge(sig("mixer_ps"), l + 1)
                for t in range(TT):
                    last = V.tensor_tensor(x_tok[:, t, :], two_banks(2 * t), x_tok[:, t, :], ALU.add)
                last.then_inc(sig("h_ready"), 1)
                ffn(1, 54)
                step.close()

            dve.wait_ge(sig("fin_loaded"), 32)
            final_norm(5, sig("out_ready"))

        @block.tensor
        def _(pe):
            M = nc.tensor
            pending = [0]

            def mm(out, lhsT, rhs, start=True, stop=True, ready=None, free=0, **more):
                ins = M.matmul(out, lhsT, rhs, start=start, stop=stop, **more)
                pending[0] += free
                if ready is not None:
                    ins.then_inc(ready, 1)
                elif pending[0]:
                    ins.then_inc(sig("slot_used"), pending[0])
                    pending[0] = 0

            def turn(out, src, rows=P, ready=None):
                ins = M.transpose(out, src, ident[0:rows, 0:rows])
                if ready is not None:
                    ins.then_inc(ready, 1)
                elif pending[0]:
                    ins.then_inc(sig("slot_used"), pending[0])
                    pending[0] = 0

            def slot(n, turns=0):
                pe.wait_ge(sig(f"slot_loaded{n % RING}"), (turns + n // RING) * 16 + 16)
                return ring[:, n % RING, :]

            pe.wait_ge(sig("filt_loaded"), 16)
            f = {k: filt[:, v:] for k, v in FILT.items()}
            mm(bank(0)[0:HID, 0:T], f["w1"][0:EMB, 0:HID], f["z"][0:EMB, 0:T], ready=sig("filter_ps"))
            pe.wait_ge(sig("hid_ready"), 1)
            mm(bank(1)[0:HID, 0:T], f["w2"][0:HID, 0:HID], hid1[0:HID, :], ready=sig("filter_ps"))
            pe.wait_ge(sig("hid_ready"), 2)
            for o in range(ORDERS):
                for side in range(2):
                    for t in range(TT):
                        last = side == 1 and t == 1
                        mm(bank((2 + 4 * o + 2 * side + t) % 8), hid2[0:HID, t * P:(t + 1) * P],
                           f["w3"][0:HID, (2 * o + side) * HYC:(2 * o + side + 1) * HYC],
                           ready=sig("filter_ps") if last else None)
            pe.wait_ge(sig("tabs_loaded"), 16)
            for o in range(ORDERS):
                pe.wait_ge(sig("pm_ready"), o + 1)
                if o == 1:
                    pe.wait_ge(sig("spec_kept"), 1)
                for j in range(2):
                    for k in range(TT):
                        for t in range(TT):
                            mm(bank(2 + 2 * j + k), dft[:, j, t, k * P:(k + 1) * P], pm[:, j, t, :],
                               start=t == 0, stop=t == 1,
                               ready=sig("spec_ready") if j == k == t == 1 else None)

            def ada(b, steps, first):
                for k in steps:
                    w = slot(first + k)
                    for g in range(4):
                        mm(bank(b)[32 * g:32 * g + 32, :], silu_c[:, k, :], w[:, 512 * g:512 * g + 512],
                           start=k == 0, stop=k == KD - 1, free=int(g == 3),
                           ready=sig("ada_ps") if k == KD - 1 and g == 3 else None)

            def ada_turn(r, b):
                pe.wait_ge(sig("const_loaded"), 16)
                pe.wait_ge(sig("ada_row"), r + 1)
                for q in range(4):
                    turn(bank(b)[:, q * P:(q + 1) * P], ada_rows[:, r, q * P:(q + 1) * P],
                         ready=sig("ada_T_ps") if q == 3 else None)

            pe.wait_ge(sig("silu_ready"), 1)
            ada(6, range(KD), 0)
            ada_turn(0, 7)

            pe.wait_ge(sig("norm_ready"), 1)
            pe.wait_ge(sig("spec_kept"), 2)
            pe.wait_ge(sig("mod1_ready"), 1)
            for k in range(KD):
                for t in range(2 * TT):
                    src = (xn if t < TT else cn)[:, t % TT, k * P:(k + 1) * P]
                    turn(bank(k)[:, t * P:(t + 1) * P], src, ready=sig("hT_ps") if t == 3 else None)
            pe.wait_ge(sig("hT_ready"), KD // 2)
            pe.wait_ge(sig("hT_ready_a"), KD // 2)

            def unit_bank(n):
                if n >= 4:
                    pe.wait_ge(sig("unit_kept"), n - 3)
                return bank(n % 4)

            pe.wait_ge(sig("wgate_loaded"), 16)
            b = unit_bank(0)
            for k in range(KD):
                for g in range(4):
                    mm(b[32 * g:32 * g + H, :], wgate[:, k, 4 * g:4 * g + H], hT[:, k, :], start=k == 0,
                       stop=k == KD - 1, ready=sig("unit_ready") if k == KD - 1 and g == 3 else None)

            def features(units, at, width):
                for i, n in enumerate(units):
                    w = slot(at + i // 2)
                    b = unit_bank(n)
                    for k in range(KD):
                        a = (i % 2) * 1024 + k * P
                        mm(b[:, 0:width], w[:, a:a + P], hT[:, k, 0:width], start=k == 0, stop=k == KD - 1,
                           free=int(k == KD - 1 and i % 2 == 1), ready=sig("unit_ready") if k == KD - 1 else None)

            features(range(1, 5), 8, 2 * T)
            features(range(5, 9), 10, T)
            for t in range(2 * TT):
                for k in range(KD):
                    w = slot(12 + k // 4)
                    a = (k % 4) * 512
                    mm(bank(4 + t), hT[:, k, t * P:(t + 1) * P], w[:, a:a + 512], start=k == 0, stop=k == KD - 1,
                       free=int(t == 3 and k % 4 == 3), ready=sig("v_ps") if k == KD - 1 else None)
            features(range(9, 13), 14, T)
            features(range(13, 25), 16, T)
            pe.wait_ge(sig("gate_exps"), 1)
            pe.wait_ge(sig("v_kept"), 2 * TT)
            for n, (rows, off) in enumerate(((g_in, 0), (lnb, 0), (lnb, T), (g_in, T))):
                for s in range(2):
                    for t in range(TT):
                        a = off + t * P
                        at = (n * 4 + s * 2 + t) * H
                        turn(bank(4)[:, at:at + H], rows[0:H, s, a:a + P], rows=H,
                             ready=sig("gcols_ps") if n == 3 and s == t == 1 else None)
            features(range(25, 33), 22, T)

            pe.wait_ge(sig("k_ready"), H)
            pe.wait_ge(sig("q_ready"), H)
            pe.wait_ge(sig("gcols_ready"), 1)
            for h in range(H):
                if h >= 1:
                    pe.wait_ge(sig("kw_ready"), h)
                for t in range(TT):
                    turn(bank(5)[:, t * P:(t + 1) * P], kT[:, h, T + t * P:T + (t + 1) * P],
                         ready=sig("kc_ps") if t == 1 else None)
                if h == 0:
                    pe.wait_ge(sig("unit_kept"), 33)
                ada(2, range(2 * h, 2 * h + 2), 26)
                pe.wait_ge(sig("kw_ready"), h + 1)
                if h >= 1:
                    pe.wait_ge(sig("state_kept"), h)
                for s in range(2):
                    for t in range(TT):
                        mm(bank(6)[:, s * VW:(s + 1) * VW], kw[:, t, s, :], v_tok[:, TT + t, h, :],
                           start=t == 0, stop=t == 1, ready=sig("state_ps") if s == t == 1 else None)
            pe.wait_ge(sig("state_kept"), H)
            for h in range(H):
                if h >= 1:
                    pe.wait_ge(sig("pairs_ready"), h)
                for t in range(TT):
                    mm(bank(4)[:, t * T:(t + 1) * T], kT[:, h, t * P:(t + 1) * P], qT[:, h, :])
                for s in range(2):
                    mm(bank(5)[:, s * T:(s + 1) * T], ident[:, h:h + 1].broadcast_to([P, P]), mrow[:, s, :],
                       ready=sig("st_ps") if s == 1 else None)
                if h >= 1:
                    pe.wait_ge(sig("inter_kept"), h)
                for t in range(TT):
                    mm(bank(t)[:, 0:2 * VW], qT[:, h, t * P:(t + 1) * P],
                       states[:, 2 * h:2 * h + 2, :].rearrange("p s e -> p (s e)"),
                       ready=sig("inter_ps") if t == 1 else None)
                if h == 0:
                    ada_turn(1, 3)
                if h < 3:
                    ada(2, range(3 * h, min(3 * h + 3, KD)), 34)
                else:
                    pe.wait_ge(sig("ada_cols_ready"), 2)
                    ada_turn(2, 3)
                pe.wait_ge(sig("pairs_ready"), h + 1)
                if h >= 1:
                    pe.wait_ge(sig("head_done"), h)
                for t in range(TT):
                    for s in range(2):
                        keys = range(0, t + 1) if s == 0 else range(t, TT)
                        for u in keys:
                            mm(bank(6 + t)[:, s * VW:(s + 1) * VW], ee[:, s, u, t * P:(t + 1) * P],
                               v_tok[:, u, h, :], start=u == keys[0], stop=u == keys[-1],
                               ready=sig("intra_ps") if t == s == 1 else None)

            def merge_units(*units):
                for n in units:
                    w = slot(42 + (n - 33) // 2)
                    if n >= 35:
                        pe.wait_ge(sig("unit_kept"), n - 1)
                    for k in range(KD):
                        a = ((n - 33) % 2) * 1024 + k * P
                        last = k == KD - 1
                        mm(bank(6 + n % 2)[:, 0:T], w[:, a:a + P], hT[:, k, 0:T], start=k == 0, stop=last,
                           free=int(last and n % 2 == 0), ready=sig("unit_ready") if last else None)

            pe.wait_ge(sig("conv_done"), 20)
            for o in range(ORDERS):
                if o == 1:
                    pe.wait_ge(sig("z_done"), 1)
                for t in range(TT):
                    for j in range(4):
                        turn(bank(4 + t)[:, j * P:(j + 1) * P], hy[:, 4 * o + j, t * P:(t + 1) * P],
                             ready=sig("z_ps") if t == 1 and j == 3 else None)
                if o == 1:
                    merge_units(37)
                pe.wait_ge(sig("z_kept"), o + 1)
                if o == 0:
                    pe.wait_ge(sig("ada_cols_ready"), 3)
                    pe.wait_ge(sig("inter_kept"), H)
                for j in range(2):
                    for k in range(TT):
                        for t in range(TT):
                            mm(bank(2 * j + k), dft[:, j, t, k * P:(k + 1) * P], z_tok[:, t, :],
                               start=t == 0, stop=t == 1,
                               ready=sig("signal_ps") if j == k == t == 1 else None)
                if o == 0:
                    pe.wait_ge(sig("hm_ready"), 1)
                    for h in range(H):
                        for t in range(TT):
                            turn(bank(6 + h // 2)[:, (h % 2) * T + t * P:(h % 2) * T + (t + 1) * P], hm[:, t, h, :],
                                 ready=sig("hmT_ps") if h == 3 and t == 1 else None)
                    pe.wait_ge(sig("yb_ready"), 1)
                    merge_units(33, 34, 35)
                else:
                    merge_units(38, 39)
                pe.wait_ge(sig("yspec_ready"), o + 1)
                for j in range(4):
                    n = 0
                    for i in range(2):
                        for k in range(TT):
                            mm(bank(4 + j // 2)[:, (j % 2) * T:(j % 2 + 1) * T], yspec[:, i, k, j * P:(j + 1) * P],
                               idft[:, i, k, :], start=n == 0, stop=n == 3,
                               ready=sig("conv_ps") if j == n == 3 else None)
                            n += 1
                merge_units(36 if o == 0 else 40)
            pe.wait_ge(sig("z_done"), ORDERS)

            def branches(at, turns, bank_of, kept, ya, yb, ready):
                for k in range(KD):
                    w = slot(at + k // 2, turns)
                    kept(k)
                    b = bank_of(k)
                    for g, y in enumerate((ya, yb)):
                        for i in range(4):
                            a = (k % 2) * 1024 + g * 512 + i * P
                            last = g == 1 and i == 3
                            mm(b[:, g * T:(g + 1) * T], w[:, a:a + P], y(i), start=i == 0, stop=i == 3,
                               free=int(last and k % 2 == 1), ready=ready if last else None)

            def kept1(k):
                if k >= 4:
                    pe.wait_ge(sig("merged"), k - 3)

            branches(46, 0, lambda k: bank(k % 4), kept1, lambda i: hy[:, 8 + i, :], lambda i: oT[:, i, :],
                     sig("branch_ps"))

            def token_out(at, turns, banks, x, tiles, ready):
                for i in range(tiles // 2):
                    w = slot(at + i, turns)
                    for j in range(2):
                        k = 2 * i + j
                        src = x(k)
                        for t in range(TT):
                            for c in range(2):
                                last = j == t == c == 1
                                mm(bank(banks + 2 * t + c), src[:, t * P:(t + 1) * P],
                                   w[:, j * 1024 + c * 512:j * 1024 + (c + 1) * 512], start=k == 0,
                                   stop=k == tiles - 1, free=int(last),
                                   ready=ready if last and i == tiles // 2 - 1 else None)

            pe.wait_ge(sig("merged"), KD)
            token_out(50, 0, 4, lambda k: merge[:, k, 0, :], KD, sig("mixed1_ps"))
            slot(54)
            slot(55)
            pending[0] += 2
            for g in range(2):
                mm(bank(g), ident[:, 32 * g:32 * g + 1].broadcast_to([P, P]), ada_rows[:, 1, :],
                   ready=sig("grow_ps") if g == 1 else None)
            assert pending[0] == 0

            pe.wait_ge(sig("norm_ready"), 2)
            pe.wait_ge(sig("grow_ready"), 1)
            for k in range(KD):
                for t in range(TT):
                    turn(bank(k // 2)[:, (k % 2) * T + t * P:(k % 2) * T + (t + 1) * P], xn[:, t, k * P:(k + 1) * P],
                         ready=sig("h2T_ps") if k % 2 == 1 and t == 1 else None)
            pe.wait_ge(sig("h2T_ready"), KD)
            pe.wait_ge(sig("wrouter_loaded"), 16)
            for t in range(TT):
                for k in range(KD):
                    mm(bank(4)[:, t * NE:(t + 1) * NE], h2T[:, k, t * P:(t + 1) * P], wrouter[:, k, :],
                       start=k == 0, stop=k == KD - 1, ready=sig("logits_ps") if t == 1 and k == KD - 1 else None)
            pe.wait_ge(sig("aff_ready"), 1)
            for t in range(TT):
                turn(bank(5)[0:NE, t * P:(t + 1) * P], aff[:, t, :], ready=sig("affT_ps") if t == 1 else None)
            pe.wait_ge(sig("top_ready"), 1)
            for a in range(2):
                turn(bank(7)[:, a * NE:(a + 1) * NE], rep[0:NE, a].rearrange("p g c -> p (g c)"), rows=NE)
            mm(bank(6), ones[0:NE, :], bdiag[0:NE].rearrange("p e c -> p (e c)"), ready=sig("top_ps"))
            pe.wait_ge(sig("sel_ready"), 1)
            for k in range(KD):
                if k >= 4:
                    pe.wait_ge(sig("xg_ready") if k % 2 == 0 else sig("xg_ready_a"), (k - 4) // 2 + 1)
                for t in range(TT):
                    mm(bank(k % 4), xn[:, t, k * P:(k + 1) * P], sel[:, t, :], start=t == 0, stop=t == 1,
                       ready=sig("xg_ps") if t == 1 else None)
            pe.wait_ge(sig("xg_ready"), KD // 2)
            pe.wait_ge(sig("xg_ready_a"), KD // 2)
            for b in range(4):
                mm(bank(b), zeros[:, 0:P], zeros, start=True, stop=False, ready=sig("combined") if b == 3 else None)

            turns0 = FIRST_SLOTS // RING
            with pe.Fori(0, NE) as e:
                turns = e * (EXPERT_SLOTS // RING) + turns0
                pe.wait_ge(sig("xe_ready"), e + 1)
                for i, ready in enumerate((sig("a_ps"), sig("b_ps"))):
                    for k in range(KD):
                        w = slot(i * KD + k, turns)
                        for g in range(4):
                            mm(bank(4 + i)[32 * g:32 * g + 32, :], xe[:, k, :], w[:, 512 * g:512 * g + 512],
                               start=k == 0, stop=k == KD - 1, free=int(g == 3),
                               ready=ready if k == KD - 1 and g == 3 else None)
                pe.wait_ge(sig("hid_e_ready"), e + 1)
                for q in range(4):
                    turn(bank(4)[:, q * P:(q + 1) * P], hid_e[:, q * P:(q + 1) * P],
                         ready=sig("hTe_ps") if q == 3 else None)
                pe.wait_ge(sig("hTe_ready"), e + 1)
                for i in range(8):
                    w = slot(2 * KD + i, turns)
                    for c in range(2):
                        for j in range(2):
                            k = 2 * i + j
                            q, g = k % 4, k // 4
                            last = c == j == 1
                            mm(bank(6 + c)[32 * q:32 * q + 32, :], hTe[:, q, 32 * g:32 * g + 32],
                               w[:, j * 1024 + c * 512:j * 1024 + (c + 1) * 512], start=g == 0, stop=g == 3,
                               free=int(last), ready=sig("ye_ps") if last and i == 7 else None)
                pe.wait_ge(sig("ye_ready"), e + 1)
                pe.wait_ge(sig("scat_ready"), e + 1)
                for t in range(TT):
                    for c in range(2):
                        mm(bank(2 * t + c), scat[:, t * P:(t + 1) * P], ye[:, c * 512:(c + 1) * 512],
                           start=False, stop=False,
                           ready=sig("combined") if t == c == 1 else None)
                assert pending[0] == 0
            for b in range(4):
                mm(bank(b), zeros[:, 0:P], zeros, start=False, stop=True,
                   ready=sig("moe_ps") if b == 3 else None)
            for g in range(2):
                mm(bank(4 + g), ident[:, 64 + 32 * g:65 + 32 * g].broadcast_to([P, P]), ada_rows[:, 2, :],
                   ready=sig("grow_ps") if g == 1 else None)

            turns1 = (FIRST_SLOTS + NE * EXPERT_SLOTS) // RING
            with pe.Fori(0, LAYERS) as l:
                turns = l * (LAYER_SLOTS // RING) + turns1

                def norm(n):
                    pe.wait_ge(sig("norm2_ready"), l * 3 + n + 1)
                    for k in range(KD):
                        for t in range(TT):
                            turn(bank(k // 2)[:, (k % 2) * T + t * P:(k % 2) * T + (t + 1) * P],
                                 xn[:, t, k * P:(k + 1) * P], ready=sig("uT_ps") if k % 2 == 1 and t == 1 else None)
                    pe.wait_ge(sig("uT_ready"), l * 6 + (n + 1) * 2)
                    pe.wait_ge(sig("uT_ready_a"), l * 6 + (n + 1) * 2)

                def pair(at, w, b, ready):
                    for g in range(2):
                        for k in range(KD):
                            a = g * 1024 + k * P
                            last = g == 1 and k == KD - 1
                            mm(b[:, g * T:(g + 1) * T], w[:, a:a + P], uT[:, k, :], start=k == 0, stop=k == KD - 1,
                               free=int(last), ready=ready if last else None)

                def product3(out, lhs, rhs, start, stop, **more):
                    mm(out, lhs[0], rhs[0], start=start, stop=False)
                    mm(out, lhs[0], rhs[1], start=False, stop=False)
                    mm(out, lhs[1], rhs[0], start=False, stop=stop, **more)

                def ffn(f, at):
                    norm(2 * f)
                    for n, (kind, i) in enumerate(FFN_SLOTS):
                        pe.wait_ge(sig("w_ready"), l * 2 * len(FFN_SLOTS) + f * len(FFN_SLOTS) + n + 1)
                        w = (w_hi[:, n % SPLITS, :], w_lo[:, n % SPLITS, :])
                        if kind == "up":
                            if i >= 4:
                                pe.wait_ge(sig("hid_done"), l * 2 * FT + f * FT + i - 3)
                            b = bank(4 + i % 4)
                            for g in range(2):
                                for k in range(KD):
                                    if n == g == 0 and k % 2 == 0:
                                        pe.wait_ge(sig("u_ready"), l * 8 + f * 4 + k // 2 + 1)
                                    a = g * 1024 + k * P
                                    last = g == 1 and k == KD - 1
                                    product3(b[:, g * T:(g + 1) * T], [v[:, a:a + P] for v in w],
                                             (u_hi[:, k, :], u_lo[:, k, :]), k == 0, k == KD - 1,
                                             free=int(last), ready=sig("ffn_ps") if last else None)
                        else:
                            for j in range(2):
                                k = 2 * i + j
                                pe.wait_ge(sig("hid_done"), l * 2 * FT + f * FT + k + 1)
                                for t in range(TT):
                                    for c in range(2):
                                        a = j * 1024 + c * 512
                                        last = j == t == c == 1
                                        h = [v[:, k % 4, t * P:(t + 1) * P] for v in (hid_hi, hid_lo)]
                                        product3(bank(2 * t + c), h, [v[:, a:a + 512] for v in w], k == 0,
                                                 k == FT - 1, free=int(last),
                                                 ready=sig("down_step") if last else None)

                ffn(0, 0)
                at = 33
                norm(1)
                for t in range(TT):
                    for k in range(KD):
                        w = slot(at + k // 4, turns)
                        a = (k % 4) * 512
                        mm(bank(t), uT[:, k, t * P:(t + 1) * P], w[:, a:a + 512], start=k == 0, stop=k == KD - 1,
                           free=int(t == 1 and k % 4 == 3))
                w = slot(at + 2, turns)
                for t in range(TT):
                    for k in range(KD):
                        mm(bank(2)[:, t * T:(t + 1) * T], uT[:, k, t * P:(t + 1) * P], w[:, k * T:(k + 1) * T],
                           start=k == 0, stop=k == KD - 1, free=int(t == 1 and k == KD - 1))
                for t in range(TT):
                    for k in range(KD):
                        w = slot(at + 3 + k // 4, turns)
                        a = (k % 4) * 512
                        mm(bank(3 + t), uT[:, k, t * P:(t + 1) * P], w[:, a:a + 512], start=k == 0, stop=k == KD - 1,
                           free=int(t == 1 and k % 4 == 3), ready=sig("qkvp_ps") if t == 1 and k == KD - 1 else None)

                def gate(k):
                    if k >= 2:
                        pe.wait_ge(sig("gate_kept"), l * KD + k - 1)
                    pair(at + 5 + k, slot(at + 5 + k, turns), bank(6 + k % 2), sig("gate_ps"))

                for k in range(4):
                    gate(k)
                pe.wait_ge(sig("rope_ready"), l + 1)
                pe.wait_ge(sig("vp_kept"), l + 1)
                for j in range(5):
                    for t in range(TT):
                        turn(bank(j // 2)[:, (j % 2) * T + t * P:(j % 2) * T + (t + 1) * P],
                             qk[:, t, 2 * j:2 * j + 2, :].rearrange("p h c -> p (h c)"),
                             ready=sig("qkT_ps") if j == 4 and t == 1 else None)
                for k in range(4, 6):
                    gate(k)
                pe.wait_ge(sig("qkT_kept"), l + 1)

                def scores(t):
                    for j in range(4):
                        for f in range(2):
                            mm(bank(2 * f + j // 2)[:, (j % 2) * T:(j % 2 + 1) * T], q2T[64 * f:64 * f + 64, j, t * P:(t + 1) * P],
                               k2T[64 * f:64 * f + 64, :], ready=sig("scores_ps") if j == 3 and f == 1 else None)

                scores(0)
                gate(6)
                pe.wait_ge(sig("scores_kept"), l * TT + 1)
                scores(1)
                gate(7)
                for c in range(8):
                    t, k, half = c // 4, (c // 2) % 2, c % 2
                    pe.wait_ge(sig("att_ready"), l * TT + t + 1)
                    if c >= 2:
                        pe.wait_ge(sig("attT_kept") if c % 2 == 0 else sig("attT_kept_a"), l * 4 + c // 2)
                    for i in range(4):
                        turn(bank(4 + c % 2)[:, i * P:(i + 1) * P], att[:, t, half * 4 + i, k * P:(k + 1) * P],
                             ready=sig("attT_ps") if i == 3 else None)
                pe.wait_ge(sig("scores_kept"), l * TT + 2)
                for g in range(4):
                    for t in range(TT):
                        mm(bank(2 + g // 2)[:, (g % 2) * T:(g % 2 + 1) * T], p_tok[:, t, g * P:(g + 1) * P],
                           poolm[:, g, t, :], start=t == 0, stop=t == 1,
                           ready=sig("pooled_ps") if g == 3 and t == 1 else None)
                pe.wait_ge(sig("attT_kept"), l * 4 + 4)
                pe.wait_ge(sig("attT_kept_a"), l * 4 + 4)
                for j in range(4):
                    for f in range(2):
                        for k in range(TT):
                            mm(bank(j // 2)[64 * f:64 * f + 64, (j % 2) * T:(j % 2 + 1) * T],
                               v2[:, k, 64 * f:64 * f + 64], attT[:, k, 4 * f + j, :], start=k == 0, stop=k == 1,
                               ready=sig("a2T_ps") if j == 3 and f == k == 1 else None)
                pe.wait_ge(sig("pooled_kept"), l + 1)
                for g in range(4):
                    mm(bank(4 + g // 2)[:, (g % 2) * T:(g % 2 + 1) * T], pool_w[:, g, :], pooledT[:, g, :],
                       ready=sig("mixed_ps") if g == 3 else None)
                pe.wait_ge(sig("mixT_ready"), l + 1)
                pe.wait_ge(sig("gate_kept"), l * KD + KD)

                def kept2(k):
                    if k >= 2:
                        pe.wait_ge(sig("mT_ready"), l * KD + k - 1)

                branches(at + 13, turns, lambda k: bank(6 + k % 2), kept2, lambda i: a2T[:, i, :],
                         lambda i: mixT[:, i, :], sig("branch2_ps"))
                pe.wait_ge(sig("mT_ready"), l * KD + KD)
                token_out(at + 17, turns, 0, lambda k: mT[:, k, :], KD, sig("mixer_ps"))
                ffn(1, 54)
                slot(LAYER_SLOTS - 1, turns)
                pe.wait_ge(sig("down_step"), l * FT + FT)
                pe.sem_inc(sig("slot_used"), pending[0] + 1)
                pending[0] = 0

def shape_tables():
    f = np.float32
    t = np.arange(T)
    w = np.pi * (2 * np.arange(T) + 1) / (2 * T)
    ang = np.outer(t, w)
    dft = np.stack([np.cos(ang), np.sin(ang)])
    dft_t = dft.reshape(2, TT, P, T).transpose(2, 0, 1, 3).reshape(P, -1)
    idft_t = (dft.transpose(0, 2, 1) / T).reshape(2, TT, P, T).transpose(2, 0, 1, 3).reshape(P, -1)
    s, q = np.arange(P)[:, None], np.arange(P)[None, :]
    big, zero = np.full((P, P), BIG), np.zeros((P, P))
    fwd, bwd = np.where(s <= q, 0, BIG), np.where(s >= q, 0, BIG)
    causal = np.concatenate([big, fwd, zero, zero, bwd, big], axis=1)
    tabs = np.concatenate([dft_t, idft_t, causal], axis=1).astype(f)
    const = np.concatenate([np.eye(P), np.ones((P, P)), np.tile(t, (P, 1))], axis=1).astype(f)
    tl = np.linspace(0.0, 1.0, T, dtype=f)[:, None]
    bands = np.linspace(1e-4, 15, 16, dtype=f)[None, :]
    za = (f(2.0 * np.pi / T) * np.arange(T, dtype=f)[:, None] * bands).astype(f)
    z = np.concatenate([tl, np.cos(za), np.sin(za)], axis=1).astype(f)
    lo, hi = np.log(1e-2) / 1.5, np.log(1e-2) / 0.3
    deltas = np.abs(np.linspace(lo, hi, HYC, dtype=f))
    decay = np.exp(-tl * deltas).astype(f).reshape(TT, P, HYC).transpose(1, 0, 2).reshape(P, -1)
    half = 8
    inv = (1.0 / (f(500000.0) ** (np.arange(0, 16, 2, dtype=f) / f(16)))).astype(f)
    ra = (np.arange(T, dtype=f)[:, None] * inv[None, :]).astype(f)
    rope = np.stack([np.cos(ra), np.sin(ra)]).astype(f).reshape(2, TT, P, half).transpose(2, 0, 1, 3).reshape(P, -1)
    amask = np.where(np.abs(t[:, None] - t[None, :]) <= 128, 0.0, -1e30)
    amask = amask.reshape(TT, P, T).transpose(1, 0, 2).reshape(P, -1)
    pool = np.zeros((4, T, T))
    for g, n in enumerate(POOLS):
        for q_ in range(T):
            a, b = max(q_ - n // 2, 0), min(q_ + n // 2, T)
            pool[g, a:b, q_] = 1.0 / (b - a)
            pool[g, q_, q_] -= 1.0
    pool = pool.reshape(4, TT, P, T).transpose(2, 0, 1, 3).reshape(P, -1)
    tabs2 = np.concatenate([rope, amask, pool], axis=1).astype(f)
    bmask = np.zeros((P, NE, CAP), f)
    bmask[np.arange(NE), np.arange(NE)] = 1.0
    not_first = np.ones((P, 2), f)
    not_first[0, 0] = 0.0
    tokens = t.reshape(TT, P).T.astype(f)
    return tabs, const, z, decay, tabs2, bmask, not_first, tokens


def lay_out(a):
    f = np.float32

    def cols_of(v):
        return v.reshape(-1, P).T

    def on_rows(v, rows=P):
        out = np.zeros((rows,) + v.shape[1:], v.dtype)
        out[0:v.shape[0]] = v
        return out

    def tiles(w):
        k, n = w.shape[0] // P, w.shape[1] // P
        return w.reshape(k, P, n, P).transpose(2, 1, 0, 3).reshape(n, P, k * P)

    def paired(v):
        return v.reshape(-1, 2, P, v.shape[2]).transpose(0, 2, 1, 3).reshape(-1, P, 2 * v.shape[2])

    def rows_in(w, per):
        return w.reshape(-1, per, P, w.shape[1]).transpose(0, 2, 1, 3).reshape(-1, P, per * w.shape[1])

    tabs, const, z, decay, tabs2, bmask, not_first, tokens = shape_tables()
    b_in, w_in = a["b_in"][0], a["w_in"][0]
    ML = 3 * HYC
    GATE = ML + 4 * H * P
    MERGE = GATE + 4 * H
    merge_tiles = tiles(w_in[:, MERGE:])
    merge_pairs = np.stack([merge_tiles[0:KD], merge_tiles[KD:]], axis=1).reshape(2 * KD, P, 1024)
    b_merge = cols_of(b_in[MERGE:]).reshape(P, 2, KD).transpose(0, 2, 1).reshape(P, 16)

    def branch(wa, wb):
        return paired(np.concatenate([tiles(wa), tiles(wb)], axis=2))

    stream = [
        a["w_ada"][0].reshape(KD, P, 3, SLOT).transpose(2, 0, 1, 3)[0],
        paired(tiles(w_in[:, ML + 512:ML + 1024])), paired(tiles(w_in[:, ML:ML + 512])),
        rows_in(w_in[:, ML + 1024:ML + 1536], 4), paired(tiles(w_in[:, ML + 1536:ML + 2048])),
        paired(tiles(w_in[:, 0:ML])), paired(merge_pairs)[0:4],
        a["w_ada"][0].reshape(KD, P, 3, SLOT).transpose(2, 0, 1, 3)[1],
        a["w_ada"][0].reshape(KD, P, 3, SLOT).transpose(2, 0, 1, 3)[2], paired(merge_pairs)[4:],
        branch(a["w_branch_hy"][0], a["w_branch_ml"][0]), rows_in(a["w_out"][0], 2), np.zeros((2, P, SLOT), f)]
    assert sum(len(s) for s in stream) == FIRST_SLOTS
    for e in range(NE):
        stream += [a["w_exp1"][0, e].reshape(KD, P, SLOT), a["w_exp3"][0, e].reshape(KD, P, SLOT),
                   rows_in(a["w_exp2"][0, e], 2)]
    for l in range(LAYERS):
        w = a["w_in_2"][l]

        def ffn(n):
            up = np.concatenate([tiles(a[f"{n}_w1_2"][l]), tiles(a[f"{n}_w3_2"][l])], axis=2)
            down = rows_in(a[f"{n}_w2_2"][l], 2)
            return [np.stack([(up if kind == "up" else down)[i] for kind, i in FFN_SLOTS])]

        gt = tiles(w[:, 1280:])
        wba = a["w_branch_attn_2"][l].reshape(2, 4, 64, D).transpose(1, 0, 2, 3).reshape(512, D)
        stream += ffn("ffn1")
        stream += [rows_in(w[:, 0:512], 4), rows_in(w[:, 512:768], 8), rows_in(w[:, 768:1280], 4),
                   np.concatenate([gt[0:KD], gt[KD:]], axis=2), branch(wba, a["w_branch_pool_2"][l]),
                   rows_in(a["w_out_2"][l], 2)]
        stream += ffn("ffn2")
        stream += [np.zeros((1, P, SLOT), f)]
    out = {"stream": np.concatenate(stream)}
    assert out["stream"].shape == (N_SLOTS, P, SLOT), out["stream"].shape

    c = np.stack([cols_of(a["c"][0]), cols_of(a["c_ctx"])], axis=2).reshape(P, 16)

    def taps(w, n):
        return w.reshape(3, n, P).transpose(2, 1, 0).reshape(P, 3 * n)

    out["cols"] = np.concatenate([
        c, cols_of(a["norm_mix_g"][0]), cols_of(a["norm_ffn_g"][0]), cols_of(b_in[0:ML]),
        cols_of(b_in[ML:ML + 512]), cols_of(b_in[ML + 512:ML + 1024]), cols_of(b_in[ML + 1536:ML + 2048]), b_merge,
        taps(a["hy_conv"][0], 12), taps(a["ml_conv"][0], 8),
        a["hy_skip"][0].reshape(ORDERS, 4, P).transpose(2, 0, 1).reshape(P, 8), cols_of(a["ml_norm_g"][0]),
        on_rows(a["hy_f_b1"][0][:, None]), on_rows(a["hy_f_b2"][0][:, None]),
        on_rows(b_in[GATE:MERGE].reshape(4, H).T), not_first, np.full((P, 1), EPS, f), np.ones((P, 1), f), tokens],
        axis=1)
    assert out["cols"].shape == (P, N_COLS)
    out["lcols"] = np.stack([np.concatenate([
        cols_of(a["ffn1_norm_2"][l]), cols_of(a["mix_norm_2"][l]), cols_of(a["ffn2_norm_2"][l]),
        cols_of(a["b_gate_2"][l]), cols_of(a["pool_scale_2"][l]),
        np.tile(a["attn_sink_2"][l][None, :], (P, 1)),
        a["pool_w_2"][l].transpose(1, 0, 2).reshape(P, 512)], axis=1) for l in range(LAYERS)])
    out["filt"] = np.concatenate([on_rows(z.T), on_rows(a["hy_f_w1"][0]), on_rows(a["hy_f_w2"][0]),
                                  on_rows(a["hy_f_w3"][0]), decay], axis=1)
    out["const"], out["tabs"], out["tabs2"], out["bmask"] = const, tabs, tabs2, bmask
    rows = np.zeros((P, 3, 512), f)
    for g in range(4):
        rows[32 * g] = rows[32 * g + 1] = a["b_ada"][0].reshape(3, 4, 512)[:, g]
    out["ada_rows"] = rows
    out["wgate"] = w_in[:, GATE:MERGE].reshape(KD, P, 16).transpose(1, 0, 2)
    out["vbias"] = np.tile(b_in[ML + 1024:ML + 1536][None, :], (P, 1))
    out["wrouter"] = a["w_router"][0].reshape(KD, P, NE).transpose(1, 0, 2)
    out["fin_rows"] = np.stack([np.tile(a["final_norm_g"][None, :], (P, 1)), np.tile(a["final_norm_2"][None, :], (P, 1))])
    out["x"] = a["x"][0].reshape(TT, P, D).transpose(1, 0, 2)
    out["ctx"] = a["ctx"][0].reshape(TT, P, D).transpose(1, 0, 2)
    return {k: np.ascontiguousarray(v) for k, v in out.items()}


def kernel(**inputs):
    import concourse.bacc as bacc
    from concourse.bass_utils import run_bass_kernel_spmd

    nc = bacc.Bacc("TRN2", target_bir_lowering=False, num_devices=1)
    arrays = lay_out({k: np.asarray(v) for k, v in inputs.items()})
    d = {k: nc.dram_tensor(f"{k}_dram", v.shape, F32, kind="ExternalInput").ap() for k, v in arrays.items()}
    d["out"] = nc.dram_tensor("out_dram", (P, TT, D), F32, kind="ExternalOutput").ap()
    build(nc, d)
    r = run_bass_kernel_spmd(nc, [{f"{k}_dram": v for k, v in arrays.items()}], core_ids=[0])
    return r.results[0]["out_dram"].reshape(P, TT, D).transpose(1, 0, 2).reshape(1, T, D)
```

```python
from contextlib import ExitStack

import numpy as np
import concourse.bass as bass
from concourse import mybir
from concourse.alu_op_type import AluOpType as ALU

F32 = mybir.dt.float32
F32R = mybir.dt.float32r
U32 = mybir.dt.uint32
ACT = mybir.ActivationFunctionType
X = mybir.AxisListType.X

P = 128
D = 1024
KD = D // P
T = 256
TT = T // P
ROW = 64
HYC = 512
ORDERS = 2
HID = 64
EMB = 33
H = 4
VW = P + 2
NE = 16
CAP = 2 * T // NE
DFE = 2 * D
FT = 22
LAYERS = 2
POOLS = (2, 4, 8, 16)
EPS = 1e-6
QSCALE = P ** -0.5
BIG = 30000.0

RING = 8
SLOT = 2048
FIRST_SLOTS = 56
EXPERT_SLOTS = 24
LAYER_SLOTS = 88
N_SLOTS = FIRST_SLOTS + NE * EXPERT_SLOTS + LAYERS * LAYER_SLOTS


def offsets(*widths):
    at, out = 0, {}
    for name, n in widths:
        out[name] = at
        at += n
    return out, at


SPLITS = 3
FFN_SLOTS = [("up", 0), ("up", 1)]
for _i in range(1, FT // 2):
    FFN_SLOTS += [("up", 2 * _i), ("up", 2 * _i + 1), ("down", _i - 1)]
FFN_SLOTS.append(("down", FT // 2 - 1))
FFN_AT = (0, 54)
DOWN_STEPS = FT // 2 + 1

COLS, N_COLS = offsets(("c", 16), ("g_mix", 8), ("g_ffn", 8), ("b_hy", 12), ("b_q", 4), ("b_k", 4), ("b_o", 4),
                       ("b_merge", 16), ("hy_conv", 36), ("ml_conv", 24), ("skip", 8), ("ml_g", 4),
                       ("f_b1", 1), ("f_b2", 1), ("b_gate", 4), ("not_first", 2), ("eps", 1), ("one", 1),
                       ("token", 2))
LCOLS, N_LCOLS = offsets(("norm", 24), ("b_gates", 16), ("pool_scale", 4), ("sink", 8), ("pool_w", 512))
FILT, N_FILT = offsets(("z", T), ("w1", HID), ("w2", HID), ("w3", 4 * HYC), ("decay", TT * HYC))
TABS, N_TABS = offsets(("dft", 2 * TT * T), ("idft", 2 * TT * T), ("causal", 2 * 384))
TABS2, N_TABS2 = offsets(("rope", 2 * TT * 8), ("amask", TT * T), ("pool", 4 * TT * T))


class Link:

    def __init__(self, eng, sem, trip=None, per_trip=0):
        self.eng, self.sem, self.trip, self.per_trip, self.n = eng, sem, trip, per_trip, 0

    def __call__(self, ins):
        self.n += 1
        ins.then_inc(self.sem, 1)
        self.eng.wait_ge(self.sem, self.n if self.trip is None else self.trip * self.per_trip + self.n)

    def close(self):
        assert self.trip is None or self.n == self.per_trip, self.n


class Region:

    def __init__(self, tensor, at, end):
        self.tensor, self.at, self.end = tensor, at, end

    def take(self, *dims):
        n = int(np.prod(dims))
        v = self.tensor[:, self.at:self.at + n]
        self.at += n
        assert self.at <= self.end, (self.at, self.end)
        if len(dims) == 2:
            return v.rearrange("p (a b) -> p a b", a=dims[0])
        if len(dims) == 3:
            return v.rearrange("p (a b c) -> p a b c", a=dims[0], b=dims[1])
        if len(dims) == 4:
            return v.rearrange("p (a b c d) -> p a b c d", a=dims[0], b=dims[1], c=dims[2])
        return v


def build(nc, d):
    with ExitStack() as ctx:
        def sb(name, shape, dt=F32):
            return ctx.enter_context(nc.sbuf_tensor(name, shape, dt))

        signals = {}

        def sig(name):
            if name not in signals:
                signals[name] = ctx.enter_context(nc.semaphore(name))
            return signals[name]

        ring = sb("ring", [P, RING, SLOT])
        cols = sb("cols", [P, N_COLS])
        lcols = sb("lcols", [P, N_LCOLS])
        const = sb("const", [P, 2 * P + T])
        ident, ones, iota = const[:, 0:P], const[:, P:2 * P], const[:, 2 * P:]
        x_tok = sb("x_tok", [P, TT, D])
        area_n = sb("area_n", [P, 4096])
        area_h = sb("area_h", [P, 4096])
        ada_rows = sb("ada_rows", [P, 3, 512])
        ada_cols = sb("ada_cols", [P, 2, 48])
        mod1 = sb("mod1", [P, 2, KD])
        mod2 = sb("mod2", [P, KD])
        stat = sb("stat", [P, 3, 4])
        silu_c = sb("silu_c", [P, KD, 32])
        wgate = sb("wgate", [P, KD, 16])
        vbias = sb("vbias", [P, HYC])
        wrouter = sb("wrouter", [P, KD, NE])
        topi = sb("topi", [P, NE * 2], U32)
        fin_rows = sb("fin_rows", [P, D])
        WIDE = 21590
        with nc.sbuf_tensor("wide", [P, WIDE], F32) as wide:
            pass
        tabs2 = sb("tabs2", [P, N_TABS2])
        LATER = WIDE - N_TABS2
        with nc.sbuf_tensor("later", [P, LATER], F32) as later:
            pass
        w_hi = sb("w_hi", [P, SPLITS, SLOT], F32R)
        w_lo = sb("w_lo", [P, SPLITS, SLOT], F32R)
        u_hi = sb("u_hi", [P, KD, T], F32R)
        u_lo = sb("u_lo", [P, KD, T], F32R)
        hid_hi = sb("hid_hi", [P, 4, T], F32R)
        hid_lo = sb("hid_lo", [P, 4, T], F32R)
        ps = ctx.enter_context(nc.psum_tensor("ps", [P, 8, 512], F32))

        def bank(i):
            return ps[:, i, :]

        def col(name, i=0, n=1, rows=P):
            return cols[0:rows, COLS[name] + i:COLS[name] + i + n]

        def lcol(name, i=0, n=1):
            return lcols[:, LCOLS[name] + i:LCOLS[name] + i + n]

        xn = area_n[:, 0:2048].rearrange("p (t d) -> p t d", t=TT)
        cn = area_n[:, 2048:].rearrange("p (t d) -> p t d", t=TT)
        merge = area_n[:, :].rearrange("p (d g t) -> p d g t", d=KD, g=2)
        hT = area_h[:, :].rearrange("p (k t) -> p k t", k=KD)
        r = Region(area_h, 0, 4096)
        pm0 = r.take(2, TT, HYC)
        pm_tmp = r.take(2, HYC)
        r = Region(area_n, 0, 4096)
        gates = r.take(4, 2 * T)
        lnb = r.take(2, 2 * T)
        bcum = r.take(2, 2 * T)
        g_in, g_forget = gates[:, 0::2, :], gates[:, 1::2, :]
        r = Region(wide, 0, WIDE)
        dft = r.take(2, TT, T)
        idft = r.take(2, TT, T)
        causal = r.take(2, 384)
        spec = r.take(ORDERS, 2, TT, HYC)
        hy = r.take(12, T)
        pm = (pm0, hy[:, 4:, :].rearrange("p (j t h) c -> p j t (h c)", j=2, t=TT))
        kT = r.take(H, 2 * T)
        qT = r.take(H, T)
        oT = r.take(H, T)
        z_tok = wide[:, r.at:r.at + TT * HYC].rearrange("p (t c) -> p t c", t=TT)
        v_tok = r.take(2 * TT, H, VW)
        base = r.at
        filt = r.take(N_FILT)
        hid1 = r.take(T)
        hid2 = r.take(T)
        arg = r.take(T)
        turns = r.take(T)
        r = Region(wide, base, WIDE)
        raw = r.take(4, 2 * T)
        mrow = r.take(2, T)
        zrow = r.take(T)
        kw = r.take(TT, 2, P)
        states = r.take(2 * H, VW)
        hm = r.take(TT, H, P)
        r = Region(lcols, 0, N_LCOLS)
        gcols = r.take(4, 2, TT, H)
        mcols = r.take(8)
        r = Region(wide, base, base + 2048)
        ee = r.take(2, TT, T)
        inter = r.take(TT, 2 * VW)
        den = r.take(TT, 2)
        hsq = wide[:, base:base + 1024].rearrange("p (h e) -> p h e", h=TT * H)
        hstat = stat[:, 0:2, :].rearrange("p a b -> p (a b)")
        r = Region(wide, base, WIDE)
        yspec = r.take(2, TT, HYC)
        yt = r.take(4, HYC)
        r = Region(wide, base, WIDE)
        grow = r.take(D)
        gtmp = r.take(TT, D)
        sq1 = hy[:, 0:4, :].rearrange("p a b -> p (a b)")

        r = Region(later, 0, LATER)
        sel = r.take(TT, NE * CAP)
        h2T = r.take(KD, T)
        aff = r.take(TT, NE)
        esum = r.take(TT)
        affT = r.take(T)
        topv = r.take(NE * 2)
        topf = r.take(NE * 2)
        rep = r.take(2, 4, CAP)
        bdiag = r.take(NE, CAP)
        bmask = r.take(NE, CAP)
        igcols = r.take(2, NE)
        zeros = r.take(512)
        xe = r.take(KD, CAP)
        sa = r.take(512)
        hid_e = r.take(512)
        hTe = r.take(4, P)
        ye = r.take(D)
        scat = r.take(T)
        grow2 = r.take(D)
        gtmp2 = r.take(TT, D)

        sq = area_n[:, 2048:3072]
        uT = area_h[:, 0:2048].rearrange("p (k t) -> p k t", k=KD)
        mT = area_h[:, 2048:].rearrange("p (k t) -> p k t", k=KD)
        r = Region(area_n, 3072, 4096)
        sa2 = r.take(2, T)
        hid = r.take(2, T)
        r = Region(later, 0, LATER)
        qk = r.take(TT, 10, 64)
        p_tok = r.take(TT, 512)
        v2 = r.take(TT, P)
        q2T = r.take(4, T)
        k2T = r.take(T)
        r.at = 2 * SLOT
        a2T = r.take(4, T)
        mixT = r.take(4, T)
        att = r.take(TT, 8, T)
        sgate = r.take(KD, 2, T)
        rtmp = r.take(4, TT, 80)
        pooledT = r.take(4, T)
        mst = r.take(TT, 4, 8)
        attT = area_n[:, :].rearrange("p (k h q) -> p k h q", k=TT, h=8)
        rope = tabs2[:, 0:32].rearrange("p (f t c) -> p f t c", f=2, t=TT)
        amask = tabs2[:, TABS2["amask"]:TABS2["pool"]].rearrange("p (t k) -> p t k", t=TT)
        poolm = tabs2[:, TABS2["pool"]:].rearrange("p (g s t) -> p g s t", g=4, s=TT)
        pool_w = lcols[:, LCOLS["pool_w"]:].rearrange("p (g e) -> p g e", g=4)

        block = ctx.enter_context(nc.Block())

        @block.sync
        def _(sp):
            sp.wait_ge(sig("filt_loaded"), 16)
            for s in range(RING):
                sp.dma_start(ring[:, s, :], d["stream"][s]).then_inc(sig(f"slot_loaded{s}"), 16)
            with sp.Fori(1, N_SLOTS // RING) as rev:
                for s in range(RING):
                    sp.wait_ge(sig("slot_used"), rev * RING + (s + 1 - RING))
                    sp.dma_start(ring[:, s, :], d["stream"][rev * RING + s]).then_inc(sig(f"slot_loaded{s}"), 16)
            for t in range(TT):
                sp.wait_ge(sig("out_ready"), t + 1)
                sp.dma_start(d["out"][:, t, :], x_tok[:, t, :]).then_inc(sig("stored"), 16)
            sp.wait_ge(sig("stored"), TT * 16)

        @block.scalar
        def _(act):
            A = nc.scalar
            act.dma_start(cols[:, :], d["cols"]).then_inc(sig("cols_loaded"), 16)
            act.dma_start(filt, d["filt"]).then_inc(sig("filt_loaded"), 16)
            act.dma_start(wide[:, 0:N_TABS], d["tabs"]).then_inc(sig("tabs_loaded"), 16)
            act.dma_start(x_tok[:, :, :], d["x"]).then_inc(sig("x_loaded"), 16)
            act.dma_start(cn, d["ctx"]).then_inc(sig("ctx_loaded"), 16)
            act.dma_start(const[:, :], d["const"]).then_inc(sig("const_loaded"), 16)
            act.dma_start(ada_rows[:, :, :], d["ada_rows"]).then_inc(sig("ada_bias_loaded"), 16)
            act.dma_start(wgate[:, :, :], d["wgate"]).then_inc(sig("wgate_loaded"), 16)
            step = Link(act, sig("act_step"))

            def root_mean_square(step, src, scratch, at, ready, source=None, before=0):
                if source is not None:
                    A.activation(stat[:, 2, 0:1], col("eps"), ACT.Sqrt)
                for t in range(TT):
                    if source is not None:
                        act.wait_ge(source, before + t + 1)
                    step(A.activation(scratch, src[:, t, :], ACT.Square, accum_out=stat[:, at, t:t + 1]))
                    A.activation(stat[:, at, 2 + t:3 + t], stat[:, at, t:t + 1], ACT.Sqrt, scale=1.0 / D,
                                 bias=col("eps")).then_inc(ready, 1)

            act.wait_ge(sig("cols_loaded"), 16)
            act.wait_ge(sig("cleared"), 1)
            A.activation(silu_c[:, :, 0:2], cols[:, 0:16].rearrange("p (k s) -> p k s", s=2),
                         ACT.Silu).then_inc(sig("silu_ready"), 1)
            for n, h in enumerate((hid1, hid2)):
                act.wait_ge(sig("arg_ready"), n + 1)
                A.activation(h[0:HID, :], arg[0:HID, :], ACT.Sin).then_inc(sig("hid_ready"), 1)
            act.wait_ge(sig("x_loaded"), 16)
            root_mean_square(step, x_tok, sq1, 0, sig("rms_ready"))
            act.wait_ge(sig("ctx_loaded"), 16)
            act.wait_ge(sig("rms_ready"), TT)
            root_mean_square(step, cn, sq1, 1, sig("rms_ready"))
            for o in range(ORDERS):
                act.wait_ge(sig("spec_ready"), o + 1)
                for j in range(2):
                    last = A.copy(spec[:, o, j, :, :], ps[:, 2 + 2 * j:4 + 2 * j, :])
                last.then_inc(sig("spec_kept"), 1)
            act.dma_start(vbias[:, :], d["vbias"]).then_inc(sig("vbias_loaded"), 16)
            act.dma_start(wrouter[:, :, :], d["wrouter"]).then_inc(sig("wrouter_loaded"), 16)
            act.dma_start(fin_rows[:, :], d["fin_rows"][0]).then_inc(sig("fin_loaded"), 16)
            act.wait_ge(sig("mod1_ready"), 1)
            for k in range(0, KD, 2):
                act.wait_ge(sig("hT_ps"), k + 1)
                for s in range(2):
                    last = A.activation(hT[:, k, s * T:(s + 1) * T], ps[:, k, s * T:(s + 1) * T], ACT.Identity,
                                        scale=mod1[:, s, k:k + 1], bias=ada_cols[:, s, k:k + 1])
                last.then_inc(sig("hT_ready_a"), 1)

            def unit_ready(n):
                act.wait_ge(sig("unit_ready"), n + 1)
                return bank(n % 4 if n < 33 else 6 + n % 2)

            def to_conv(n, c, bias, width):
                b = unit_ready(n)
                if c >= 4:
                    act.wait_ge(sig("conv_done"), c - 3)
                A.activation(raw[:, c % 4, 0:width], b[:, 0:width], ACT.Identity,
                             bias=bias).then_inc(sig("unit_kept"), 1)

            b = unit_ready(0)
            for g in range(4):
                last = A.copy(gates[0:H, g, :], b[32 * g:32 * g + H, :])
            last.then_inc(sig("unit_kept"), 1)
            for h in range(H):
                to_conv(1 + h, h, col("b_k", h), 2 * T)
            act.wait_ge(sig("gates_biased"), 1)
            step(A.activation(lnb[0:H, :, :], g_forget[0:H], ACT.Abs))
            step(A.activation(lnb[0:H, :, :], lnb[0:H, :, :], ACT.Exp, scale=-1.0))
            A.activation(lnb[0:H, :, :], lnb[0:H, :, :], ACT.Ln,
                         bias=col("one", rows=H)).then_inc(sig("softplus_ready"), 1)
            for h in range(H):
                to_conv(5 + h, 4 + h, col("b_q", h), T)
            act.wait_ge(sig("gate_rows"), 1)
            act.wait_ge(sig("softplus_ready"), 1)
            A.activation(g_in[0:H, :, T:], g_in[0:H, :, T:], ACT.Exp)
            A.activation(lnb[0:H, :, :], lnb[0:H, :, :], ACT.Exp, scale=-1.0).then_inc(sig("gate_exps"), 1)
            for h in range(H):
                act.wait_ge(sig("conv_done"), h + 1)
                A.activation(kT[:, h, :], kT[:, h, :], ACT.Silu).then_inc(sig("k_ready"), 1)
            for h in range(H):
                act.wait_ge(sig("conv_done"), 4 + h + 1)
                A.activation(qT[:, h, :], qT[:, h, :], ACT.Silu).then_inc(sig("q_ready"), 1)
            for h in range(H):
                b = unit_ready(9 + h)
                A.activation(oT[:, h, :], b[:, 0:T], ACT.Sigmoid, bias=col("b_o", h)).then_inc(sig("unit_kept"), 1)
            for c in range(12):
                to_conv(13 + c, 8 + c, col("b_hy", c), T)
            act.wait_ge(sig("gcols_ps"), 1)

            def merge_gates(*units):
                for n in units:
                    b, m = unit_ready(n), n - 25
                    A.activation(merge[:, m // 2, m % 2, :], b[:, 0:T], ACT.Sigmoid,
                                 bias=col("b_merge", m)).then_inc(sig("unit_kept"), 1)

            merge_gates(*range(25, 33))

            for h in range(H):
                act.wait_ge(sig("state_ps"), h + 1)
                A.copy(states[:, 2 * h:2 * h + 2, :],
                       bank(6)[:, 0:2 * VW].rearrange("p (s e) -> p s e", s=2)).then_inc(sig("state_kept"), 1)
            for h in range(H):
                act.wait_ge(sig("gaps_ready"), h + 1)
                A.activation(ee, ee, ACT.Exp, scale=-1.0).then_inc(sig("decay_ready"), 1)
                act.wait_ge(sig("inter_ps"), h + 1)
                if h >= 1:
                    act.wait_ge(sig("head_done"), h)
                for t in range(TT):
                    for s in range(2):
                        last = A.activation(inter[:, t, s * VW:(s + 1) * VW], bank(t)[:, s * VW:(s + 1) * VW],
                                            ACT.Copy, scale=gcols[:, 1, s, t, h:h + 1])
                last.then_inc(sig("inter_kept"), 1)
            for o in range(ORDERS):
                act.wait_ge(sig("z_ps"), o + 1)
                if o >= 1:
                    act.wait_ge(sig("signal_ps"), o)
                A.copy(z_tok, ps[:, 4:6, :]).then_inc(sig("z_kept"), 1)
                if o == 0:
                    act.wait_ge(sig("hsum_ready"), 1)
                    A.activation(hstat, hstat, ACT.Sqrt, scale=1.0 / P, bias=col("eps")).then_inc(sig("hrms_ready"), 1)
                    merge_gates(33, 34, 35, 36)
                else:
                    merge_gates(37, 38, 39, 40)
            act.wait_ge(sig("grow_ps"), 1)
            A.copy(grow, ps[:, 4:6, :].rearrange("p b n -> p (b n)")).then_inc(sig("grow_ready"), 1)

            root_mean_square(step, x_tok, sq, 0, sig("rms_ready"), sig("x1_ready"))
            act.dma_start(tabs2[:, :], d["tabs2"]).then_inc(sig("tabs2_loaded"), 16)
            act.dma_start(bmask, d["bmask"]).then_inc(sig("bmask_loaded"), 16)
            for k in (0, 1, 4, 5):
                if k % 2 == 0:
                    act.wait_ge(sig("h2T_ps"), k // 2 + 1)
                A.activation(h2T[:, k, :], bank(k // 2)[:, (k % 2) * T:(k % 2 + 1) * T], ACT.Identity,
                             scale=mod2[:, k:k + 1], bias=ada_cols[:, 0, 24 + k:25 + k]).then_inc(sig("h2T_ready"), 1)
            act.wait_ge(sig("logits_ready"), 1)
            A.activation(aff, aff, ACT.Exp).then_inc(sig("exp_ready"), 1)
            act.wait_ge(sig("grow_ps"), 2)
            A.copy(grow2, ps[:, 0:2, :].rearrange("p b n -> p (b n)")).then_inc(sig("grow_ready"), 1)
            with act.Fori(0, NE) as e:
                act.wait_ge(sig("a_ps"), e + 1)
                A.activation(sa, bank(4), ACT.Silu).then_inc(sig("sa_ready"), 1)
                act.wait_ge(sig("ye_ps"), e + 1)
                A.copy(ye, ps[:, 6:8, :].rearrange("p b n -> p (b n)")).then_inc(sig("ye_ready"), 1)
            root_mean_square(step, x_tok, sq, 0, sig("rms_ready"), sig("x2_ready"))
            before = step.n

            with act.Fori(0, LAYERS) as l:
                step = Link(act, sig("act_layer_step"), l, 6)
                act.wait_ge(sig("h_ready"), l * 3 * TT + 1)
                act.dma_start(lcols[:, :], d["lcols"][l]).then_inc(sig("lcols_loaded"), 16)

                def norm(n):
                    root_mean_square(step, x_tok, sq, 0, sig("rms2_ready"), sig("h_ready"), (l * 3 + n) * TT)

                def norm_turned(n):
                    for b in (1, 3):
                        act.wait_ge(sig("uT_ps"), l * 12 + n * 4 + b + 1)
                        for k in (2 * b, 2 * b + 1):
                            last = A.activation(uT[:, k, :], bank(b)[:, (k % 2) * T:(k % 2 + 1) * T], ACT.Copy,
                                                scale=lcol("norm", 8 * n + k))
                        last.then_inc(sig("uT_ready_a"), 1)

                def ffn(f):
                    first = FIRST_SLOTS + NE * EXPERT_SLOTS + FFN_AT[f]

                    def upper(n):
                        if n >= len(FFN_SLOTS):
                            return
                        turn = l * (LAYER_SLOTS // RING) + (first + n) // RING
                        act.wait_ge(sig(f"slot_loaded{(first + n) % RING}"), turn * 16 + 16)
                        if n >= SPLITS:
                            act.wait_ge(sig("slot_used"), l * LAYER_SLOTS + first + n + 1 - SPLITS)
                        A.copy(w_hi[:, n % SPLITS, :], ring[:, (first + n) % RING, :]).then_inc(sig("w_hi_ready"), 1)

                    if f == 1:
                        for n in range(2):
                            upper(n)
                    norm(2 * f)
                    if f == 0:
                        upper(0)
                        act.wait_ge(sig("lcols_loaded"), l * 16 + 16)
                    for b in range(4):
                        act.wait_ge(sig("uT_ps"), l * 12 + f * 8 + b + 1)
                        for k in (2 * b, 2 * b + 1):
                            last = A.activation(u_hi[:, k, :], bank(b)[:, (k % 2) * T:(k % 2 + 1) * T], ACT.Copy,
                                                scale=lcol("norm", 16 * f + k))
                        last.then_inc(sig("u_hi_ready"), 1)
                    if f == 0:
                        upper(1)
                    upper(2)
                    for n, (kind, i) in enumerate(FFN_SLOTS):
                        if kind == "up":
                            act.wait_ge(sig("ffn_ps"), l * 2 * FT + f * FT + i + 1)
                            if i >= 2:
                                act.wait_ge(sig("hid_done"), l * 2 * FT + f * FT + i - 1)
                            A.activation(sa2[:, i % 2, :], bank(4 + i % 4)[:, 0:T],
                                         ACT.Silu).then_inc(sig("silu2_ready"), 1)
                        upper(n + SPLITS)

                ffn(0)
                norm(1)
                norm_turned(1)
                act.wait_ge(sig("qkvp_ps"), l + 1)
                for t in range(TT):
                    A.copy(qk[:, t, 0:8, :].rearrange("p (j f) c -> p j f c", f=2),
                           bank(t).rearrange("p (f j c) -> p j f c", f=2, j=4))
                    last = A.copy(qk[:, t, 8:10, :],
                                  bank(2)[:, t * T:t * T + P].rearrange("p (f c) -> p f c", f=2))
                last.then_inc(sig("qk_kept"), 1)
                for t in range(TT):
                    A.copy(v2[:, t, :], bank(2)[:, t * T + P:(t + 1) * T])
                    last = A.copy(p_tok[:, t, :], bank(3 + t))
                last.then_inc(sig("vp_kept"), 1)

                def gate(k):
                    act.wait_ge(sig("gate_ps"), l * KD + k + 1)
                    for g in range(2):
                        last = A.activation(sgate[:, k, g, :], bank(6 + k % 2)[:, g * T:(g + 1) * T], ACT.Sigmoid,
                                            bias=lcol("b_gates", 8 * g + k))
                    last.then_inc(sig("gate_kept"), 1)

                for k in range(2):
                    gate(k)
                act.wait_ge(sig("qkT_ps"), l + 1)
                A.copy(q2T[:, 0:2, :], bank(0).rearrange("p (j t) -> p j t", j=2))
                A.copy(q2T[:, 2:4, :], bank(1).rearrange("p (j t) -> p j t", j=2))
                A.copy(k2T, bank(2)[:, 0:T]).then_inc(sig("qkT_kept"), 1)

                def exponentials(t):
                    act.wait_ge(sig("max_ready"), l * TT + t + 1)
                    for h in range(8):
                        A.activation(att[:, t, h, :], att[:, t, h, :], ACT.Exp, bias=mst[:, t, 2, h:h + 1],
                                     accum_out=mst[:, t, 3, h:h + 1])
                    A.activation(mst[:, t, 1, :], mst[:, t, 1, :], ACT.Exp).then_inc(sig("att_exp"), 1)

                def keep_att(c):
                    act.wait_ge(sig("attT_ps"), l * 8 + c + 1)
                    A.copy(attT[:, (c // 2) % 2, (c % 2) * 4:(c % 2) * 4 + 4, (c // 4) * P:(c // 4 + 1) * P],
                           bank(4 + c % 2).rearrange("p (h q) -> p h q", h=4)).then_inc(sig("attT_kept_a"), 1)

                gate(2)
                exponentials(0)
                gate(3)
                gate(4)
                keep_att(1)
                exponentials(1)
                gate(5)
                keep_att(3)
                act.wait_ge(sig("pooled_ps"), l + 1)
                A.copy(pooledT, ps[:, 2:4, :].rearrange("p b (j t) -> p (b j) t", j=2)).then_inc(sig("pooled_kept"), 1)
                gate(6)
                for g in range(4):
                    if g == 0:
                        act.wait_ge(sig("mixed_ps"), l + 1)
                    last = A.activation(mixT[:, g, :], bank(2 + g // 2)[:, (g % 2) * T:(g % 2 + 1) * T], ACT.Copy,
                                        scale=lcol("pool_scale", g))
                last.then_inc(sig("mixT_ready"), 1)
                gate(7)
                keep_att(5)
                keep_att(7)
                act.wait_ge(sig("a2T_ps"), l + 1)
                A.copy(a2T, ps[:, 0:2, :].rearrange("p b (j t) -> p (b j) t", j=2)).then_inc(sig("a2T_kept"), 1)
                ffn(1)
                step.close()

            act.dma_start(fin_rows[:, :], d["fin_rows"][1]).then_inc(sig("fin_loaded"), 16)
            step = Link(act, sig("act_step"))
            step.n = before
            root_mean_square(step, x_tok, sq, 0, sig("rms_ready"), sig("h_ready"), LAYERS * 3 * TT)

        @block.vector
        def _(dve):
            V = nc.vector
            step = Link(dve, sig("dve_step"))
            V.memset(silu_c[:, :, :], 0.0)
            V.memset(v_tok[:, :, :, P:], 1.0).then_inc(sig("cleared"), 1)

            def normalize(step, rms, before, at, src, out, ready):
                for t in range(TT):
                    dve.wait_ge(rms, before + t + 1)
                    step(V.reciprocal(stat[:, at, t:t + 1], stat[:, at, 2 + t:3 + t]))
                    V.tensor_scalar(out[:, t, :], src[:, t, :], stat[:, at, t:t + 1], None,
                                    ALU.mult).then_inc(ready, 1)

            def sine_argument(n, bias):
                dve.wait_ge(sig("filter_ps"), n + 1)
                a, k = arg[0:HID, :], turns[0:HID, :]
                step(V.tensor_scalar(a, bank(n)[0:HID, 0:T], bias, None, ALU.add))
                step(V.tensor_scalar(k, a, 1 / (2 * np.pi), 12582912.0, ALU.mult, ALU.add))
                step(V.tensor_scalar(k, k, 12582912.0, None, ALU.subtract))
                step(V.scalar_tensor_tensor(a, k, -6.28125, a, ALU.mult, ALU.add))
                step(V.scalar_tensor_tensor(a, k, -(2 * np.pi - 6.28125), a, ALU.mult, ALU.add))
                V.tensor_scalar(a, a, 3.14159, -3.14159, ALU.min, ALU.max).then_inc(sig("arg_ready"), 1)

            dve.wait_ge(sig("cols_loaded"), 16)
            sine_argument(0, col("f_b1", rows=HID))
            dve.wait_ge(sig("hid_ready"), 1)
            sine_argument(1, col("f_b2", rows=HID))
            decay = filt[:, FILT["decay"]:].rearrange("p (t c) -> p t c", t=TT)
            for o in range(ORDERS):
                dve.wait_ge(sig("filter_ps"), 3 + o)
                for t in range(TT):
                    b0, b1 = bank((2 + 4 * o + t) % 8), bank((4 + 4 * o + t) % 8)
                    V.tensor_tensor(pm_tmp[:, 0, :], b0, decay[:, t, :], ALU.mult)
                    step(V.scalar_tensor_tensor(pm_tmp[:, 1, :], b1, col("not_first", t), decay[:, t, :],
                                                ALU.mult, ALU.mult))
                    V.tensor_tensor(pm[o][:, 0, t, :], pm_tmp[:, 0, :], pm_tmp[:, 1, :], ALU.add)
                    last = V.tensor_tensor(pm[o][:, 1, t, :], pm_tmp[:, 0, :], pm_tmp[:, 1, :], ALU.subtract)
                    if t == 0:
                        step(last)
                last.then_inc(sig("pm_ready"), 1)
                dve.wait_ge(sig("pm_ready"), o + 1)
            V.memset(mrow, 0.0)
            step(V.memset(zrow, 0.0))
            dve.wait_ge(sig("x_loaded"), 16)
            dve.wait_ge(sig("ctx_loaded"), 16)
            normalize(step, sig("rms_ready"), 0, 0, x_tok, xn, sig("norm_ready"))
            normalize(step, sig("rms_ready"), TT, 1, cn, cn, sig("norm_ready"))

            def ada_row(r, b):
                dve.wait_ge(sig("ada_ps"), r + 1)
                V.tensor_tensor(ada_rows[:, r, :], bank(b), ada_rows[:, r, :], ALU.add).then_inc(sig("ada_row"), 1)

            def ada_col(r, b):
                dve.wait_ge(sig("ada_T_ps"), r + 1)
                v = bank(b).rearrange("p (q g s) -> p q g s", q=4, g=4)
                for s in range(2):
                    out = ada_cols[:, s, 16 * r:16 * r + 16].rearrange("p (g q) -> p q g", q=4)
                    last = V.tensor_copy(out, v[:, :, :, s])
                last.then_inc(sig("ada_cols_ready"), 1)

            dve.wait_ge(sig("ada_bias_loaded"), 16)
            ada_row(0, 7)
            ada_col(0, 7)
            dve.wait_ge(sig("ada_cols_ready"), 1)
            for s in range(2):
                last = V.scalar_tensor_tensor(mod1[:, s, :], ada_cols[:, s, 8:16], 1.0, col("g_mix", 0, 8),
                                              ALU.add, ALU.mult)
            last.then_inc(sig("mod1_ready"), 1)
            dve.wait_ge(sig("mod1_ready"), 1)
            for k in range(1, KD, 2):
                dve.wait_ge(sig("hT_ps"), k + 1)
                for s in range(2):
                    last = V.tensor_scalar(hT[:, k, s * T:(s + 1) * T], ps[:, k, s * T:(s + 1) * T],
                                           mod1[:, s, k:k + 1], ada_cols[:, s, k:k + 1], ALU.mult, ALU.add)
                last.then_inc(sig("hT_ready"), 1)

            dve.wait_ge(sig("unit_kept"), 1)
            V.tensor_tensor(gates[0:H], gates[0:H], cols[0:H, COLS["b_gate"]:COLS["b_gate"] + 4].unsqueeze(2)
                            .broadcast_to([H, 4, 2 * T]), ALU.add).then_inc(sig("gates_biased"), 1)

            def short_conv(c, dst, taps, parts):
                dve.wait_ge(sig("unit_kept"), 1 + c + 1 if c < 8 else 1 + c + 4 + 1)
                width = sum(n * w for _, n, w in parts)
                u = raw[:, c % 4, 0:width]
                step(V.tensor_scalar(dst[:, 0:width], u, taps[:, 1:2], None, ALU.mult))
                for start, n, w in parts:
                    ui = u[:, start:start + n * w].rearrange("p (n w) -> p n w", w=w)
                    yi = dst[:, start:start + n * w].rearrange("p (n w) -> p n w", w=w)
                    step(V.scalar_tensor_tensor(yi[:, :, 1:], ui[:, :, 0:w - 1], taps[:, 0:1], yi[:, :, 1:],
                                                ALU.mult, ALU.add))
                    last = V.scalar_tensor_tensor(yi[:, :, 0:w - 1], ui[:, :, 1:], taps[:, 2:3],
                                                  yi[:, :, 0:w - 1], ALU.mult, ALU.add)
                    if start + n * w < width:
                        step(last)
                last.then_inc(sig("conv_done"), 1)

            on_x, on_ctx = (0, T // ROW, ROW), (T, 1, T)
            for h in range(H):
                short_conv(h, kT[:, h, :], col("ml_conv", 3 * (4 + h), 3), (on_x, on_ctx))
            dve.wait_ge(sig("softplus_ready"), 1)
            dve.wait_ge(sig("gates_biased"), 1)
            step(V.scalar_tensor_tensor(g_forget[0:H], g_forget[0:H], 0.0, lnb[0:H], ALU.min, ALU.subtract))

            def along(v, s, part):
                w = v[0:H, s, part * T:(part + 1) * T]
                return w if s == 0 else w[:, ::-1]

            for s in range(2):
                for part in range(2):
                    last = V.tensor_tensor_scan(along(bcum, s, part), along(g_forget, s, part), zrow[0:H, :], 0.0,
                                                ALU.add, ALU.add)
            step(last)
            step(V.tensor_tensor(g_in[0:H], g_in[0:H], bcum[0:H], ALU.subtract))
            step(V.tensor_reduce(mcols[0:H, 0:2], g_in[0:H, :, T:], X, ALU.max))
            step(V.tensor_scalar(mcols[0:H, 2:4], mcols[0:H, 0:2], 0.0, None, ALU.max))
            for s in range(2):
                end = 2 * T - 1 if s == 0 else T
                last = V.tensor_tensor(mcols[0:H, 4 + s:5 + s], mcols[0:H, 2 + s:3 + s],
                                       bcum[0:H, s, end:end + 1], ALU.add)
            step(last)
            for s in range(2):
                V.tensor_scalar(g_in[0:H, s, T:], g_in[0:H, s, T:], mcols[0:H, 2 + s:3 + s], None, ALU.subtract)
                m = mrow[0:H, s, :] if s == 0 else mrow[0:H, s, ::-1]
                step(V.tensor_tensor_scan(m, along(g_in, s, 0), along(g_in, s, 0), mcols[0:H, 4 + s:5 + s],
                                          ALU.max, ALU.max))
            for s in range(2):
                V.tensor_scalar(lnb[0:H, s, 0:T], mrow[0:H, s, :], mcols[0:H, 4 + s:5 + s], None, ALU.subtract)
                last = V.tensor_tensor(lnb[0:H, s, T:], mrow[0:H, s, :], bcum[0:H, s, 0:T], ALU.add)
            last.then_inc(sig("gate_rows"), 1)
            for h in range(H):
                short_conv(4 + h, qT[:, h, :], col("ml_conv", 3 * h, 3), (on_x,))
            dve.wait_ge(sig("vbias_loaded"), 16)
            for t in range(2 * TT):
                dve.wait_ge(sig("v_ps"), t + 1)
                V.tensor_tensor(v_tok[:, t, :, 0:P], bank(4 + t).rearrange("p (h e) -> p h e", h=H),
                                vbias[:, :].rearrange("p (h e) -> p h e", h=H), ALU.add).then_inc(sig("v_kept"), 1)
            for c in range(12):
                short_conv(8 + c, hy[:, c, :], col("hy_conv", 3 * c, 3), (on_x,))
            dve.wait_ge(sig("gcols_ps"), 1)
            step(V.tensor_copy(gcols, bank(4)[:, 0:64].rearrange("p (n s t h) -> p n s t h", n=4, s=2, t=TT)))
            V.tensor_scalar(gcols[:, 1], gcols[:, 1], QSCALE, None, ALU.mult).then_inc(sig("gcols_ready"), 1)
            dve.wait_ge(sig("gcols_ready"), 1)

            for h in range(H):
                dve.wait_ge(sig("kc_ps"), h + 1)
                if h >= 1:
                    dve.wait_ge(sig("state_ps"), h)
                for t in range(TT):
                    for s in range(2):
                        last = V.tensor_scalar(kw[:, t, s, :], bank(5)[:, t * P:(t + 1) * P],
                                               gcols[:, 3, s, t, h:h + 1], None, ALU.mult)
                last.then_inc(sig("kw_ready"), 1)
            ada_row(1, 2)
            for h in range(H):
                dve.wait_ge(sig("st_ps"), h + 1)
                if h >= 1:
                    dve.wait_ge(sig("intra_ps"), h)
                for s in range(2):
                    for t in range(TT):
                        a = (P if t == 0 else 0) if s == 0 else (P if t == 0 else 0)
                        last = V.scalar_tensor_tensor(ee[:, s, t, :], bank(5)[:, s * T:(s + 1) * T],
                                                      gcols[:, 0, s, t, h:h + 1], causal[:, s, a:a + T],
                                                      ALU.subtract, ALU.max)
                last.then_inc(sig("gaps_ready"), 1)
                dve.wait_ge(sig("decay_ready"), h + 1)
                for s in range(2):
                    e2 = ee[:, s, :, :].rearrange("p t q -> p (t q)")
                    last = V.scalar_tensor_tensor(e2, bank(4), QSCALE, e2, ALU.mult, ALU.mult)
                last.then_inc(sig("pairs_ready"), 1)
                if h == 0:
                    ada_col(1, 3)
                elif h == 2:
                    ada_row(2, 2)
                elif h == 3:
                    ada_col(2, 3)
                dve.wait_ge(sig("inter_kept"), h + 1)
                dve.wait_ge(sig("intra_ps"), h + 1)
                for t in range(TT):
                    step(V.tensor_tensor(inter[:, t, :], bank(6 + t)[:, 0:2 * VW], inter[:, t, :], ALU.add))
                n = inter.rearrange("p t (s e) -> p t s e", s=2)[:, :, :, P]
                step(V.scalar_tensor_tensor(den, n, -1.0, n, ALU.mult, ALU.max))
                step(V.tensor_tensor(den, den, gcols[:, 2, :, :, h].rearrange("p s t -> p t s"), ALU.max))
                step(V.reciprocal(den, den))
                for t in range(TT):
                    step(V.tensor_scalar(hm[:, t, h, :], inter[:, t, 0:P], den[:, t, 0:1], None, ALU.mult))
                    last = V.scalar_tensor_tensor(hm[:, t, h, :], inter[:, t, VW:VW + P], den[:, t, 1:2],
                                                  hm[:, t, h, :], ALU.mult, ALU.add)
                last.then_inc(sig("head_done"), 1)
            dve.wait_ge(sig("head_done"), H)
            h8 = hm.rearrange("p t h e -> p (t h) e")
            step(V.tensor_tensor(hsq, h8, h8, ALU.mult))
            V.tensor_reduce(hstat, hsq, X, ALU.add).then_inc(sig("hsum_ready"), 1)
            dve.wait_ge(sig("hrms_ready"), 1)
            step(V.reciprocal(hstat, hstat))
            V.tensor_tensor(h8, h8, hstat.unsqueeze(2).broadcast_to([P, TT * H, P]),
                            ALU.mult).then_inc(sig("hm_ready"), 1)
            dve.wait_ge(sig("hmT_ps"), 1)
            for h in range(H):
                last = V.scalar_tensor_tensor(oT[:, h, :], bank(6 + h // 2)[:, (h % 2) * T:(h % 2 + 1) * T],
                                              col("ml_g", h), oT[:, h, :], ALU.mult, ALU.mult)
            last.then_inc(sig("yb_ready"), 1)

            for o in range(ORDERS):
                dve.wait_ge(sig("signal_ps"), o + 1)
                for t in range(TT):
                    re, im = bank(t), bank(2 + t)
                    V.tensor_tensor(yt[:, 0, :], re, spec[:, o, 0, t, :], ALU.mult)
                    V.tensor_tensor(yt[:, 1, :], im, spec[:, o, 1, t, :], ALU.mult)
                    V.tensor_tensor(yt[:, 2, :], im, spec[:, o, 0, t, :], ALU.mult)
                    step(V.tensor_tensor(yt[:, 3, :], re, spec[:, o, 1, t, :], ALU.mult))
                    V.tensor_tensor(yspec[:, 0, t, :], yt[:, 0, :], yt[:, 1, :], ALU.subtract)
                    last = V.tensor_tensor(yspec[:, 1, t, :], yt[:, 2, :], yt[:, 3, :], ALU.add)
                    if t == 0:
                        step(last)
                last.then_inc(sig("yspec_ready"), 1)
                dve.wait_ge(sig("conv_ps"), o + 1)
                for j in range(4):
                    z = hy[:, 4 * o + j, :]
                    step(V.scalar_tensor_tensor(z, z, col("skip", 4 * o + j),
                                                bank(4 + j // 2)[:, (j % 2) * T:(j % 2 + 1) * T], ALU.mult, ALU.add))
                    last = V.tensor_tensor(hy[:, 4 * o + 4 + j, :], hy[:, 4 * o + 4 + j, :], z, ALU.mult)
                last.then_inc(sig("z_done"), 1)
            dve.wait_ge(sig("unit_kept"), 41)
            for k in range(KD):
                dve.wait_ge(sig("branch_ps"), k + 1)
                m = merge[:, k, :, :].rearrange("p g t -> p (g t)")
                step(V.tensor_tensor(m, bank(k % 4), m, ALU.mult))
                V.tensor_tensor(merge[:, k, 0, :], merge[:, k, 0, :], merge[:, k, 1, :],
                                ALU.add).then_inc(sig("merged"), 1)

            def two_banks(b):
                return ps[:, b:b + 2, :].rearrange("p b n -> p (b n)")

            dve.wait_ge(sig("grow_ready"), 1)
            for t in range(TT):
                dve.wait_ge(sig("mixed1_ps"), t + 1)
                step(V.tensor_tensor(gtmp[:, t, :], two_banks(4 + 2 * t), grow, ALU.mult))
                V.tensor_tensor(x_tok[:, t, :], x_tok[:, t, :], gtmp[:, t, :], ALU.add).then_inc(sig("x1_ready"), 1)
            dve.wait_ge(sig("ada_cols_ready"), 3)
            step(V.scalar_tensor_tensor(mod2[:, :], ada_cols[:, 0, 32:40], 1.0, col("g_ffn", 0, 8),
                                        ALU.add, ALU.mult))
            V.memset(zeros, 0.0)
            normalize(step, sig("rms_ready"), 2 * TT, 0, x_tok, xn, sig("norm_ready"))
            for k in (2, 3, 6, 7):
                if k % 2 == 0:
                    dve.wait_ge(sig("h2T_ps"), k // 2 + 1)
                V.tensor_scalar(h2T[:, k, :], bank(k // 2)[:, (k % 2) * T:(k % 2 + 1) * T], mod2[:, k:k + 1],
                                ada_cols[:, 0, 24 + k:25 + k], ALU.mult, ALU.add).then_inc(sig("h2T_ready_v"), 1)

            dve.wait_ge(sig("logits_ps"), 1)
            lg = ps[:, 4:8:2, 0:NE]
            step(V.tensor_reduce(esum, lg, X, ALU.max))
            V.tensor_tensor(aff, lg, esum.unsqueeze(2).broadcast_to([P, TT, NE]),
                            ALU.subtract).then_inc(sig("logits_ready"), 1)
            dve.wait_ge(sig("exp_ready"), 1)
            step(V.tensor_reduce(esum, aff, X, ALU.add))
            step(V.reciprocal(esum, esum))
            V.tensor_tensor(aff, aff, esum.unsqueeze(2).broadcast_to([P, TT, NE]),
                            ALU.mult).then_inc(sig("aff_ready"), 1)
            dve.wait_ge(sig("affT_ps"), 1)
            step(V.tensor_copy(affT[0:NE, :], bank(5)[0:NE, 0:T]))
            for n in range(CAP // 8):
                v, i = topv[0:NE, 8 * n:8 * n + 8], topi[0:NE, 8 * n:8 * n + 8]
                step(V.max(v, affT[0:NE, :]))
                step(V.max_index(i, v, affT[0:NE, :]))
                step(V.match_replace(affT[0:NE, :], v, affT[0:NE, :], -1.0))
            step(V.tensor_copy(topf[0:NE, :], topi[0:NE, :]))
            dve.wait_ge(sig("bmask_loaded"), 16)
            V.tensor_tensor(bdiag[0:NE], bmask[0:NE], topf[0:NE, :].unsqueeze(1).broadcast_to([NE, NE, CAP]), ALU.mult)
            V.tensor_copy(rep[0:NE, 0], topf[0:NE, :].unsqueeze(1).broadcast_to([NE, 4, CAP]))
            V.tensor_copy(rep[0:NE, 1], topv[0:NE, :].unsqueeze(1).broadcast_to([NE, 4, CAP])).then_inc(sig("top_ready"), 1)
            dve.wait_ge(sig("top_ps"), 1)
            for t in range(TT):
                last = V.tensor_scalar(sel[:, t, :], bank(6), col("token", t), None, ALU.is_equal)
            last.then_inc(sig("sel_ready"), 1)
            step(V.tensor_copy(igcols, bank(7)[:, 0:2 * NE].rearrange("p (a e) -> p a e", a=2)))
            with dve.Fori(0, NE) as e:
                dve.wait_ge(sig("xg_ps"), e + 1)
                V.tensor_tensor(xe, bank(5)[:, 0:KD * CAP].rearrange("p (k c) -> p k c", k=KD),
                                mod2[:, :].unsqueeze(2).broadcast_to([P, KD, CAP]),
                                ALU.mult).then_inc(sig("xe_scaled"), 1)
                dve.wait_ge(sig("xe_scaled"), e + 1)
                V.tensor_tensor(xe, xe, ada_cols[:, 0, 24:32].unsqueeze(2).broadcast_to([P, KD, CAP]),
                                ALU.add).then_inc(sig("xe_ready"), 1)
                V.tensor_scalar(scat, iota, igcols[:, 0, bass.ds(e, 1)], igcols[:, 1, bass.ds(e, 1)],
                                ALU.is_equal, ALU.mult).then_inc(sig("scat_ready"), 1)
                dve.wait_ge(sig("b_ps"), e + 1)
                dve.wait_ge(sig("sa_ready"), e + 1)
                V.tensor_tensor(hid_e, sa, bank(5), ALU.mult).then_inc(sig("hid_e_ready"), 1)
                dve.wait_ge(sig("hTe_ps"), e + 1)
                V.tensor_copy(hTe, bank(4).rearrange("p (q c) -> p q c", q=4)).then_inc(sig("hTe_ready"), 1)

            step2 = Link(dve, sig("dve_step2"))
            dve.wait_ge(sig("grow_ready"), 2)
            dve.wait_ge(sig("moe_ps"), 1)
            for t in range(TT):
                step2(V.tensor_tensor(gtmp2[:, t, :], two_banks(2 * t), grow2, ALU.mult))
                V.tensor_tensor(x_tok[:, t, :], x_tok[:, t, :], gtmp2[:, t, :], ALU.add).then_inc(sig("x2_ready"), 1)

            def final_norm(before, done):
                for t in range(TT):
                    dve.wait_ge(sig("rms_ready"), before + t + 1)
                    step2(V.reciprocal(stat[:, 0, t:t + 1], stat[:, 0, 2 + t:3 + t]))
                    V.scalar_tensor_tensor(x_tok[:, t, :], x_tok[:, t, :], stat[:, 0, t:t + 1], fin_rows[:, :],
                                           ALU.mult, ALU.mult).then_inc(done, 1)

            dve.wait_ge(sig("fin_loaded"), 16)
            final_norm(3 * TT, sig("h_ready"))

            with dve.Fori(0, LAYERS) as l:
                step = Link(dve, sig("dve_layer_step"), l, 3 * TT + 1 + TT * 4 + KD)

                def norm(n):
                    normalize(step, sig("rms2_ready"), (l * 3 + n) * TT, 0, x_tok, xn, sig("norm2_ready"))

                def norm_turned(n):
                    for b in (0, 2):
                        dve.wait_ge(sig("uT_ps"), l * 12 + n * 4 + b + 1)
                        for k in (2 * b, 2 * b + 1):
                            last = V.tensor_scalar(uT[:, k, :], bank(b)[:, (k % 2) * T:(k % 2 + 1) * T],
                                                   lcol("norm", 8 * n + k), None, ALU.mult)
                        last.then_inc(sig("uT_ready"), 1)

                def lower(f, n):
                    if n < len(FFN_SLOTS):
                        at = (FIRST_SLOTS + NE * EXPERT_SLOTS + FFN_AT[f] + n) % RING
                        dve.wait_ge(sig("w_hi_ready"), (l * 2 + f) * len(FFN_SLOTS) + n + 1)
                        V.tensor_tensor(w_lo[:, n % SPLITS, :], ring[:, at, :], w_hi[:, n % SPLITS, :].bitcast(F32),
                                        ALU.subtract).then_inc(sig("w_ready"), 1)

                def ffn(f):
                    norm(2 * f)
                    if f == 0:
                        lower(f, 0)
                        dve.wait_ge(sig("lcols_loaded"), l * 16 + 16)
                    for b in range(4):
                        dve.wait_ge(sig("u_hi_ready"), l * 8 + f * 4 + b + 1)
                        for k in (2 * b, 2 * b + 1):
                            last = V.scalar_tensor_tensor(u_lo[:, k, :], bank(b)[:, (k % 2) * T:(k % 2 + 1) * T],
                                                          lcol("norm", 16 * f + k), u_hi[:, k, :].bitcast(F32),
                                                          ALU.mult, ALU.subtract)
                        last.then_inc(sig("u_ready"), 1)
                    if f == 0:
                        lower(f, 1)
                    lower(f, 2)
                    for n, (kind, i) in enumerate(FFN_SLOTS):
                        if kind == "up":
                            dve.wait_ge(sig("silu2_ready"), l * 2 * FT + f * FT + i + 1)
                            if i >= 4:
                                dve.wait_ge(sig("down_step"), (l * 2 + f) * DOWN_STEPS + (i - 4) // 2 + 1)
                            b = bank(4 + i % 4)[:, T:]
                            V.tensor_tensor(hid_hi[:, i % 4, :], b, sa2[:, i % 2, :], ALU.mult)
                            V.tensor_tensor(hid[:, i % 2, :], b, sa2[:, i % 2, :], ALU.mult).then_inc(sig("hid_mid"), 1)
                            dve.wait_ge(sig("hid_mid"), l * 2 * FT + f * FT + i + 1)
                            V.tensor_tensor(hid_lo[:, i % 4, :], hid[:, i % 2, :], hid_hi[:, i % 4, :].bitcast(F32),
                                            ALU.subtract).then_inc(sig("hid_done"), 1)
                        lower(f, n + SPLITS)
                    for t in range(TT):
                        dve.wait_ge(sig("down_step"), (l * 2 + f + 1) * DOWN_STEPS - 1 + t)
                        V.scalar_tensor_tensor(x_tok[:, t, :], two_banks(2 * t), 0.5, x_tok[:, t, :],
                                               ALU.mult, ALU.add).then_inc(sig("h_ready"), 1)

                ffn(0)
                norm(1)
                norm_turned(1)
                dve.wait_ge(sig("qk_kept"), l + 1)
                dve.wait_ge(sig("tabs2_loaded"), 16)
                q1, q2 = qk[:, :, :, 0:8], qk[:, :, :, 8:16]

                def table(f):
                    return rope[:, f].unsqueeze(2).broadcast_to([P, TT, 10, 8])

                tmp = [rtmp[:, i].rearrange("p t (h c) -> p t h c", c=8) for i in range(4)]
                V.tensor_tensor(tmp[0], q1, table(0), ALU.mult)
                V.tensor_tensor(tmp[1], q2, table(1), ALU.mult)
                V.tensor_tensor(tmp[2], q2, table(0), ALU.mult)
                step(V.tensor_tensor(tmp[3], q1, table(1), ALU.mult))
                V.tensor_tensor(q1, tmp[0], tmp[1], ALU.subtract)
                V.tensor_tensor(q2, tmp[2], tmp[3], ALU.add).then_inc(sig("rope_ready"), 1)

                def scores(t):
                    dve.wait_ge(sig("scores_ps"), l * TT + t + 1)
                    a = att[:, t, :, :]
                    m = mst[:, t, 0, :]
                    V.scalar_tensor_tensor(a, ps[:, 0:4, :].rearrange("p b (f k) -> p (b f) k", f=2), 0.125,
                                           amask[:, t, :].unsqueeze(1).broadcast_to([P, 8, T]),
                                           ALU.mult, ALU.add).then_inc(sig("scores_kept"), 1)
                    dve.wait_ge(sig("scores_kept"), l * TT + t + 1)
                    step(V.tensor_reduce(m, a, X, ALU.max))
                    step(V.tensor_tensor(m, m, lcol("sink", 0, 8), ALU.max))
                    V.tensor_tensor(mst[:, t, 1, :], lcol("sink", 0, 8), m, ALU.subtract)
                    V.tensor_scalar(mst[:, t, 2, :], m, -1.0, None, ALU.mult).then_inc(sig("max_ready"), 1)

                def probabilities(t):
                    dve.wait_ge(sig("att_exp"), l * TT + t + 1)
                    a = att[:, t, :, :]
                    m = mst[:, t, 0, :]
                    step(V.tensor_tensor(m, mst[:, t, 3, :], mst[:, t, 1, :], ALU.add))
                    step(V.reciprocal(m, m))
                    V.tensor_tensor(a, a, m.unsqueeze(2).broadcast_to([P, 8, T]),
                                    ALU.mult).then_inc(sig("att_ready"), 1)

                def keep_att(c):
                    dve.wait_ge(sig("attT_ps"), l * 8 + c + 1)
                    V.tensor_copy(attT[:, (c // 2) % 2, 0:4, (c // 4) * P:(c // 4 + 1) * P],
                                  bank(4).rearrange("p (h q) -> p h q", h=4)).then_inc(sig("attT_kept"), 1)

                scores(0)
                probabilities(0)
                scores(1)
                keep_att(0)
                keep_att(2)
                probabilities(1)
                keep_att(4)
                keep_att(6)
                for k in range(KD):
                    dve.wait_ge(sig("branch2_ps"), l * KD + k + 1)
                    g = sgate[:, k, :, :].rearrange("p g t -> p (g t)")
                    step(V.tensor_tensor(g, bank(6 + k % 2), g, ALU.mult))
                    V.tensor_tensor(mT[:, k, :], sgate[:, k, 0, :], sgate[:, k, 1, :],
                                    ALU.add).then_inc(sig("mT_ready"), 1)
                    if k in (5, 7):
                        lower(1, (k - 5) // 2)
                for t in range(TT):
                    dve.wait_ge(sig("mixer_ps"), l * TT + t + 1)
                    V.tensor_tensor(x_tok[:, t, :], two_banks(2 * t), x_tok[:, t, :],
                                    ALU.add).then_inc(sig("h_ready"), 1)
                ffn(1)
                step.close()

            dve.wait_ge(sig("fin_loaded"), 32)
            final_norm(4 * TT, sig("out_ready"))

        @block.tensor
        def _(pe):
            M = nc.tensor
            pending = [0]

            def mm(out, lhsT, rhs, start=True, stop=True, ready=None, free=0, **more):
                ins = M.matmul(out, lhsT, rhs, start=start, stop=stop, **more)
                pending[0] += free
                if ready is not None:
                    ins.then_inc(ready, 1)
                elif pending[0]:
                    ins.then_inc(sig("slot_used"), pending[0])
                    pending[0] = 0

            def turn(out, src, rows=P, ready=None):
                ins = M.transpose(out, src, ident[0:rows, 0:rows])
                if ready is not None:
                    ins.then_inc(ready, 1)
                elif pending[0]:
                    ins.then_inc(sig("slot_used"), pending[0])
                    pending[0] = 0

            def slot(n, turns=0):
                pe.wait_ge(sig(f"slot_loaded{n % RING}"), (turns + n // RING) * 16 + 16)
                return ring[:, n % RING, :]

            def ada(b, steps, first):
                for k in steps:
                    w = slot(first + k)
                    for g in range(4):
                        mm(bank(b)[32 * g:32 * g + 32, :], silu_c[:, k, :], w[:, 512 * g:512 * g + 512],
                           start=k == 0, stop=k == KD - 1, free=int(g == 3),
                           ready=sig("ada_ps") if k == KD - 1 and g == 3 else None)

            def ada_turn(r, b):
                pe.wait_ge(sig("const_loaded"), 16)
                pe.wait_ge(sig("ada_row"), r + 1)
                for q in range(4):
                    turn(bank(b)[:, q * P:(q + 1) * P], ada_rows[:, r, q * P:(q + 1) * P],
                         ready=sig("ada_T_ps") if q == 3 else None)
            pe.wait_ge(sig("filt_loaded"), 16)
            f = {k: filt[:, v:] for k, v in FILT.items()}
            mm(bank(0)[0:HID, 0:T], f["w1"][0:EMB, 0:HID], f["z"][0:EMB, 0:T], ready=sig("filter_ps"))
            pe.wait_ge(sig("hid_ready"), 1)
            mm(bank(1)[0:HID, 0:T], f["w2"][0:HID, 0:HID], hid1[0:HID, :], ready=sig("filter_ps"))
            pe.wait_ge(sig("hid_ready"), 2)
            for o in range(ORDERS):
                for side in range(2):
                    for t in range(TT):
                        last = side == 1 and t == 1
                        mm(bank((2 + 4 * o + 2 * side + t) % 8), hid2[0:HID, t * P:(t + 1) * P],
                           f["w3"][0:HID, (2 * o + side) * HYC:(2 * o + side + 1) * HYC],
                           ready=sig("filter_ps") if last else None)
            pe.wait_ge(sig("tabs_loaded"), 16)
            for o in range(ORDERS):
                pe.wait_ge(sig("pm_ready"), o + 1)
                if o == 1:
                    pe.wait_ge(sig("spec_kept"), 1)
                for j in range(2):
                    for k in range(TT):
                        for t in range(TT):
                            mm(bank(2 + 2 * j + k), dft[:, j, t, k * P:(k + 1) * P], pm[o][:, j, t, :],
                               start=t == 0, stop=t == 1,
                               ready=sig("spec_ready") if j == k == t == 1 else None)
                if o == 0:
                    pe.wait_ge(sig("pm_ready"), ORDERS)
                    pe.wait_ge(sig("silu_ready"), 1)
                    ada(7, range(4), 0)

            pe.wait_ge(sig("const_loaded"), 16)
            pe.wait_ge(sig("norm_ready"), 2 * TT)
            pe.wait_ge(sig("spec_kept"), 2)
            for k in range(KD):
                if k == KD - 1:
                    ada(7, range(4, KD), 0)
                    ada_turn(0, 7)
                    pe.wait_ge(sig("mod1_ready"), 1)
                for t in range(2 * TT):
                    src = (xn if t < TT else cn)[:, t % TT, k * P:(k + 1) * P]
                    turn(bank(k)[:, t * P:(t + 1) * P], src, ready=sig("hT_ps") if t == 3 else None)
            pe.wait_ge(sig("hT_ready"), KD // 2)
            pe.wait_ge(sig("hT_ready_a"), KD // 2)

            def unit_bank(n):
                if n >= 4:
                    pe.wait_ge(sig("unit_kept"), n - 3)
                return bank(n % 4)

            pe.wait_ge(sig("wgate_loaded"), 16)
            b = unit_bank(0)
            for k in range(KD):
                for g in range(4):
                    mm(b[32 * g:32 * g + H, :], wgate[:, k, 4 * g:4 * g + H], hT[:, k, :], start=k == 0,
                       stop=k == KD - 1, ready=sig("unit_ready") if k == KD - 1 and g == 3 else None)

            def features(units, at, width):
                for i, n in enumerate(units):
                    w = slot(at + i // 2)
                    b = unit_bank(n)
                    for k in range(KD):
                        a = (i % 2) * 1024 + k * P
                        mm(b[:, 0:width], w[:, a:a + P], hT[:, k, 0:width], start=k == 0, stop=k == KD - 1,
                           free=int(k == KD - 1 and i % 2 == 1), ready=sig("unit_ready") if k == KD - 1 else None)

            features(range(1, 5), 8, 2 * T)
            features(range(5, 9), 10, T)
            for t in range(2 * TT):
                for k in range(KD):
                    w = slot(12 + k // 4)
                    a = (k % 4) * 512
                    mm(bank(4 + t), hT[:, k, t * P:(t + 1) * P], w[:, a:a + 512], start=k == 0, stop=k == KD - 1,
                       free=int(t == 3 and k % 4 == 3), ready=sig("v_ps") if k == KD - 1 else None)
            features(range(9, 13), 14, T)
            features(range(13, 25), 16, T)
            pe.wait_ge(sig("gate_exps"), 1)
            pe.wait_ge(sig("v_kept"), 2 * TT)
            for n, (rows, off) in enumerate(((g_in, 0), (lnb, 0), (lnb, T), (g_in, T))):
                for s in range(2):
                    for t in range(TT):
                        a = off + t * P
                        at = (n * 4 + s * 2 + t) * H
                        turn(bank(4)[:, at:at + H], rows[0:H, s, a:a + P], rows=H,
                             ready=sig("gcols_ps") if n == 3 and s == t == 1 else None)
            features(range(25, 33), 22, T)

            pe.wait_ge(sig("k_ready"), H)
            pe.wait_ge(sig("q_ready"), H)
            pe.wait_ge(sig("gcols_ready"), 1)
            for h in range(H):
                if h >= 1:
                    pe.wait_ge(sig("kw_ready"), h)
                for t in range(TT):
                    turn(bank(5)[:, t * P:(t + 1) * P], kT[:, h, T + t * P:T + (t + 1) * P],
                         ready=sig("kc_ps") if t == 1 else None)
                if h == 0:
                    pe.wait_ge(sig("unit_kept"), 33)
                ada(2, range(2 * h, 2 * h + 2), 26)
                pe.wait_ge(sig("kw_ready"), h + 1)
                if h >= 1:
                    pe.wait_ge(sig("state_kept"), h)
                for s in range(2):
                    for t in range(TT):
                        mm(bank(6)[:, s * VW:(s + 1) * VW], kw[:, t, s, :], v_tok[:, TT + t, h, :],
                           start=t == 0, stop=t == 1, ready=sig("state_ps") if s == t == 1 else None)
            pe.wait_ge(sig("state_kept"), H)
            for h in range(H):
                if h >= 1:
                    pe.wait_ge(sig("pairs_ready"), h)
                for t in range(TT):
                    mm(bank(4)[:, t * T:(t + 1) * T], kT[:, h, t * P:(t + 1) * P], qT[:, h, :])
                for s in range(2):
                    mm(bank(5)[:, s * T:(s + 1) * T], ident[:, h:h + 1].broadcast_to([P, P]), mrow[:, s, :],
                       ready=sig("st_ps") if s == 1 else None)
                if h >= 1:
                    pe.wait_ge(sig("inter_kept"), h)
                for t in range(TT):
                    mm(bank(t)[:, 0:2 * VW], qT[:, h, t * P:(t + 1) * P],
                       states[:, 2 * h:2 * h + 2, :].rearrange("p s e -> p (s e)"),
                       ready=sig("inter_ps") if t == 1 else None)
                if h == 0:
                    ada_turn(1, 3)
                if h < 3:
                    ada(2, range(3 * h, min(3 * h + 3, KD)), 34)
                else:
                    pe.wait_ge(sig("ada_cols_ready"), 2)
                    ada_turn(2, 3)
                pe.wait_ge(sig("pairs_ready"), h + 1)
                if h >= 1:
                    pe.wait_ge(sig("head_done"), h)
                for t in range(TT):
                    for s in range(2):
                        keys = range(0, t + 1) if s == 0 else range(t, TT)
                        for u in keys:
                            mm(bank(6 + t)[:, s * VW:(s + 1) * VW], ee[:, s, u, t * P:(t + 1) * P],
                               v_tok[:, u, h, :], start=u == keys[0], stop=u == keys[-1],
                               ready=sig("intra_ps") if t == s == 1 else None)

            def merge_units(*units):
                for n in units:
                    w = slot(42 + (n - 33) // 2)
                    if n >= 35:
                        pe.wait_ge(sig("unit_kept"), n - 1)
                    for k in range(KD):
                        a = ((n - 33) % 2) * 1024 + k * P
                        last = k == KD - 1
                        mm(bank(6 + n % 2)[:, 0:T], w[:, a:a + P], hT[:, k, 0:T], start=k == 0, stop=last,
                           free=int(last and n % 2 == 0), ready=sig("unit_ready") if last else None)

            pe.wait_ge(sig("conv_done"), 20)
            for o in range(ORDERS):
                if o == 1:
                    pe.wait_ge(sig("z_done"), 1)
                for t in range(TT):
                    for j in range(4):
                        turn(bank(4 + t)[:, j * P:(j + 1) * P], hy[:, 4 * o + j, t * P:(t + 1) * P],
                             ready=sig("z_ps") if t == 1 and j == 3 else None)
                if o == 1:
                    merge_units(37)
                pe.wait_ge(sig("z_kept"), o + 1)
                if o == 0:
                    pe.wait_ge(sig("ada_cols_ready"), 3)
                    pe.wait_ge(sig("inter_kept"), H)
                for j in range(2):
                    for k in range(TT):
                        for t in range(TT):
                            mm(bank(2 * j + k), dft[:, j, t, k * P:(k + 1) * P], z_tok[:, t, :],
                               start=t == 0, stop=t == 1,
                               ready=sig("signal_ps") if j == k == t == 1 else None)
                if o == 0:
                    pe.wait_ge(sig("hm_ready"), 1)
                    for h in range(H):
                        for t in range(TT):
                            turn(bank(6 + h // 2)[:, (h % 2) * T + t * P:(h % 2) * T + (t + 1) * P], hm[:, t, h, :],
                                 ready=sig("hmT_ps") if h == 3 and t == 1 else None)
                    pe.wait_ge(sig("yb_ready"), 1)
                    merge_units(33, 34, 35)
                else:
                    merge_units(38, 39)
                pe.wait_ge(sig("yspec_ready"), o + 1)
                for j in range(4):
                    n = 0
                    for i in range(2):
                        for k in range(TT):
                            mm(bank(4 + j // 2)[:, (j % 2) * T:(j % 2 + 1) * T], yspec[:, i, k, j * P:(j + 1) * P],
                               idft[:, i, k, :], start=n == 0, stop=n == 3,
                               ready=sig("conv_ps") if j == n == 3 else None)
                            n += 1
                merge_units(36 if o == 0 else 40)
            pe.wait_ge(sig("z_done"), ORDERS)

            def branches(at, turns, bank_of, kept, ya, yb, ready):
                for k in range(KD):
                    w = slot(at + k // 2, turns)
                    kept(k)
                    b = bank_of(k)
                    for g, y in enumerate((ya, yb)):
                        for i in range(4):
                            a = (k % 2) * 1024 + g * 512 + i * P
                            last = g == 1 and i == 3
                            mm(b[:, g * T:(g + 1) * T], w[:, a:a + P], y(i), start=i == 0, stop=i == 3,
                               free=int(last and k % 2 == 1), ready=ready if last else None)

            def kept1(k):
                if k >= 4:
                    pe.wait_ge(sig("merged"), k - 3)

            branches(46, 0, lambda k: bank(k % 4), kept1, lambda i: hy[:, 8 + i, :], lambda i: oT[:, i, :],
                     sig("branch_ps"))

            def token_out(at, turns, banks, x, tiles, ready):
                for i in range(tiles // 2):
                    w = slot(at + i, turns)
                    for t in range(TT):
                        for j in range(2):
                            k = 2 * i + j
                            src = x(k)
                            for c in range(2):
                                last = j == c == 1
                                mm(bank(banks + 2 * t + c), src[:, t * P:(t + 1) * P],
                                   w[:, j * 1024 + c * 512:j * 1024 + (c + 1) * 512], start=k == 0,
                                   stop=k == tiles - 1, free=int(last and t == 1),
                                   ready=ready if last and i == tiles // 2 - 1 else None)

            for g in range(2):
                mm(bank(4 + g), ident[:, 32 * g:32 * g + 1].broadcast_to([P, P]), ada_rows[:, 1, :],
                   ready=sig("grow_ps") if g == 1 else None)
            pe.wait_ge(sig("grow_ready"), 1)
            pe.wait_ge(sig("merged"), KD)
            token_out(50, 0, 4, lambda k: merge[:, k, 0, :], KD, sig("mixed1_ps"))
            slot(54)
            slot(55)
            pending[0] += 2

            for t in range(TT):
                pe.wait_ge(sig("norm_ready"), 2 * TT + t + 1)
                for k in range(KD):
                    turn(bank(k // 2)[:, (k % 2) * T + t * P:(k % 2) * T + (t + 1) * P], xn[:, t, k * P:(k + 1) * P],
                         ready=sig("h2T_ps") if k % 2 == 1 and t == 1 else None)
            pe.wait_ge(sig("wrouter_loaded"), 16)
            pe.wait_ge(sig("x1_ready"), TT)
            for k in range(KD):
                pe.wait_ge(sig("h2T_ready") if k % 4 < 2 else sig("h2T_ready_v"), k // 4 * 2 + k % 2 + 1)
                for t in range(TT):
                    mm(bank(4 + 2 * t)[:, 0:NE], h2T[:, k, t * P:(t + 1) * P], wrouter[:, k, :],
                       start=k == 0, stop=k == KD - 1, ready=sig("logits_ps") if t == 1 and k == KD - 1 else None)
            pe.wait_ge(sig("aff_ready"), 1)
            for t in range(TT):
                turn(bank(5)[0:NE, t * P:(t + 1) * P], aff[:, t, :], ready=sig("affT_ps") if t == 1 else None)
            for g in range(2):
                mm(bank(g), ident[:, 64 + 32 * g:65 + 32 * g].broadcast_to([P, P]), ada_rows[:, 2, :],
                   ready=sig("grow_ps") if g == 1 else None)
            pe.wait_ge(sig("top_ready"), 1)
            for a in range(2):
                turn(bank(7)[:, a * NE:(a + 1) * NE], rep[0:NE, a].rearrange("p g c -> p (g c)"), rows=NE)
            mm(bank(6), ones[0:NE, :], bdiag[0:NE].rearrange("p e c -> p (e c)"), ready=sig("top_ps"))
            pe.wait_ge(sig("grow_ready"), 2)
            for b in range(4):
                mm(bank(b), zeros[:, 0:P], zeros, start=True, stop=False)
            pe.wait_ge(sig("sel_ready"), 1)

            turns0 = FIRST_SLOTS // RING
            with pe.Fori(0, NE) as e:
                turns = e * (EXPERT_SLOTS // RING) + turns0
                for k in range(KD):
                    for t in range(TT):
                        mm(bank(5)[:, k * CAP:(k + 1) * CAP], xn[:, t, k * P:(k + 1) * P],
                           sel[:, t, bass.ds(e * CAP, CAP)], start=t == 0, stop=t == 1,
                           ready=sig("xg_ps") if k == KD - 1 and t == 1 else None)
                pe.wait_ge(sig("xe_ready"), e + 1)
                for i, ready in enumerate((sig("a_ps"), sig("b_ps"))):
                    for k in range(KD):
                        w = slot(i * KD + k, turns)
                        for g in range(4):
                            mm(bank(4 + i)[32 * g:32 * g + 32, :], xe[:, k, :], w[:, 512 * g:512 * g + 512],
                               start=k == 0, stop=k == KD - 1, free=int(g == 3),
                               ready=ready if k == KD - 1 and g == 3 else None)
                pe.wait_ge(sig("hid_e_ready"), e + 1)
                for q in range(4):
                    turn(bank(4)[:, q * P:(q + 1) * P], hid_e[:, q * P:(q + 1) * P],
                         ready=sig("hTe_ps") if q == 3 else None)
                pe.wait_ge(sig("hTe_ready"), e + 1)
                for i in range(8):
                    w = slot(2 * KD + i, turns)
                    for c in range(2):
                        for j in range(2):
                            k = 2 * i + j
                            q, g = k % 4, k // 4
                            last = c == j == 1
                            mm(bank(6 + c)[32 * q:32 * q + 32, :], hTe[:, q, 32 * g:32 * g + 32],
                               w[:, j * 1024 + c * 512:j * 1024 + (c + 1) * 512], start=g == 0, stop=g == 3,
                               free=int(last), ready=sig("ye_ps") if last and i == 7 else None)
                pe.wait_ge(sig("ye_ready"), e + 1)
                pe.wait_ge(sig("scat_ready"), e + 1)
                for t in range(TT):
                    for c in range(2):
                        mm(bank(2 * t + c), scat[:, t * P:(t + 1) * P], ye[:, c * 512:(c + 1) * 512],
                           start=False, stop=False)
                assert pending[0] == 0
            for b in range(4):
                mm(bank(b), zeros[:, 0:P], zeros, start=False, stop=True,
                   ready=sig("moe_ps") if b == 3 else None)

            turns1 = (FIRST_SLOTS + NE * EXPERT_SLOTS) // RING
            with pe.Fori(0, LAYERS) as l:
                turns = l * (LAYER_SLOTS // RING) + turns1

                def norm(n):
                    for t in range(TT):
                        pe.wait_ge(sig("norm2_ready"), (l * 3 + n) * TT + t + 1)
                        for k in range(KD):
                            turn(bank(k // 2)[:, (k % 2) * T + t * P:(k % 2) * T + (t + 1) * P],
                                 xn[:, t, k * P:(k + 1) * P], ready=sig("uT_ps") if k % 2 == 1 and t == 1 else None)
                    if n == 1:
                        pe.wait_ge(sig("uT_ready"), l * 2 + 2)
                        pe.wait_ge(sig("uT_ready_a"), l * 2 + 2)

                def pair(at, w, b, ready):
                    for g in range(2):
                        for k in range(KD):
                            a = g * 1024 + k * P
                            last = g == 1 and k == KD - 1
                            mm(b[:, g * T:(g + 1) * T], w[:, a:a + P], uT[:, k, :], start=k == 0, stop=k == KD - 1,
                               free=int(last), ready=ready if last else None)

                def product3(out, lhs, rhs, start, stop, **more):
                    mm(out, lhs[0], rhs[0], start=start, stop=False)
                    mm(out, lhs[0], rhs[1], start=False, stop=False)
                    mm(out, lhs[1], rhs[0], start=False, stop=stop, **more)

                def ffn(f, at):
                    norm(2 * f)
                    for n, (kind, i) in enumerate(FFN_SLOTS):
                        pe.wait_ge(sig("w_ready"), l * 2 * len(FFN_SLOTS) + f * len(FFN_SLOTS) + n + 1)
                        w = (w_hi[:, n % SPLITS, :], w_lo[:, n % SPLITS, :])
                        if kind == "up":
                            if i >= 4:
                                pe.wait_ge(sig("hid_done"), l * 2 * FT + f * FT + i - 3)
                            b = bank(4 + i % 4)
                            for g in range(2):
                                for k in range(KD):
                                    if n == g == 0 and k % 2 == 0:
                                        pe.wait_ge(sig("u_ready"), l * 8 + f * 4 + k // 2 + 1)
                                    a = g * 1024 + k * P
                                    last = g == 1 and k == KD - 1
                                    product3(b[:, g * T:(g + 1) * T], [v[:, a:a + P] for v in w],
                                             (u_hi[:, k, :], u_lo[:, k, :]), k == 0, k == KD - 1,
                                             free=int(last), ready=sig("ffn_ps") if last else None)
                        else:
                            pe.wait_ge(sig("hid_done"), l * 2 * FT + f * FT + 2 * i + 2)
                            for t in range(TT):
                                for j in range(2):
                                    k = 2 * i + j
                                    for c in range(2):
                                        a = j * 1024 + c * 512
                                        last = j == c == 1
                                        h = [v[:, k % 4, t * P:(t + 1) * P] for v in (hid_hi, hid_lo)]
                                        product3(bank(2 * t + c), h, [v[:, a:a + 512] for v in w], k == 0,
                                                 k == FT - 1, free=int(last and t == 1),
                                                 ready=sig("down_step") if last and (t == 1 or k == FT - 1)
                                                 else None)

                ffn(0, 0)
                at = 33
                norm(1)
                for t in range(TT):
                    for k in range(KD):
                        w = slot(at + k // 4, turns)
                        a = (k % 4) * 512
                        mm(bank(t), uT[:, k, t * P:(t + 1) * P], w[:, a:a + 512], start=k == 0, stop=k == KD - 1,
                           free=int(t == 1 and k % 4 == 3))
                w = slot(at + 2, turns)
                for t in range(TT):
                    for k in range(KD):
                        mm(bank(2)[:, t * T:(t + 1) * T], uT[:, k, t * P:(t + 1) * P], w[:, k * T:(k + 1) * T],
                           start=k == 0, stop=k == KD - 1, free=int(t == 1 and k == KD - 1))
                for t in range(TT):
                    for k in range(KD):
                        w = slot(at + 3 + k // 4, turns)
                        a = (k % 4) * 512
                        mm(bank(3 + t), uT[:, k, t * P:(t + 1) * P], w[:, a:a + 512], start=k == 0, stop=k == KD - 1,
                           free=int(t == 1 and k % 4 == 3), ready=sig("qkvp_ps") if t == 1 and k == KD - 1 else None)

                def gate(k):
                    if k >= 2:
                        pe.wait_ge(sig("gate_kept"), l * KD + k - 1)
                    pair(at + 5 + k, slot(at + 5 + k, turns), bank(6 + k % 2), sig("gate_ps"))

                for k in range(2):
                    gate(k)
                pe.wait_ge(sig("rope_ready"), l + 1)
                pe.wait_ge(sig("vp_kept"), l + 1)
                for j in range(5):
                    for t in range(TT):
                        turn(bank(j // 2)[:, (j % 2) * T + t * P:(j % 2) * T + (t + 1) * P],
                             qk[:, t, 2 * j:2 * j + 2, :].rearrange("p h c -> p (h c)"),
                             ready=sig("qkT_ps") if j == 4 and t == 1 else None)
                gate(2)
                pe.wait_ge(sig("qkT_kept"), l + 1)

                def scores(t):
                    for j in range(4):
                        for f in range(2):
                            mm(bank(2 * f + j // 2)[:, (j % 2) * T:(j % 2 + 1) * T], q2T[64 * f:64 * f + 64, j, t * P:(t + 1) * P],
                               k2T[64 * f:64 * f + 64, :], ready=sig("scores_ps") if j == 3 and f == 1 else None)

                def turn_att(c):
                    t, k, half = c // 4, (c // 2) % 2, c % 2
                    pe.wait_ge(sig("att_ready"), l * TT + t + 1)
                    if c >= 2:
                        pe.wait_ge(sig("attT_kept") if c % 2 == 0 else sig("attT_kept_a"), l * 4 + c // 2)
                    for i in range(4):
                        turn(bank(4 + c % 2)[:, i * P:(i + 1) * P], att[:, t, half * 4 + i, k * P:(k + 1) * P],
                             ready=sig("attT_ps") if i == 3 else None)

                scores(0)
                gate(3)
                gate(4)
                pe.wait_ge(sig("scores_kept"), l * TT + 1)
                scores(1)
                turn_att(0)
                turn_att(1)
                gate(5)
                turn_att(2)
                turn_att(3)
                pe.wait_ge(sig("scores_kept"), l * TT + 2)
                for g in range(4):
                    for t in range(TT):
                        mm(bank(2 + g // 2)[:, (g % 2) * T:(g % 2 + 1) * T], p_tok[:, t, g * P:(g + 1) * P],
                           poolm[:, g, t, :], start=t == 0, stop=t == 1,
                           ready=sig("pooled_ps") if g == 3 and t == 1 else None)
                gate(6)
                pe.wait_ge(sig("pooled_kept"), l + 1)
                for g in range(4):
                    mm(bank(2 + g // 2)[:, (g % 2) * T:(g % 2 + 1) * T], pool_w[:, g, :], pooledT[:, g, :],
                       ready=sig("mixed_ps") if g == 3 else None)
                gate(7)
                for c in range(4, 8):
                    turn_att(c)
                pe.wait_ge(sig("attT_kept"), l * 4 + 4)
                pe.wait_ge(sig("attT_kept_a"), l * 4 + 4)
                for j in range(4):
                    for f in range(2):
                        for k in range(TT):
                            mm(bank(j // 2)[64 * f:64 * f + 64, (j % 2) * T:(j % 2 + 1) * T],
                               v2[:, k, 64 * f:64 * f + 64], attT[:, k, 4 * f + j, :], start=k == 0, stop=k == 1,
                               ready=sig("a2T_ps") if j == 3 and f == k == 1 else None)
                pe.wait_ge(sig("mixT_ready"), l + 1)
                pe.wait_ge(sig("a2T_kept"), l + 1)
                pe.wait_ge(sig("gate_kept"), l * KD + KD)

                def kept2(k):
                    if k >= 2:
                        pe.wait_ge(sig("mT_ready"), l * KD + k - 1)

                branches(at + 13, turns, lambda k: bank(6 + k % 2), kept2, lambda i: a2T[:, i, :],
                         lambda i: mixT[:, i, :], sig("branch2_ps"))
                pe.wait_ge(sig("mT_ready"), l * KD + KD)
                token_out(at + 17, turns, 0, lambda k: mT[:, k, :], KD, sig("mixer_ps"))
                ffn(1, 54)
                slot(LAYER_SLOTS - 1, turns)
                pe.wait_ge(sig("down_step"), (l + 1) * 2 * DOWN_STEPS)
                pe.sem_inc(sig("slot_used"), pending[0] + 1)
                pending[0] = 0

def shape_tables():
    f = np.float32
    t = np.arange(T)
    w = np.pi * (2 * np.arange(T) + 1) / (2 * T)
    ang = np.outer(t, w)
    dft = np.stack([np.cos(ang), np.sin(ang)])
    dft_t = dft.reshape(2, TT, P, T).transpose(2, 0, 1, 3).reshape(P, -1)
    idft_t = (dft.transpose(0, 2, 1) / T).reshape(2, TT, P, T).transpose(2, 0, 1, 3).reshape(P, -1)
    s, q = np.arange(P)[:, None], np.arange(P)[None, :]
    big, zero = np.full((P, P), BIG), np.zeros((P, P))
    fwd, bwd = np.where(s <= q, 0, BIG), np.where(s >= q, 0, BIG)
    causal = np.concatenate([big, fwd, zero, zero, bwd, big], axis=1)
    tabs = np.concatenate([dft_t, idft_t, causal], axis=1).astype(f)
    const = np.concatenate([np.eye(P), np.ones((P, P)), np.tile(t, (P, 1))], axis=1).astype(f)
    tl = np.linspace(0.0, 1.0, T, dtype=f)[:, None]
    bands = np.linspace(1e-4, 15, 16, dtype=f)[None, :]
    za = (f(2.0 * np.pi / T) * np.arange(T, dtype=f)[:, None] * bands).astype(f)
    z = np.concatenate([tl, np.cos(za), np.sin(za)], axis=1).astype(f)
    lo, hi = np.log(1e-2) / 1.5, np.log(1e-2) / 0.3
    deltas = np.abs(np.linspace(lo, hi, HYC, dtype=f))
    decay = np.exp(-tl * deltas).astype(f).reshape(TT, P, HYC).transpose(1, 0, 2).reshape(P, -1)
    half = 8
    inv = (1.0 / (f(500000.0) ** (np.arange(0, 16, 2, dtype=f) / f(16)))).astype(f)
    ra = (np.arange(T, dtype=f)[:, None] * inv[None, :]).astype(f)
    rope = np.stack([np.cos(ra), np.sin(ra)]).astype(f).reshape(2, TT, P, half).transpose(2, 0, 1, 3).reshape(P, -1)
    amask = np.where(np.abs(t[:, None] - t[None, :]) <= 128, 0.0, -1e30)
    amask = amask.reshape(TT, P, T).transpose(1, 0, 2).reshape(P, -1)
    pool = np.zeros((4, T, T))
    for g, n in enumerate(POOLS):
        for q_ in range(T):
            a, b = max(q_ - n // 2, 0), min(q_ + n // 2, T)
            pool[g, a:b, q_] = 1.0 / (b - a)
            pool[g, q_, q_] -= 1.0
    pool = pool.reshape(4, TT, P, T).transpose(2, 0, 1, 3).reshape(P, -1)
    tabs2 = np.concatenate([rope, amask, pool], axis=1).astype(f)
    bmask = np.zeros((P, NE, CAP), f)
    bmask[np.arange(NE), np.arange(NE)] = 1.0
    not_first = np.ones((P, 2), f)
    not_first[0, 0] = 0.0
    tokens = t.reshape(TT, P).T.astype(f)
    return tabs, const, z, decay, tabs2, bmask, not_first, tokens


def lay_out(a):
    f = np.float32

    def cols_of(v):
        return v.reshape(-1, P).T

    def on_rows(v, rows=P):
        out = np.zeros((rows,) + v.shape[1:], v.dtype)
        out[0:v.shape[0]] = v
        return out

    def tiles(w):
        k, n = w.shape[0] // P, w.shape[1] // P
        return w.reshape(k, P, n, P).transpose(2, 1, 0, 3).reshape(n, P, k * P)

    def paired(v):
        return v.reshape(-1, 2, P, v.shape[2]).transpose(0, 2, 1, 3).reshape(-1, P, 2 * v.shape[2])

    def rows_in(w, per):
        return w.reshape(-1, per, P, w.shape[1]).transpose(0, 2, 1, 3).reshape(-1, P, per * w.shape[1])

    tabs, const, z, decay, tabs2, bmask, not_first, tokens = shape_tables()
    b_in, w_in = a["b_in"][0], a["w_in"][0]
    ML = 3 * HYC
    GATE = ML + 4 * H * P
    MERGE = GATE + 4 * H
    merge_tiles = tiles(w_in[:, MERGE:])
    merge_pairs = np.stack([merge_tiles[0:KD], merge_tiles[KD:]], axis=1).reshape(2 * KD, P, 1024)
    b_merge = cols_of(b_in[MERGE:]).reshape(P, 2, KD).transpose(0, 2, 1).reshape(P, 16)

    def branch(wa, wb):
        return paired(np.concatenate([tiles(wa), tiles(wb)], axis=2))

    stream = [
        a["w_ada"][0].reshape(KD, P, 3, SLOT).transpose(2, 0, 1, 3)[0],
        paired(tiles(w_in[:, ML + 512:ML + 1024])), paired(tiles(w_in[:, ML:ML + 512])),
        rows_in(w_in[:, ML + 1024:ML + 1536], 4), paired(tiles(w_in[:, ML + 1536:ML + 2048])),
        paired(tiles(w_in[:, 0:ML])), paired(merge_pairs)[0:4],
        a["w_ada"][0].reshape(KD, P, 3, SLOT).transpose(2, 0, 1, 3)[1],
        a["w_ada"][0].reshape(KD, P, 3, SLOT).transpose(2, 0, 1, 3)[2], paired(merge_pairs)[4:],
        branch(a["w_branch_hy"][0], a["w_branch_ml"][0]), rows_in(a["w_out"][0], 2), np.zeros((2, P, SLOT), f)]
    assert sum(len(s) for s in stream) == FIRST_SLOTS
    for e in range(NE):
        stream += [a["w_exp1"][0, e].reshape(KD, P, SLOT), a["w_exp3"][0, e].reshape(KD, P, SLOT),
                   rows_in(a["w_exp2"][0, e], 2)]
    for l in range(LAYERS):
        w = a["w_in_2"][l]

        def ffn(n):
            up = np.concatenate([tiles(a[f"{n}_w1_2"][l]), tiles(a[f"{n}_w3_2"][l])], axis=2)
            down = rows_in(a[f"{n}_w2_2"][l], 2)
            return [np.stack([(up if kind == "up" else down)[i] for kind, i in FFN_SLOTS])]

        gt = tiles(w[:, 1280:])
        wba = a["w_branch_attn_2"][l].reshape(2, 4, 64, D).transpose(1, 0, 2, 3).reshape(512, D)
        stream += ffn("ffn1")
        stream += [rows_in(w[:, 0:512], 4), rows_in(w[:, 512:768], 8), rows_in(w[:, 768:1280], 4),
                   np.concatenate([gt[0:KD], gt[KD:]], axis=2), branch(wba, a["w_branch_pool_2"][l]),
                   rows_in(a["w_out_2"][l], 2)]
        stream += ffn("ffn2")
        stream += [np.zeros((1, P, SLOT), f)]
    out = {"stream": np.concatenate(stream)}
    assert out["stream"].shape == (N_SLOTS, P, SLOT), out["stream"].shape

    c = np.stack([cols_of(a["c"][0]), cols_of(a["c_ctx"])], axis=2).reshape(P, 16)

    def taps(w, n):
        return w.reshape(3, n, P).transpose(2, 1, 0).reshape(P, 3 * n)

    out["cols"] = np.concatenate([
        c, cols_of(a["norm_mix_g"][0]), cols_of(a["norm_ffn_g"][0]), cols_of(b_in[0:ML]),
        cols_of(b_in[ML:ML + 512]), cols_of(b_in[ML + 512:ML + 1024]), cols_of(b_in[ML + 1536:ML + 2048]), b_merge,
        taps(a["hy_conv"][0], 12), taps(a["ml_conv"][0], 8),
        a["hy_skip"][0].reshape(ORDERS, 4, P).transpose(2, 0, 1).reshape(P, 8), cols_of(a["ml_norm_g"][0]),
        on_rows(a["hy_f_b1"][0][:, None]), on_rows(a["hy_f_b2"][0][:, None]),
        on_rows(b_in[GATE:MERGE].reshape(4, H).T), not_first, np.full((P, 1), EPS, f), np.ones((P, 1), f), tokens],
        axis=1)
    assert out["cols"].shape == (P, N_COLS)
    out["lcols"] = np.stack([np.concatenate([
        cols_of(a["ffn1_norm_2"][l]), cols_of(a["mix_norm_2"][l]), cols_of(a["ffn2_norm_2"][l]),
        cols_of(a["b_gate_2"][l]), cols_of(a["pool_scale_2"][l]),
        np.tile(a["attn_sink_2"][l][None, :], (P, 1)),
        a["pool_w_2"][l].transpose(1, 0, 2).reshape(P, 512)], axis=1) for l in range(LAYERS)])
    out["filt"] = np.concatenate([on_rows(z.T), on_rows(a["hy_f_w1"][0]), on_rows(a["hy_f_w2"][0]),
                                  on_rows(a["hy_f_w3"][0]), decay], axis=1)
    out["const"], out["tabs"], out["tabs2"], out["bmask"] = const, tabs, tabs2, bmask
    rows = np.zeros((P, 3, 512), f)
    for g in range(4):
        rows[32 * g] = rows[32 * g + 1] = a["b_ada"][0].reshape(3, 4, 512)[:, g]
    out["ada_rows"] = rows
    out["wgate"] = w_in[:, GATE:MERGE].reshape(KD, P, 16).transpose(1, 0, 2)
    out["vbias"] = np.tile(b_in[ML + 1024:ML + 1536][None, :], (P, 1))
    out["wrouter"] = a["w_router"][0].reshape(KD, P, NE).transpose(1, 0, 2)
    out["fin_rows"] = np.stack([np.tile(a["final_norm_g"][None, :], (P, 1)), np.tile(a["final_norm_2"][None, :], (P, 1))])
    out["x"] = a["x"][0].reshape(TT, P, D).transpose(1, 0, 2)
    out["ctx"] = a["ctx"][0].reshape(TT, P, D).transpose(1, 0, 2)
    return {k: np.ascontiguousarray(v) for k, v in out.items()}


def kernel(**inputs):
    import concourse.bacc as bacc
    from concourse.bass_utils import run_bass_kernel_spmd

    nc = bacc.Bacc("TRN2", target_bir_lowering=False, num_devices=1)
    arrays = lay_out({k: np.asarray(v) for k, v in inputs.items()})
    d = {k: nc.dram_tensor(f"{k}_dram", v.shape, F32, kind="ExternalInput").ap() for k, v in arrays.items()}
    d["out"] = nc.dram_tensor("out_dram", (P, TT, D), F32, kind="ExternalOutput").ap()
    build(nc, d)
    r = run_bass_kernel_spmd(nc, [{f"{k}_dram": v for k, v in arrays.items()}], core_ids=[0])
    return r.results[0]["out_dram"].reshape(P, TT, D).transpose(1, 0, 2).reshape(1, T, D)
```
